# Optimizing a Trainium2 kernel written in Bass

```python
import math
import jax, jax.numpy as jnp
from jax import lax
import numpy as np

D_MODEL = 1024
BATCH = 1
SEQ = 256
DEPTH = 2

GRID_W = 64
P_DIM = 256
EPS = 1e-6

A_HEADS = 4
A_DK = 128
A_DV = 128
A_KDIM = A_HEADS * A_DK
A_WIDTH = A_HEADS * A_DV
A_CHUNK = 64

B_HEADS = 8
B_HEADDIM = 64
B_WIDTH = B_HEADS * B_HEADDIM
B_GROUPS = 2
B_STATE = 128
B_CONV = 5
B_CONV_DIM = B_WIDTH + 2 * B_GROUPS * B_STATE
B_CHUNK = 128

C_HEADS = 16
C_HEADDIM = 64
C_WIDTH = C_HEADS * C_HEADDIM
NA_ROWS = 8
NA_COLS = 16
NA_COL_BLOCK = 16
NA_KEY_COLS = 32

D_FF = 2816
N_EXPERTS = 8
TOP_K = 2
D_FF_EXPERT = 3584

N_EVEN = (DEPTH + 1) // 2
N_ODD = DEPTH // 2
EVEN_SPLITS = (A_KDIM, A_KDIM, A_KDIM, A_WIDTH, A_WIDTH, B_WIDTH, B_CONV_DIM, B_HEADS, B_HEADS)
EVEN_IN = sum(EVEN_SPLITS)

kernel_name = 'hybrid_hgrn2_ssd_natten_moe_encoder'

def _split(u, sizes):
    idx = np.cumsum(np.array(sizes))[:-1].tolist()
    return jnp.split(u, idx, axis=-1)

def rmsnorm(x, g):
    xf = x.astype(jnp.float32)
    y = xf * lax.rsqrt(jnp.mean(xf * xf, axis=-1, keepdims=True) + EPS)
    return (y * g.astype(jnp.float32)).astype(x.dtype)

def segsum(a):
    T = a.shape[-1]
    cs = jnp.cumsum(a, axis=-1)
    diff = cs[..., :, None] - cs[..., None, :]
    mask = jnp.tril(jnp.ones((T, T), dtype=bool))
    return jnp.where(mask, diff, -jnp.inf)

def gla_chunk_scan(q, k, v, logf):
    Bsz, H, S, dk = q.shape
    dv = v.shape[-1]
    C = A_CHUNK
    nc = S // C
    chunks = lambda t: t.reshape(Bsz, H, nc, C, t.shape[-1]).transpose(2, 0, 1, 3, 4)
    causal = jnp.tril(jnp.ones((C, C), dtype=bool))[:, :, None]

    def step(state, inp):
        qi, ki, vi, gi = inp
        b = jnp.cumsum(gi, axis=2)
        diff = b[:, :, :, None, :] - b[:, :, None, :, :]
        decay = jnp.where(causal, jnp.exp(jnp.where(causal, diff, 0.0)), 0.0)
        attn = jnp.einsum('bhtk,bhtsk,bhsk->bhts', qi, decay, ki)
        o = jnp.einsum('bhts,bhsv->bhtv', attn, vi) + jnp.einsum('bhtk,bhkv->bhtv', qi * jnp.exp(b), state)
        b_last = b[:, :, -1:, :]
        new_state = state * jnp.exp(b_last[:, :, 0, :, None]) + jnp.einsum('bhsk,bhsv->bhkv', ki * jnp.exp(b_last - b), vi)
        return new_state, o

    state0 = jnp.zeros((Bsz, H, dk, dv), jnp.float32)
    _, out = lax.scan(step, state0, (chunks(q), chunks(k), chunks(v), chunks(logf)))
    return out.transpose(1, 2, 0, 3, 4).reshape(Bsz, H, S, dv)

def hgrn2_mixer(q_raw, ff_raw, fb_raw, i_raw, g_raw, lb, norm_g):
    Bsz, S, _ = q_raw.shape
    f32 = jnp.float32
    heads = lambda t, d: t.reshape(Bsz, S, A_HEADS, d).transpose(0, 2, 1, 3).astype(f32)
    q = heads(jax.nn.silu(q_raw), A_DK)
    v = heads(i_raw, A_DV)
    lbh = lb.reshape(A_HEADS, A_DK)[None, :, None, :]

    def gates(f_raw):
        f = lbh + (1.0 - lbh) * jax.nn.sigmoid(heads(f_raw, A_DK))
        return 1.0 - f, jnp.log(f)

    k_f, lf_f = gates(ff_raw)
    k_b, lf_b = gates(fb_raw)
    flip = lambda t: jnp.flip(t, axis=2)
    o = gla_chunk_scan(q, k_f, v, lf_f) + flip(gla_chunk_scan(flip(q), flip(k_b), flip(v), flip(lf_b)))
    o = o.transpose(0, 2, 1, 3).astype(q_raw.dtype)
    o = rmsnorm(o, norm_g) * jax.nn.silu(g_raw.reshape(Bsz, S, A_HEADS, A_DV))
    return o.reshape(Bsz, S, A_WIDTH)

def ssd_chunked(xs, dt, a_coef, Bm, Cm):
    Bsz, S, H, P = xs.shape
    G, N = Bm.shape[-2:]
    R = H // G
    Q = B_CHUNK
    nc = S // Q
    f32 = jnp.float32
    xc = (xs.astype(f32) * dt[..., None]).reshape(Bsz, nc, Q, G, R, P)
    Bc = Bm.astype(f32).reshape(Bsz, nc, Q, G, N)
    Cc = Cm.astype(f32).reshape(Bsz, nc, Q, G, N)
    a = (dt * a_coef).reshape(Bsz, nc, Q, G, R).transpose(0, 3, 4, 1, 2)
    a_cs = jnp.cumsum(a, axis=-1)
    L = jnp.exp(segsum(a))
    scores = jnp.einsum('bctgn,bcsgn->bgcts', Cc, Bc)
    y_diag = jnp.einsum('bgcts,bgrcts,bcsgrp->bctgrp', scores, L, xc)
    decay_states = jnp.exp(a_cs[..., -1:] - a_cs)
    states = jnp.einsum('bcsgn,bgrcs,bcsgrp->bcgrpn', Bc, decay_states, xc)
    chunk_a = jnp.pad(a_cs[..., -1], [(0, 0), (0, 0), (0, 0), (1, 0)])
    decay_chunk = jnp.exp(segsum(chunk_a))
    states = jnp.concatenate([jnp.zeros_like(states[:, :1]), states], axis=1)
    states = jnp.einsum('bgrzc,bcgrpn->bzgrpn', decay_chunk, states)[:, :-1]
    y_off = jnp.einsum('bctgn,bcgrpn,bgrct->bctgrp', Cc, states, jnp.exp(a_cs))
    return (y_diag + y_off).reshape(Bsz, S, H, P)

def mamba2_mixer(z, xBC, dt_f_raw, dt_b_raw, conv_w, conv_b, A_log, dt_bias, D_skip, norm_g):
    Bsz, S, Cdim = xBC.shape
    f32 = jnp.float32
    xBC = lax.conv_general_dilated(xBC, conv_w[:, None, :], window_strides=(1,),
                                   padding=[(B_CONV // 2, B_CONV // 2)],
                                   dimension_numbers=('NWC', 'WIO', 'NWC'),
                                   feature_group_count=Cdim)
    xBC = jax.nn.silu(xBC + conv_b)
    xs, Bm, Cm = _split(xBC, (B_WIDTH, B_GROUPS * B_STATE, B_GROUPS * B_STATE))
    xs = xs.reshape(Bsz, S, B_HEADS, B_HEADDIM)
    Bm = Bm.reshape(Bsz, S, B_GROUPS, B_STATE)
    Cm = Cm.reshape(Bsz, S, B_GROUPS, B_STATE)
    A = -jnp.exp(A_log.astype(f32))
    dtb = dt_bias.astype(f32)
    dt_f = jax.nn.softplus(dt_f_raw.astype(f32) + dtb[0])
    dt_b = jax.nn.softplus(dt_b_raw.astype(f32) + dtb[1])
    flip = lambda t: jnp.flip(t, axis=1)
    y = (ssd_chunked(xs, dt_f, A[0], Bm, Cm)
         + flip(ssd_chunked(flip(xs), flip(dt_b), A[1], flip(Bm), flip(Cm)))
         + D_skip.astype(f32)[:, None] * xs.astype(f32))
    y = y.reshape(Bsz, S, B_WIDTH).astype(z.dtype) * jax.nn.silu(z)
    y = rmsnorm(y.reshape(Bsz, S, B_GROUPS, B_WIDTH // B_GROUPS), norm_g.reshape(B_GROUPS, B_WIDTH // B_GROUPS))
    return y.reshape(Bsz, S, B_WIDTH)

def _na_column_tables():
    n_cb = GRID_W // NA_COL_BLOCK
    j = np.arange(n_cb)
    blk_start = np.clip(j * NA_COL_BLOCK - NA_COLS // 2, 0, GRID_W - NA_KEY_COLS)
    col_idx = blk_start[:, None] + np.arange(NA_KEY_COLS)[None, :]
    qcol = j[:, None] * NA_COL_BLOCK + np.arange(NA_COL_BLOCK)[None, :]
    qs = np.clip(qcol - NA_COLS // 2, 0, GRID_W - NA_COLS)
    kc = col_idx[:, None, :]
    valid = (kc >= qs[:, :, None]) & (kc < qs[:, :, None] + NA_COLS)
    dc_idx = np.clip(kc - qcol[:, :, None] + (NA_COLS - 1), 0, 2 * NA_COLS - 2)
    return col_idx.astype(np.int32), valid, dc_idx.astype(np.int32)

def neighborhood_attention(q, k, v, rpb):
    Bsz, S, H, dh = q.shape
    rows = S // GRID_W
    kh = min(NA_ROWS, rows)
    n_cb = GRID_W // NA_COL_BLOCK
    col_idx, valid, dc_idx = _na_column_tables()
    valid = jnp.asarray(valid)[:, :, None, :]
    grid = lambda t: t.reshape(Bsz, rows, GRID_W, H, dh).transpose(1, 0, 3, 2, 4)
    qg, kg, vg = grid(q), grid(k), grid(v)
    scale = C_HEADDIM ** -0.5

    def row_block(args):
        r, q_row = args
        qb = q_row.reshape(Bsz, H, n_cb, NA_COL_BLOCK, dh)
        rs = jnp.clip(r - kh // 2, 0, rows - kh)
        kr = lax.dynamic_slice_in_dim(kg, rs, kh, axis=0)[:, :, :, col_idx, :]
        vr = lax.dynamic_slice_in_dim(vg, rs, kh, axis=0)[:, :, :, col_idx, :]
        s = jnp.einsum('bhjqd,rbhjkd->bhjqrk', qb, kr).astype(jnp.float32) * scale
        dr = rs + jnp.arange(kh) - r + (NA_ROWS - 1)
        bias = rpb[:, dr][:, :, dc_idx].transpose(0, 2, 3, 1, 4)
        s = jnp.where(valid, s + bias.astype(jnp.float32)[None], -jnp.inf)
        pr = jax.nn.softmax(s.reshape(Bsz, H, n_cb, NA_COL_BLOCK, kh * NA_KEY_COLS), axis=-1)
        pr = pr.reshape(s.shape).astype(v.dtype)
        o = jnp.einsum('bhjqrk,rbhjkd->bhjqd', pr, vr)
        return o.reshape(Bsz, H, GRID_W, dh)

    out = lax.map(row_block, (jnp.arange(rows), qg))
    return out.transpose(1, 0, 3, 2, 4).reshape(Bsz, S, H * dh)

def swiglu(h, w_gate, w_up, w_down):
    return (jax.nn.silu(h @ w_gate) * (h @ w_up)) @ w_down

def moe_swiglu(h, w_router, w_gate, w_up, w_down):
    logits = (h @ w_router).astype(jnp.float32)
    top_val, top_idx = lax.top_k(logits, TOP_K)
    wts = jax.nn.softmax(top_val, axis=-1)
    gates = jnp.sum(jax.nn.one_hot(top_idx, N_EXPERTS, dtype=jnp.float32) * wts[..., None], axis=-2)
    gates = gates.astype(h.dtype)
    out = jnp.zeros_like(h)
    for e in range(N_EXPERTS):
        out = out + gates[..., e:e + 1] * swiglu(h, w_gate[e], w_up[e], w_down[e])
    return out

def setup_inputs(seed: int = 0) -> dict:
    key = jax.random.key(seed)
    keys = iter(jax.random.split(key, 64))
    nk = lambda: next(keys)
    f32 = jnp.float32

    def w(shape, fan_in):
        return jax.random.normal(nk(), shape, f32) * fan_in ** -0.5

    def gain(shape):
        return 1.0 + 0.05 * jax.random.normal(nk(), shape, f32)

    def small(shape, s=0.02):
        return s * jax.random.normal(nk(), shape, f32)

    NE, NO, D = N_EVEN, N_ODD, D_MODEL
    x = jax.random.normal(nk(), (BATCH, SEQ, D), f32)
    p = jax.random.normal(nk(), (DEPTH, BATCH, SEQ, P_DIM), f32)
    hgrn_lb_raw = 0.5 * jax.random.normal(nk(), (DEPTH + 1, A_KDIM), f32)
    dt0 = jnp.exp(jax.random.uniform(nk(), (NE, 2, B_HEADS), f32, math.log(1e-3), math.log(1e-1)))
    return {
        'x': x,
        'p': p,
        'hgrn_lb_raw': hgrn_lb_raw,
        'e_norm_mix_pre': gain((NE, D)),
        'e_w_in': w((NE, D, EVEN_IN), D),
        'e_conv_w': w((NE, B_CONV, B_CONV_DIM), B_CONV),
        'e_conv_b': small((NE, B_CONV_DIM)),
        'e_A_log': jnp.log(jax.random.uniform(nk(), (NE, 2, B_HEADS), f32, 1.0, 16.0)),
        'e_dt_bias': dt0 + jnp.log(-jnp.expm1(-dt0)),
        'e_D': gain((NE, B_HEADS)),
        'e_a_norm': gain((NE, A_DV)),
        'e_b_norm': gain((NE, B_WIDTH)),
        'e_w_out': w((NE, A_WIDTH + B_WIDTH, D), A_WIDTH + B_WIDTH),
        'e_norm_mix_post': gain((NE, D)),
        'e_norm_ffn_pre': gain((NE, D)),
        'e_w_ffn_gate': w((NE, D, D_FF), D),
        'e_w_ffn_up': w((NE, D, D_FF), D),
        'e_w_ffn_down': w((NE, D_FF, D), D_FF),
        'e_norm_ffn_post': gain((NE, D)),
        'o_norm_mix_pre': gain((NO, D)),
        'o_w_qkv': w((NO, D, 3 * C_WIDTH), D),
        'o_rpb': small((NO, C_HEADS, 2 * NA_ROWS - 1, 2 * NA_COLS - 1), 0.5),
        'o_w_out': w((NO, C_WIDTH, D), C_WIDTH),
        'o_norm_mix_post': gain((NO, D)),
        'o_norm_ffn_pre': gain((NO, D)),
        'o_w_router': w((NO, D, N_EXPERTS), D),
        'o_w_exp_gate': w((NO, N_EXPERTS, D, D_FF_EXPERT), D),
        'o_w_exp_up': w((NO, N_EXPERTS, D, D_FF_EXPERT), D),
        'o_w_exp_down': w((NO, N_EXPERTS, D_FF_EXPERT, D), D_FF_EXPERT),
        'o_norm_ffn_post': gain((NO, D)),
        'ple_norm_in': gain((DEPTH, D)),
        'ple_w_gate': w((DEPTH, D, D), D),
        'ple_w_proj': w((DEPTH, P_DIM, D), P_DIM),
        'ple_norm_post': gain((DEPTH, D)),
    }

def reference(x, p, hgrn_lb_raw,
              e_norm_mix_pre, e_w_in, e_conv_w, e_conv_b, e_A_log, e_dt_bias, e_D,
              e_a_norm, e_b_norm, e_w_out, e_norm_mix_post,
              e_norm_ffn_pre, e_w_ffn_gate, e_w_ffn_up, e_w_ffn_down, e_norm_ffn_post,
              o_norm_mix_pre, o_w_qkv, o_rpb, o_w_out, o_norm_mix_post,
              o_norm_ffn_pre, o_w_router, o_w_exp_gate, o_w_exp_up, o_w_exp_down, o_norm_ffn_post,
              ple_norm_in, ple_w_gate, ple_w_proj, ple_norm_post):
    Bsz, S, D = x.shape
    lb_all = jnp.cumsum(jax.nn.softmax(hgrn_lb_raw.astype(jnp.float32), axis=0), axis=0)
    for li in range(DEPTH):
        j = li // 2
        if li % 2 == 0:
            h = rmsnorm(x, e_norm_mix_pre[j])
            u = h @ e_w_in[j]
            q_a, ff_a, fb_a, i_a, g_a, z_b, xbc_b, dtf_b, dtb_b = _split(u, EVEN_SPLITS)
            o_a = hgrn2_mixer(q_a, ff_a, fb_a, i_a, g_a, lb_all[li], e_a_norm[j])
            o_b = mamba2_mixer(z_b, xbc_b, dtf_b, dtb_b, e_conv_w[j], e_conv_b[j],
                               e_A_log[j], e_dt_bias[j], e_D[j], e_b_norm[j])
            mix = jnp.concatenate([o_a, o_b], axis=-1) @ e_w_out[j]
            x = x + rmsnorm(mix, e_norm_mix_post[j])
            h = rmsnorm(x, e_norm_ffn_pre[j])
            x = x + rmsnorm(swiglu(h, e_w_ffn_gate[j], e_w_ffn_up[j], e_w_ffn_down[j]), e_norm_ffn_post[j])
        else:
            h = rmsnorm(x, o_norm_mix_pre[j])
            q_c, k_c, v_c = jnp.split(h @ o_w_qkv[j], 3, axis=-1)
            heads = lambda t: t.reshape(Bsz, S, C_HEADS, C_HEADDIM)
            o_c = neighborhood_attention(heads(q_c), heads(k_c), heads(v_c), o_rpb[j])
            x = x + rmsnorm(o_c @ o_w_out[j], o_norm_mix_post[j])
            h = rmsnorm(x, o_norm_ffn_pre[j])
            moe = moe_swiglu(h, o_w_router[j], o_w_exp_gate[j], o_w_exp_up[j], o_w_exp_down[j])
            x = x + rmsnorm(moe, o_norm_ffn_post[j])
        gate = jax.nn.sigmoid(rmsnorm(x, ple_norm_in[li]) @ ple_w_gate[li])
        x = x + rmsnorm(gate * (p[li] @ ple_w_proj[li]), ple_norm_post[li])
    return x


_drawn_inputs = setup_inputs


def setup_inputs(seed=0):
    import zlib

    import numpy as np

    out = dict(_drawn_inputs(seed))
    spreads = {}
    factors = {'o_norm_ffn_post': 3.062}
    for name, (base, spread) in spreads.items():
        noise = np.random.default_rng([zlib.crc32(name.encode()), seed]).standard_normal(out[name].shape)
        drawn = base * np.exp(spread * noise) if base else spread * noise
        out[name] = __import__('jax').numpy.asarray(drawn.astype(out[name].dtype))
    for name, factor in factors.items():
        out[name] = (out[name] * factor).astype(out[name].dtype)
    return out
```

```python
from contextlib import ExitStack

import concourse.bass as bass
import numpy as np
from concourse import mybir

P = 128
SEQ = 256
NT = SEQ // P
D = 1024
KT = D // P
GRID_W = 64
EPS = 1e-6
A_HEADS, A_DK = 4, 128
B_HEADS, B_HD, B_GROUPS, B_CONV = 8, 64, 2, 5
C_HEADS, C_HD = 16, 64
NA_ROWS, NA_COLS = 8, 16
RPB_W = 2 * NA_COLS - 1
RPB_H = (2 * NA_ROWS - 1) * RPB_W
D_FF = 2816
N_EXPERTS, D_FFE = 8, 3584
WIN = 3 * RPB_W + GRID_W
P_DIM = 256
H = 512
UNIT = 2048
RAW, SPLIT = 6, 3
FF_STEP = 256
FF_STEPS = D_FF // FF_STEP
FE_STEPS = D_FFE // H
MAX_ITEMS = N_EXPERTS + 3
NEG = -1e30

F32 = mybir.dt.float32
F32R = mybir.dt.float32r
I32 = mybir.dt.int32
U32 = mybir.dt.uint32
ALU = mybir.AluOpType
ACT = mybir.ActivationFunctionType
AX = mybir.AxisListType

U_WIN = 0
U_WOUT0 = U_WIN + 16
U_FFN = U_WOUT0 + 4
U_PLE0 = U_FFN + 3 * FF_STEPS
U_QKV = U_PLE0 + 5
U_WOUT1 = U_QKV + 12
U_MOE = U_WOUT1 + 4
U_STEP = U_MOE + 4 - RAW
U_TAIL = U_MOE + 4

V_GAIN = {"mix0": 0, "ffn0": 8, "ple0": 16, "mix1": 24, "ple1": 32}
V_LB = 40
V_CW = 52
V_CB = 92
V_N = 100

WIN_GROUPS = [("ff", 512), ("fb", 1024), ("q", 0), ("xs", 3072), ("v", 1536),
              ("bc", 3584), ("g", 2048), ("z", 2560)]
DT_COL = 4096

JOBS = [(d, lv) for d in (0, 1) for lv in (0, 16, 32, 64, 128)]
JOB_ROUND0 = 3


def job_buffers():
    out, w = [], 0
    for _, lv in JOBS:
        n = 2 if lv == 0 else 1
        out.append(list(range(w, w + n)))
        w += n
    return out


def job_banks():
    out, w = [], 0
    for _, lv in JOBS:
        n = 1 if lv == 128 else 2
        out.append(list(range(w, w + n)))
        w += n
    return out


JBUF, JBANK = job_buffers(), job_banks()
JOB_OF_BUF = {w: j for j, ws in enumerate(JBUF) for w in ws}


def trunk(nc, a, out):
    ctx = ExitStack()
    with ctx:
        def sb(name, shape, dt=F32, stack=None):
            return (stack or ctx).enter_context(nc.sbuf_tensor(name, shape, dt))

        raw = [sb(f"raw{i}", [P, UNIT]) for i in range(RAW)]
        hi = [sb(f"hi{i}", [P, UNIT], F32R) for i in range(SPLIT)]
        lo = [sb(f"lo{i}", [P, UNIT], F32R) for i in range(SPLIT)]
        x = sb("x", [P, NT, D])
        xn = sb("xn", [P, NT, D])
        hT_hi = sb("hT_hi", [P, KT, SEQ], F32R)
        hT_lo = sb("hT_lo", [P, KT, SEQ], F32R)
        gb = [sb(f"gb{i}", [P, D]) for i in range(2)]
        ident = sb("ident", [P, P])
        ones = sb("ones", [P, P])
        le = sb("le", [P, P])
        ge = sb("ge", [P, P])
        lt = sb("lt", [P, P])
        vcol = sb("vcol", [P, V_N])
        sums = sb("sums", [P, 8])
        rstd = sb("rstd", [P, 8])

        s0 = ExitStack()
        vrow = xn[0:V_N, 0, 0:P]
        qT = sb("qT", [P, A_HEADS, SEQ], F32, s0)
        kT = [sb(f"kT{d}", [P, A_HEADS, SEQ], F32, s0) for d in (0, 1)]
        G = [sb(f"G{d}", [P, A_HEADS, SEQ], F32, s0) for d in (0, 1)]
        PS = [sb(f"PS{d}", [P, A_HEADS, SEQ], F32, s0) for d in (0, 1)]
        E2 = sb("E2", [P, A_HEADS, SEQ], F32, s0)
        gb1_as_e = gb[1][:, :].rearrange("p (h t) -> p h t", h=A_HEADS)
        EB = [G[0][:, :, :], E2[:, :, :], gb1_as_e, G[1][:, :, :]]
        AT = xn[:, :, :].rearrange("p a d -> p (a d)").rearrange("p (h s t) -> p h s t", h=A_HEADS, s=NT)
        AT2 = sb("AT2", [P, A_HEADS, P], F32, s0)
        btot = sb("btot", [P, A_HEADS, 1], F32, s0)
        hmask = {(d, lv): sb(f"hmask{d}_{lv}", [P, P], F32, s0) for d, lv in JOBS if lv < 64}
        cin = sb("cin", [P, 4, SEQ + 4], F32, s0)
        cout = sb("cout", [P, 8, SEQ], F32, s0)
        vgz = sb("vgz", [P, 3, NT, H], F32, s0)
        wdt = sb("wdt", [P, KT, 16], F32, s0)
        wdt_hi = sb("wdt_hi", [P, KT, 16], F32R, s0)
        wdt_lo = sb("wdt_lo", [P, KT, 16], F32R, s0)
        lbt = sb("lbt", [P, 10, 4], F32, s0)
        smallb = sb("smallb", [P, 16 + 16 + 8 + 128], F32, s0)
        dtbb, alogb, db = smallb[:, 0:16], smallb[:, 16:32], smallb[:, 32:40]
        anb = smallb[:, 40:168]
        bnb = AT2[:, :, :].rearrange("p h t -> p (h t)")
        dts = sb("dts", [P, 8, NT, 16], F32, s0)
        dta = sb("dta", [P, NT, 16], F32, s0)
        nexpa = sb("nexpa", [P, 16], F32, s0)
        acs = sb("acs", [P, NT, 16], F32, s0)
        Ccol = sb("Ccol", [P, NT, 16], F32, s0)
        Cx = sb("Cx", [P, 16], F32, s0)
        csrow = sb("csrow", [16, SEQ], F32, s0)
        nrm = sb("nrm", [P, 12], F32, s0)
        flat = lambda v: v.rearrange("p h t -> p (h t)")
        Gm = [flat(EB[0]), flat(EB[1])]
        Lb = [gb[1][:, :], flat(EB[3])]
        Wb = [flat(kT[0][:, :, :]), flat(kT[1][:, :, :])]
        xsn = flat(PS[0][:, :, :]).rearrange("p (t c) -> p t c", t=NT)
        tmpn = flat(PS[1][:, :, :]).rearrange("p (t c) -> p t c", t=NT)
        squ = flat(qT[:, :, :]).rearrange("p (t c) -> p t c", t=NT)
        s0.close()

        s1 = ExitStack()
        ffs = sb("ffs", [P, 2, SEQ], F32, s1)
        ffh = [sb(f"ffh{i}", [P, 2, SEQ], F32R, s1) for i in range(2)]
        ffl = [sb(f"ffl{i}", [P, 2, SEQ], F32R, s1) for i in range(2)]
        sb("space1", [P, 640], F32, s1)
        bias = sb("bias", [P, C_HEADS, NT, SEQ], F32, s1)
        s1w = ExitStack()
        win = sb("win", [P, NT, C_HEADS, WIN], F32, s1w)
        tab = sb("tab", [C_HEADS, RPB_H], F32, s1w)
        tab_r = sb("tab_r", [C_HEADS, RPB_H], F32, s1w)
        s1w.close()
        pin = [sb("pin0", [P, NT, P_DIM], F32, s1w)]
        pT_hi = [sb("pT_hi0", [P, 2, SEQ], F32R, s1w)]
        pT_lo = [sb("pT_lo0", [P, 2, SEQ], F32R, s1w)]
        gate = [sb("gate0", [P, NT, D], F32, s1w)]
        s1w.close()
        qcT = sb("qcT", [P, KT, SEQ], F32, s1w)
        kcT = sb("kcT", [P, KT, SEQ], F32, s1w)
        vc = sb("vc", [P, NT, D], F32, s1w)
        s1w.close()
        s1.close()
        s3 = ExitStack()
        sc = [sb(f"sc{i}", [P, NT, SEQ], F32, s3) for i in range(2)]
        pr = [sb(f"pr{i}", [P, NT, SEQ], F32, s3) for i in range(2)]
        prT = [sb(f"prT{i}", [P, NT, SEQ], F32, s3) for i in range(2)]
        nmax = sb("nmax", [P, C_HEADS, NT], F32, s3)
        den = sb("den", [P, NT, C_HEADS], F32, s3)
        rden = sb("rden", [P, NT, C_HEADS], F32, s3)
        s3.close()

        s4 = ExitStack()
        pin.append(sb("pin1", [P, NT, P_DIM], F32, s4))
        pT_hi.append(sb("pT_hi1", [P, 2, SEQ], F32R, s4))
        pT_lo.append(sb("pT_lo1", [P, 2, SEQ], F32R, s4))
        hF = sb("hF", [P, KT, SEQ], F32, s4)
        gate.append(hF[:, :, :].rearrange("p k t -> p (k t)").rearrange("p (t d) -> p t d", t=NT))
        wr = sb("wr", [P, KT, N_EXPERTS], F32, s4)
        xg_hi = sb("xg_hi", [P, NT, D], F32R, s4)
        xg_lo = sb("xg_lo", [P, NT, D], F32R, s4)
        he_hi = sb("he_hi", [P, KT, P], F32R, s4)
        he_lo = sb("he_lo", [P, KT, P], F32R, s4)
        acc = sb("acc", [P, NT, D], F32, s4)
        es = sb("es", [P, H], F32, s4)
        ea = sb("ea", [P, H], F32, s4)
        eT_hi = sb("eT_hi", [P, 4, P], F32R, s4)
        eT_lo = sb("eT_lo", [P, 4, P], F32R, s4)
        y_hi = sb("y_hi", [P, D], F32R, s4)
        y_lo = sb("y_lo", [P, D], F32R, s4)
        sel = sb("sel", [P, NT, P], F32R, s4)
        selT = sb("selT", [P, SEQ], F32R, s4)
        gcol = sb("gcol", [P, NT, 1], F32, s4)
        gslot = sb("gslot", [P, 1], F32, s4)
        iota_f = sb("iota_f", [P, P], F32, s4)
        lg = sb("lg", [P, NT, 8], F32, s4)
        mx8 = sb("mx8", [P, NT, 8], F32, s4)
        ix8 = sb("ix8", [P, NT, 8], U32, s4)
        ixf = sb("ixf", [P, NT, 8], F32, s4)
        oh = sb("oh", [P, 2, NT, 8], F32, s4)
        msk = sb("msk", [P, NT, 8], F32, s4)
        gat = sb("gat", [P, NT, 12], F32, s4)
        posx = sb("posx", [P, NT, 12], F32, s4)
        r1 = sb("r1", [P, 8, NT, 8], F32, s4)
        cnt = sb("cnt", [P, 8], F32, s4)
        flag = sb("flag", [P, 8], F32, s4)
        fpos = sb("fpos", [P, 9], F32, s4)
        ohx = sb("ohx", [P, 3, 8], F32, s4)
        itf = sb("itf", [P, 16], F32, s4)
        items = sb("items", [1, 16], I32, s4)
        s4.close()

        B = [ctx.enter_context(nc.psum_tensor(f"bank{i}", [P, H], F32)) for i in range(8)]

        def sem(name):
            return ctx.enter_context(nc.semaphore(name))

        S = {}
        for n in (
                "act_step bnb_in cols_copied cols_done comb_added comb_done consts conv_done conv_silu "
                "dt_done dt_mm dt_ready dve_step e_done ehi elo emul esilu "
                "eturned ff_hi ff_lo ff_mul ff_silu g_done gates_done gath_done geh "
                "gel gm_done hF_copied hF_turned hT_hi_done hT_lo_done hi_ready ident_ready items_ready "
                "job_evac job_exp job_mul job_pe job_sub l_exp lg_done lo_ready logs_done "
                "mask_done mean_done mix_a mix_b moe_acc moe_consts moe_init nm_done o_copied "
                "o_done oa_done ob_done oc_done oc_norm out_done pT_hi_done pT_lo_done p_in "
                "p_turned ply_done pool_step pos_done post_mean post_root post_scaled post_sq pt_copied "
                "pt_done qkv_evac rbc_done rbc_used root_a root_b root_done rows_copied rows_turned "
                "s_done scans_done selT_copied selT_done sel_built sig_done small_in sumsq_done tab_in "
                "tab_out top_done top_exp turned unit_used vcol_ready vcol_t vrow_in w_done "
                "wdt_hi_done wdt_in wdt_lo_done win_evac win_in win_masked wr_in x_in x_ready "
                "xg_ready xgh_done xgl_done xn_act xn_dve xs_copied xs_turned y_pe yhi "
                "ylo "
        ).split():
            S[n] = sem(n)
        raw_in = [sem(f"raw_in{i}") for i in range(RAW)]
        gb_in = [sem(f"gb_in{i}") for i in range(2)]

        block = ctx.enter_context(nc.Block())

        def unit_count(u, turns):
            return u if turns is None else turns * RAW + u

        def used(eng, u, turns=None):
            eng.wait_ge(S["unit_used"], unit_count(u + 1, turns))

        def views(t, k):
            return t[:, :].rearrange("p (k n) -> p k n", k=k)

        def rows(w, k0, k, c0, c):
            return w[k0 * P:(k0 + k) * P, c0:c0 + c].rearrange("(k p) n -> p k n", p=P)

        e_w_in, e_w_out, o_w_qkv, o_w_out = a["e_w_in"][0], a["e_w_out"][0], a["o_w_qkv"][0], a["o_w_out"][0]
        w_g, w_u, w_d = a["e_w_ffn_gate"][0], a["e_w_ffn_up"][0], a["e_w_ffn_down"][0]
        x_in_d, out_d = a["x"][0], out[0]
        rev = nc.dram_tensor("rpb_reversed", (C_HEADS, RPB_H), F32, kind="Internal").ap()

        @block.sync
        def _(sp):
            def load(u, src, k, turns=None):
                if u >= RAW:
                    sp.wait_ge(S["lo_ready"], unit_count(u - RAW + 1, turns))
                sp.dma_start(views(raw[u % RAW], k), src).then_inc(raw_in[u % RAW], 16)

            for t in range(NT):
                sp.dma_start(x[:, t, :], x_in_d[t * P:(t + 1) * P, :]).then_inc(S["x_in"], 16)
            n = 0
            for name in ("e_norm_mix_pre", "e_norm_ffn_pre"):
                sp.dma_start(vrow[n:n + 8, :], a[name][0].rearrange("(k p) -> k p", p=P)).then_inc(S["vrow_in"], 16)
                n += 8
            sp.dma_start(vrow[n:n + 8, :], a["ple_norm_in"][0].rearrange("(k p) -> k p", p=P)).then_inc(S["vrow_in"], 16)
            n += 8
            sp.dma_start(vrow[n:n + 8, :], a["o_norm_mix_pre"][0].rearrange("(k p) -> k p", p=P)).then_inc(S["vrow_in"], 16)
            n += 8
            sp.dma_start(vrow[n:n + 8, :], a["ple_norm_in"][1].rearrange("(k p) -> k p", p=P)).then_inc(S["vrow_in"], 16)
            n += 8
            sp.dma_start(vrow[n:n + 12, :], a["hgrn_lb_raw"].rearrange("l (h p) -> (l h) p", p=P)).then_inc(S["vrow_in"], 16)
            n += 12
            sp.dma_start(vrow[n:n + 40, :], a["e_conv_w"][0].rearrange("j (c p) -> (j c) p", p=P)).then_inc(S["vrow_in"], 16)
            n += 40
            sp.dma_start(vrow[n:n + 8, :], a["e_conv_b"][0].rearrange("(c p) -> c p", p=P)).then_inc(S["vrow_in"], 16)
            for c, (_, col) in enumerate(WIN_GROUPS):
                for hf in range(2):
                    load(U_WIN + 2 * c + hf, rows(e_w_in, 4 * hf, 4, col, H), 4)
            def square(w, u0, cols):
                for c in range(cols):
                    for hf in range(2):
                        load(u0 + 2 * c + hf, rows(w, 4 * hf, 4, c * H, H), 4)
            square(e_w_out, U_WOUT0, 2)
            for m, w in enumerate((w_g, w_u)):
                load(U_FFN + m, rows(w, 0, KT, 0, FF_STEP), KT)
            with sp.Fori(0, (FF_STEPS - 1) // 2) as it:
                for b in range(2):
                    for m, w in enumerate((w_g, w_u)):
                        src = w[:, bass.ds(it * (2 * FF_STEP) + (b + 1) * FF_STEP, FF_STEP)].rearrange("(k p) n -> p k n", p=P)
                        load(U_FFN + 2 + 3 * b + m, src, KT, it)
                    src = w_d[bass.ds(it * (2 * FF_STEP) + b * FF_STEP, FF_STEP), :].rearrange("(k p) n -> p k n", p=P)
                    load(U_FFN + 2 + 3 * b + 2, src, 2, it)
            load(U_PLE0 - 1, rows(w_d, 2 * (FF_STEPS - 1), 2, 0, D), 2)
            def ple(u0, li, turns=None):
                for c in range(2):
                    for hf in range(2):
                        load(u0 + 2 * c + hf, rows(a["ple_w_gate"][li], 4 * hf, 4, c * H, H), 4, turns)
                load(u0 + 4, rows(a["ple_w_proj"][li], 0, 2, 0, D), 2, turns)
            ple(U_PLE0, 0)
            square(o_w_qkv, U_QKV, 6)
            square(o_w_out, U_WOUT1, 2)

            def gu(e, f, u, turns):
                for m, name in enumerate(("o_w_exp_gate", "o_w_exp_up")):
                    w = a[name][0]
                    for hf in range(2):
                        src = w[bass.ds(e, 1), hf * H:(hf + 1) * H, bass.ds(f * H, H)] \
                            .rearrange("e (k p) n -> p (e k) n", p=P)
                        load(u + 2 * m + hf, src, 4, turns)

            def dn(e, f, u, turns):
                w = a["o_w_exp_down"][0]
                for hf in range(2):
                    src = w[bass.ds(e, 1), bass.ds(f * H + hf * 256, 256), :] \
                        .rearrange("e (k p) n -> p (e k) n", p=P)
                    load(u + hf, src, 2, turns)

            def item(e, turns):
                gu(e, 0, U_MOE, turns)
                with sp.Fori(1, FE_STEPS) as f:
                    gu(e, f, U_MOE + 4 - RAW, turns + f)
                    dn(e, f - 1, U_MOE + 8 - RAW, turns + f)
                dn(e, FE_STEPS - 1, U_MOE + 4, turns + (FE_STEPS - 1))

            with sp.Fori(0, 1) as zero:
                item(zero, zero * FE_STEPS)
            sp.wait_ge(S["items_ready"], 1)
            n_items = sp.value_load(items[0:1, 12:13], min_val=N_EXPERTS, max_val=MAX_ITEMS)
            with sp.Fori(1, n_items) as i:
                e = sp.value_load(items[0:1, bass.ds(i, 1)], min_val=0, max_val=N_EXPERTS - 1)
                item(e, i * FE_STEPS)
            ple(U_MOE, 1, n_items * FE_STEPS)
            for t in range(NT):
                sp.wait_ge(S["x_ready"], 6 * 4)
                sp.dma_start(out_d[t * P:(t + 1) * P, :], x[:, t, :]).then_inc(S["out_done"], 16)
            sp.wait_ge(S["out_done"], 16 * NT)

        @block.gpsimd
        def _(pool):
            steps = [0]

            def link(ins):
                steps[0] += 1
                ins.then_inc(S["pool_step"], 1)
                pool.wait_ge(S["pool_step"], steps[0])

            def keep(t, pattern, base, cm):
                link(pool.affine_select(out=t, in_=t, compare_op=ALU.is_ge, fill=0.0, base=base,
                                        pattern=pattern, channel_multiplier=cm))

            def bcast(dst, src, n, s):
                pool.dma_start(dst, src.partition_broadcast(P)).then_inc(S[s], 16)

            link(pool.memset(ident[:, :], 0.0))
            pool.affine_select(out=ident[:, :], in_=ident[:, :], compare_op=ALU.not_equal, fill=1.0, base=0,
                               pattern=[[-1, P]], channel_multiplier=1).then_inc(S["ident_ready"], 1)
            gains = [a["e_norm_mix_post"][0], a["e_norm_ffn_post"][0], a["ple_norm_post"][0], a["o_norm_mix_post"][0],
                     a["o_norm_ffn_pre"][0], a["o_norm_ffn_post"][0], a["ple_norm_post"][1]]

            def load_gain(n):
                if n in (2, 3, 4, 5):
                    pool.wait_ge(S["post_scaled"], 4 * (n - 1))
                elif n == 6:
                    pool.wait_ge(S["xg_ready"], 1)
                pool.dma_start(gb[n % 2][:, :], gains[n].partition_broadcast(P)).then_inc(gb_in[n % 2], 16)

            bcast(dtbb, a["e_dt_bias"][0].rearrange("a h -> (a h)"), 16, "small_in")
            bcast(alogb, a["e_A_log"][0].rearrange("a h -> (a h)"), 16, "small_in")
            bcast(db, a["e_D"][0], 8, "small_in")
            bcast(anb, a["e_a_norm"][0], 128, "small_in")
            pool.dma_start(wdt[:, :, :], rows(e_w_in, 0, KT, DT_COL, 16)).then_inc(S["wdt_in"], 16)
            load_gain(0)
            pool.memset(ones[:, :], 1.0).then_inc(S["consts"], 1)
            for t, pat, cm, base in ((le, 1, -1, 0), (ge, -1, 1, 0), (lt, 1, -1, -1)):
                link(pool.memset(t[:, :], 1.0))
                keep(t[:, :], [[pat, P]], base, cm)
            for d, lv in JOBS:
                if lv >= 64:
                    continue
                m = hmask[(d, lv)]
                if lv == 0:
                    link(pool.memset(m[:, :], 1.0))
                    v = m[:, :].rearrange("p (b x) -> p b x", x=16)
                    nb = P // 16
                    if d == 0:
                        keep(v, [[-16, nb], [0, 16]], 0, 1)
                        keep(v, [[16, nb], [1, 16]], 0, -1)
                    else:
                        keep(v, [[16, nb], [0, 16]], 15, -1)
                        keep(v, [[-16, nb], [-1, 16]], 0, 1)
                else:
                    nb = P // (2 * lv)
                    link(pool.memset(m[:, :], 0.0))
                    v = m[:, :].rearrange("p (b x) -> p b x", x=2 * lv)
                    w = v[:, :, lv:] if d == 0 else v[:, :, :lv]
                    link(pool.memset(w, 1.0))
                    off = 0 if d == 0 else lv
                    keep(w, [[-2 * lv, nb], [0, lv]], -off, 1)
                    keep(w, [[2 * lv, nb], [0, lv]], off + lv - 1, -1)
            pool.memset(cin[:, :, 0:2], 0.0)
            link(pool.memset(cin[:, :, SEQ + 2:], 0.0))
            pool.memset(AT2[:, :, :], 0.0).then_inc(S["consts"], 1)
            pool.wait_ge(S["turned"], 4)
            pool.memset(AT, 0.0).then_inc(S["consts"], 1)

            pool.wait_ge(S["scans_done"], 1)
            for j, (d, lv) in enumerate(JOBS):
                if j == 2:
                    pool.wait_ge(S["scans_done"], 2)
                Y = PS[d]
                last = max(JBUF[j])
                if last >= 4:
                    pool.wait_ge(S["job_pe"], JOB_OF_BUF[last - 4] + 1)
                E = EB[JBUF[j][0] % 4]
                if lv == 0:
                    y = Y[:, :, :].rearrange("p h (b x) -> p (h b) x", x=16)
                    e = E.rearrange("p h (b x) -> p (h b) x", x=16)
                    pool.tensor_tensor(e, y, y[:, :, 7:8].to_broadcast([P, A_HEADS * SEQ // 16, 16]),
                                       ALU.subtract).then_inc(S["job_sub"], 1)
                elif lv < 128:
                    nb = A_HEADS * SEQ // (2 * lv)
                    y = Y[:, :, :].rearrange("p h (b x) -> p (h b) x", x=2 * lv)
                    e = E.rearrange("p h (b x) -> p (h b) x", x=2 * lv)
                    at = lv - 1 if d == 0 else lv
                    ref = y[:, :, at:at + 1].to_broadcast([P, nb, lv])
                    pool.tensor_tensor(e[:, :, :lv], ref, y[:, :, :lv], ALU.subtract)
                    pool.tensor_tensor(e[:, :, lv:], y[:, :, lv:], ref, ALU.subtract).then_inc(S["job_sub"], 1)
                else:
                    ref = (PS[0][:, :, P - 1:P] if d == 0 else btot[:, :, :]).to_broadcast([P, A_HEADS, P])
                    pool.tensor_tensor(E[:, :, 0:P], ref, Y[:, :, 0:P], ALU.subtract).then_inc(S["job_sub"], 1)

            pool.wait_ge(S["job_evac"], JBANK[5][-1] + 1)
            bcast(bnb, a["e_b_norm"][0], 512, "bnb_in")

            def update(n, add):
                for q in range(4):
                    t, hf = q // 2, q % 2
                    pool.wait_ge(S["post_scaled"], 4 * n + q + 1)
                    pool.tensor_tensor(x[:, t, hf * H:(hf + 1) * H], x[:, t, hf * H:(hf + 1) * H],
                                       add(t, hf), ALU.add).then_inc(S["x_ready"], 1)

            scaled = lambda t, hf: xn[:, t, hf * H:(hf + 1) * H]
            update(0, scaled)
            pool.wait_ge(S["x_ready"], 4)
            pool.dma_start(tab[:, :], a["o_rpb"][0].rearrange("h r c -> h (r c)")).then_inc(S["tab_in"], 16)
            pool.wait_ge(S["tab_in"], 16)
            whole = tab[:, :]
            backwards = bass.AP(tensor=whole.tensor, offset=whole.offset + RPB_H - 1,
                                ap=[list(whole.ap[0]), [-1, RPB_H]])
            link(pool.tensor_copy(tab_r[:, :], backwards))
            pool.dma_start(rev, tab_r[:, :]).then_inc(S["tab_out"], 16)
            pool.wait_ge(S["tab_out"], 16)
            for r in range(SEQ // GRID_W):
                src = bass.AP(tensor=rev.tensor,
                              offset=RPB_H - 1 - (NA_ROWS - 1 - r) * RPB_W - (NA_COLS - 1) - (WIN - 1),
                              ap=[[1, GRID_W], [RPB_H, C_HEADS], [1, WIN]])
                pool.dma_start(win[(r % 2) * GRID_W:(r % 2 + 1) * GRID_W, r // 2, :, :], src).then_inc(S["win_in"], 16)
            def load_p(li):
                pool.dma_start(pin[li][:, :, :], a["p"][li, 0].rearrange("(t p) n -> p t n", p=P)).then_inc(S["p_in"], 16)
            load_gain(1)
            load_gain(2)
            pool.wait_ge(S["win_in"], 16 * 4)
            for t in range(NT):
                for h in range(C_HEADS):
                    base_ap = win[:, t, h, :]
                    src = bass.AP(tensor=base_ap.tensor, offset=base_ap.offset + WIN - 1,
                                  ap=[list(base_ap.ap[0]), [-RPB_W, 4], [-1, GRID_W]])
                    ins = pool.tensor_copy(bias[:, h, t, :].rearrange("p (r c) -> p r c", c=GRID_W), src)
            link(ins)
            for r in range(2):
                v = bias[r * GRID_W:(r + 1) * GRID_W, :, :, :].rearrange("p h t (r c) -> p (h t r) c", c=GRID_W)
                link(pool.affine_select(out=v[:, :, NA_COLS:], in_=v[:, :, NA_COLS:], compare_op=ALU.is_ge, fill=NEG,
                                        base=NA_COLS // 2 - 1 - NA_COLS,
                                        pattern=[[0, C_HEADS * NT * 4], [-1, GRID_W - NA_COLS]], channel_multiplier=1))
                ins = pool.affine_select(out=v[:, :, :GRID_W - NA_COLS], in_=v[:, :, :GRID_W - NA_COLS],
                                         compare_op=ALU.is_ge, fill=NEG, base=NA_COLS // 2,
                                         pattern=[[0, C_HEADS * NT * 4], [1, GRID_W - NA_COLS]], channel_multiplier=-1)
                ins.then_inc(S["win_masked"], 1)
            pool.wait_ge(S["win_masked"], 2)
            load_p(0)
            update(1, scaled)
            load_gain(3)
            update(2, scaled)
            load_gain(4)
            update(3, scaled)
            load_gain(5)
            load_p(1)
            pool.dma_start(wr[:, :, :], a["o_w_router"][0].rearrange("(k p) e -> p k e", p=P)).then_inc(S["wr_in"], 16)
            pool.iota(iota_f[:, :], pattern=[[1, P]], base=0, channel_multiplier=0,
                      allow_small_or_imprecise_dtypes=True).then_inc(S["moe_consts"], 1)
            pool.iota(itf[:, :], pattern=[[1, 16]], base=0, channel_multiplier=0,
                      allow_small_or_imprecise_dtypes=True).then_inc(S["moe_consts"], 1)
            pool.memset(acc[:, :, :], 0.0).then_inc(S["moe_consts"], 1)
            pool.memset(y_hi[:, :].bitcast(F32), 0.0).then_inc(S["moe_init"], 1)
            pool.memset(y_lo[:, :].bitcast(F32), 0.0).then_inc(S["moe_init"], 1)
            pool.memset(selT[:, :].bitcast(F32), 0.0).then_inc(S["moe_init"], 1)
            load_gain(6)
            update(4, scaled)
            update(5, scaled)

        @block.scalar
        def _(act):
            steps = [0]
            A = act.activation

            def link(ins):
                steps[0] += 1
                ins.then_inc(S["act_step"], 1)
                act.wait_ge(S["act_step"], steps[0])

            def round_hi(u, turns=None):
                act.wait_ge(raw_in[u % RAW], 16 * (u // RAW + 1) if turns is None else turns * 16 + 16 * (u // RAW + 1))
                if u >= SPLIT:
                    act.wait_ge(S["unit_used"], unit_count(u - SPLIT + 1, turns))
                A(hi[u % SPLIT][:, :], raw[u % RAW][:, :], ACT.Copy).then_inc(S["hi_ready"], 1)

            def norm(n, wait_x):
                wait_x()
                for t in range(NT):
                    A(xn[:, t, :], x[:, t, :], ACT.Square, accum_out=sums[:, t:t + 1]).then_inc(S["sumsq_done"], 1)
                act.wait_ge(S["mean_done"], n + 1)
                A(sums[:, 2:4], sums[:, 0:2], ACT.Sqrt).then_inc(S["root_done"], 1)
                act.wait_ge(S["xn_dve"], 2 * n + 1)
                A(xn[:, 1, :], x[:, 1, :], ACT.Copy, scale=rstd[:, 1:2]).then_inc(S["xn_act"], 1)

            def turned(m, gain=None):
                for j in range(4):
                    act.wait_ge(S["turned"], 4 * m + j + 1)
                    for b in range(2):
                        kt = 2 * j + b
                        sc_ = 1.0 if gain is None else vcol[:, gain + kt:gain + kt + 1]
                        ins = A(hT_hi[:, kt, :], B[6 + j % 2][:, b * SEQ:(b + 1) * SEQ], ACT.Copy, scale=sc_)
                    ins.then_inc(S["hT_hi_done"], 1)

            def post(n, src, ready):
                for q in range(4):
                    ready(q)
                    A(xn[:, q // 2, (q % 2) * H:(q % 2 + 1) * H], src(q // 2, q % 2), ACT.Square,
                      accum_out=sums[:, 4 + q:5 + q]).then_inc(S["post_sq"], 1)
                act.wait_ge(S["post_mean"], n + 1)
                A(sums[:, 2:4], sums[:, 0:2], ACT.Sqrt).then_inc(S["post_root"], 1)

            x_of = lambda n: (lambda: act.wait_ge(S["x_ready"], 4 * n) if n else act.wait_ge(S["x_in"], 16 * NT))

            act.wait_ge(S["vcol_t"], 1)
            norm(0, x_of(0))
            act.wait_ge(S["vcol_ready"], 1)
            turned(0, V_GAIN["mix0"])
            act.wait_ge(S["wdt_in"], 16)
            A(wdt_hi[:, :, :], wdt[:, :, :], ACT.Copy).then_inc(S["wdt_hi_done"], 1)

            def evac_group(c):
                name = WIN_GROUPS[c][0]
                used(act, U_WIN + 2 * c + 1)
                for b in range(2):
                    bank = B[2 * (c % 2) + b]
                    if name in ("ff", "fb"):
                        g = G[0] if name == "ff" else G[1]
                        ins = A(g[:, 2 * b:2 * b + 2, :], bank[:, :].rearrange("p (h t) -> p h t", h=2), ACT.Sigmoid)
                    elif name == "q":
                        ins = A(qT[:, 2 * b:2 * b + 2, :], bank[:, :].rearrange("p (h t) -> p h t", h=2), ACT.Silu)
                    elif name in ("xs", "bc"):
                        if name == "bc":
                            act.wait_ge(S["conv_done"], 4)
                        ins = A(cin[:, 2 * b:2 * b + 2, 2:2 + SEQ], bank[:, :].rearrange("p (h t) -> p h t", h=2), ACT.Copy)
                    else:
                        k = ("v", "g", "z").index(name)
                        ins = A(vgz[:, k, b, :], bank[:, :], ACT.Silu if k else ACT.Copy)
                ins.then_inc(S["win_evac"], 1)

            def job_exp(j):
                d, lv = JOBS[j]
                act.wait_ge(S["job_sub"], j + 1)
                E = EB[JBUF[j][0] % 4]
                if lv == 0:
                    link(A(EB[JBUF[j][1] % 4], E, ACT.Exp, scale=-1.0))
                    A(E, E, ACT.Exp).then_inc(S["job_exp"], 1)
                elif lv < 128:
                    A(E, E, ACT.Exp).then_inc(S["job_exp"], 1)
                else:
                    A(E[:, :, P:], PS[d][:, :, P:], ACT.Exp)
                    A(E[:, :, 0:P], E[:, :, 0:P], ACT.Exp).then_inc(S["job_exp"], 1)

            def softplus_exps():
                act.wait_ge(S["dt_ready"], 1)
                A(dts[:, 2, :, :], dts[:, 1, :, :], ACT.Exp, scale=-1.0).then_inc(S["dt_done"], 1)
                act.wait_ge(S["small_in"], 16 * 4)
                A(nexpa[:, :], alogb, ACT.Exp).then_inc(S["dt_done"], 1)

            def softplus_log():
                act.wait_ge(S["dt_ready"], 2)
                A(dts[:, 4, :, :], dts[:, 3, :, :], ACT.Ln).then_inc(S["dt_done"], 1)

            nxt = [0]

            def ahead(end, turns=None):
                while nxt[0] < end:
                    round_hi(nxt[0], turns)
                    nxt[0] += 1

            for c in range(9):
                ahead(U_WIN + 2 * c + SPLIT)
                if c:
                    evac_group(c - 1)
                if c == 1:
                    act.wait_ge(S["gates_done"], 1)
                    A(lbt[:, 3:6, :], lbt[:, 0:3, :], ACT.Exp).then_inc(S["logs_done"], 1)
                if c == 3:
                    for d in (0, 1):
                        act.wait_ge(S["gates_done"], 2 + d)
                        A(G[d][:, :, :], G[d][:, :, :], ACT.Ln).then_inc(S["logs_done"], 1)
                if JOB_ROUND0 <= c < 8:
                    for j in (2 * (c - JOB_ROUND0), 2 * (c - JOB_ROUND0) + 1):
                        job_exp(j)
                if c == 4:
                    softplus_exps()
                if c == 6:
                    softplus_log()
            for b in range(2):
                act.wait_ge(S["conv_done"], 4 * b + 4)
                A(cout[:, 4 * b:4 * b + 4, :], cout[:, 4 * b:4 * b + 4, :], ACT.Silu).then_inc(S["conv_silu"], 1)
            act.wait_ge(S["o_done"], 1)
            for t in range(NT):
                A(xn[:, t, 0:H], B[t][:, :], ACT.Copy).then_inc(S["o_copied"], 1)
            act.wait_ge(S["oa_done"], 1)
            A(nrm[:, 0:8], nrm[:, 0:8], ACT.Sqrt).then_inc(S["root_a"], 1)
            for h in range(B_HEADS):
                act.wait_ge(S["rbc_used"], h + 1)
                A(Lb[h % 2][:, 0:768], Lb[h % 2][:, 0:768], ACT.Exp).then_inc(S["l_exp"], 1)
            act.wait_ge(S["ob_done"], 1)
            A(nrm[:, 8:12], nrm[:, 8:12], ACT.Sqrt).then_inc(S["root_b"], 1)
            turned(1)
            ahead(U_FFN + 1)

            def bank_src(t, hf):
                return B[2 * hf + t][:, :]
            ahead(U_FFN + SPLIT)
            post(0, bank_src, lambda q: used(act, U_WOUT0 + 3))
            norm(1, x_of(1))
            turned(2, V_GAIN["ffn0"])

            def ff_evac(c, b, loop=None):
                k = lambda v: v if loop is None else loop * 2 + v
                used(act, U_FFN + 1 if c == 0 else U_FFN + 3 * c, loop)
                for j in range(2):
                    ins = A(ffs[:, j, :], B[2 * b + j][:, 0:SEQ], ACT.Silu)
                ins.then_inc(S["ff_silu"], 1)
                act.wait_ge(S["ff_mul"], k(c + 1))
                A(ffh[b][:, :, :], ffs[:, :, :], ACT.Copy).then_inc(S["ff_hi"], 1)

            ff_evac(0, 0)
            with act.Fori(0, (FF_STEPS - 1) // 2) as it:
                for b in range(2):
                    for m in range(3):
                        round_hi(U_FFN + 3 + 3 * b + m, it)
                    ff_evac(1 + b, (1 + b) % 2, it)
            nxt[0] = U_PLE0
            ahead(U_PLE0 + SPLIT)

            def bank_y(t, hf):
                return B[4 + 2 * t + hf][:, :]
            post(1, bank_y, lambda q: used(act, U_PLE0 - 1))
            norm(2, x_of(2))
            turned(3, V_GAIN["ple0"])

            def ple(n, u0, turns=None):
                act.wait_ge(S["p_turned"], n + 1)
                A(pT_hi[n][:, :, :], B[5][:, :].rearrange("p (k t) -> p k t", k=2), ACT.Copy).then_inc(S["pT_hi_done"], 1)
                for c in range(2):
                    ahead(u0 + 5, turns)
                    used(act, u0 + 2 * c + 1, turns)
                    for t in range(NT):
                        ins = A(gate[n][:, t, c * H:(c + 1) * H], B[2 * c + t][:, :], ACT.Sigmoid)
                    ins.then_inc(S["sig_done"], 1)

            def gate_src(n):
                return lambda t, hf: gate[n][:, t, hf * H:(hf + 1) * H]

            ple(0, U_PLE0)
            ahead(U_QKV + SPLIT)
            post(2, gate_src(0), lambda q: act.wait_ge(S["ply_done"], q + 1))
            norm(3, x_of(3))
            turned(4, V_GAIN["mix1"])

            def qkv_evac(c):
                used(act, U_QKV + 2 * c + 1)
                for b in range(2):
                    bank = B[2 * (c % 2) + b]
                    if c < 4:
                        dst = qcT if c < 2 else kcT
                        k0 = 4 * (c % 2) + 2 * b
                        ins = A(dst[:, k0:k0 + 2, :], bank[:, :].rearrange("p (k t) -> p k t", k=2), ACT.Copy)
                    else:
                        ins = A(vc[:, b, (c - 4) * H:(c - 3) * H], bank[:, :], ACT.Copy)
                ins.then_inc(S["qkv_evac"], 1)

            for c in range(6):
                ahead(U_QKV + 2 * c + 2 + SPLIT)
                qkv_evac(c)
            for i in range(C_HEADS + 1):
                if i < C_HEADS:
                    act.wait_ge(S["nm_done"], i + 1)
                    if i >= 2:
                        act.wait_ge(S["pt_done"], i - 1)
                    for t in range(NT):
                        ins = A(pr[i % 2][:, t, :], sc[i % 2][:, t, :], ACT.Exp, bias=nmax[:, i, t:t + 1],
                                accum_out=den[:, t, i:i + 1])
                        ins.then_inc(S["e_done"], 1)
                if i:
                    h = i - 1
                    act.wait_ge(S["pt_done"], h + 1)
                    if h >= 2:
                        act.wait_ge(S["oc_done"], h - 1)
                    A(prT[h % 2][:, :, :], B[2 + h % 2][:, :].rearrange("p (s t) -> p s t", s=NT),
                      ACT.Copy).then_inc(S["pt_copied"], 1)
            turned(5)
            ahead(U_MOE + 1)
            post(3, bank_src, lambda q: used(act, U_WOUT1 + 3))
            norm(4, x_of(4))

            act.wait_ge(S["xg_ready"], 1)
            A(xg_hi[:, :, :], xn[:, :, :], ACT.Copy).then_inc(S["xgh_done"], 1)
            for j in range(4):
                act.wait_ge(S["hF_turned"], j + 1)
                A(hF[:, 2 * j:2 * j + 2, :], B[6 + j % 2][:, :].rearrange("p (k t) -> p k t", k=2),
                  ACT.Copy).then_inc(S["hF_copied"], 1)
            act.wait_ge(S["top_done"], 1)
            A(r1[:, 1, :, 0:1], r1[:, 0, :, 0:1], ACT.Exp).then_inc(S["top_exp"], 1)
            act.wait_ge(S["items_ready"], 1)
            n_items = act.value_load(items[0:1, 12:13], min_val=N_EXPERTS, max_val=MAX_ITEMS)

            def gather_evac(k):
                act.wait_ge(S["gath_done"], k)
                for b in range(2):
                    ins = A(he_hi[:, 4 * b:4 * b + 4, :], B[5 + b][:, :].rearrange("p (k s) -> p k s", k=4), ACT.Copy)
                ins.then_inc(S["geh"], 1)

            def silu(u, turns):
                used(act, u + 1, turns)
                A(es[:, :], B[0][:, :], ACT.Silu).then_inc(S["esilu"], 1)

            def turned_hi(u):
                act.wait_ge(S["eturned"], u)
                A(eT_hi[:, :, :], B[4][:, :].rearrange("p (k s) -> p k s", k=4), ACT.Copy).then_inc(S["ehi"], 1)

            def y_high(i):
                used(act, U_MOE - 1, i * FE_STEPS)
                act.wait_ge(S["comb_done"], i + 1)
                act.wait_ge(S["selT_copied"], i + 1)
                for hf in range(2):
                    ins = A(y_hi[:, hf * H:(hf + 1) * H], B[2 + hf][:, :], ACT.Copy, scale=gslot[:, 0:1])
                ins.then_inc(S["yhi"], 1)

            gather_evac(1)
            act.wait_ge(S["moe_init"], 3)
            with act.Fori(0, n_items) as i:
                turns = i * FE_STEPS
                round_hi(U_MOE + 1, turns)
                round_hi(U_MOE + 2, turns)
                y_high(i)
                round_hi(U_MOE + 3, turns)
                round_hi(U_MOE + 4, turns)
                silu(U_MOE, turns)
                with act.Fori(1, FE_STEPS) as f:
                    done = turns + f
                    round_hi(U_STEP + 1, done)
                    round_hi(U_STEP + 2, done)
                    turned_hi(done)
                    for k in range(3, 7):
                        round_hi(U_STEP + k, done)
                    silu(U_STEP, done)
                round_hi(U_TAIL + 1, turns + (FE_STEPS - 1))
                turned_hi(turns + FE_STEPS)
                gather_evac(i + 2)
                round_hi(U_TAIL + 2, turns + (FE_STEPS - 1))
            y_high(n_items + 0)
            all_turns = n_items * FE_STEPS
            nxt[0] = U_MOE + 1
            ahead(U_MOE + SPLIT, all_turns)
            post(4, lambda t, hf: acc[:, t, hf * H:(hf + 1) * H], lambda q: act.wait_ge(S["moe_acc"], q + 1))
            norm(5, x_of(5))
            turned(6, V_GAIN["ple1"])
            ple(1, U_MOE, all_turns)
            post(5, gate_src(1), lambda q: act.wait_ge(S["ply_done"], 4 + q + 1))

        @block.vector
        def _(dve):
            steps = [0]
            TT, TS, STT = dve.tensor_tensor, dve.tensor_scalar, dve.scalar_tensor_tensor

            def mark(ins):
                steps[0] += 1
                ins.then_inc(S["dve_step"], 1)
                return steps[0]

            def link(ins):
                dve.wait_ge(S["dve_step"], mark(ins))

            def take_lo(u, turns=None):
                dve.wait_ge(S["hi_ready"], unit_count(u + 1, turns))
                TT(lo[u % SPLIT][:, :], raw[u % RAW][:, :], hi[u % SPLIT][:, :].bitcast(F32),
                   ALU.subtract).then_inc(S["lo_ready"], 1)

            nxt = [0]

            def ahead(end, turns=None):
                while nxt[0] < end:
                    take_lo(nxt[0], turns)
                    nxt[0] += 1

            def inverse_root(n):
                dve.wait_ge(S["root_done"], n + 1)
                link(dve.reciprocal(rstd[:, 0:2], sums[:, 2:4]))

            def norm(n):
                dve.wait_ge(S["sumsq_done"], 2 * n + 2)
                TS(sums[:, 0:2], sums[:, 0:2], 1.0 / D, EPS, ALU.mult, ALU.add).then_inc(S["mean_done"], 1)
                dve.wait_ge(S["root_done"], n + 1)
                dve.reciprocal(rstd[:, 0:2], sums[:, 2:4]).then_inc(S["xn_dve"], 1)
                dve.wait_ge(S["xn_dve"], 2 * n + 1)
                TS(xn[:, 0, :], x[:, 0, :], rstd[:, 0:1], None, ALU.mult).then_inc(S["xn_dve"], 1)

            def turned(m, gain=None):
                for j in range(4):
                    dve.wait_ge(S["hT_hi_done"], 4 * m + j + 1)
                    for b in range(2):
                        kt = 2 * j + b
                        src, top = B[6 + j % 2][:, b * SEQ:(b + 1) * SEQ], hT_hi[:, kt, :].bitcast(F32)
                        if gain is None:
                            ins = TT(hT_lo[:, kt, :], src, top, ALU.subtract)
                        else:
                            ins = STT(hT_lo[:, kt, :], src, vcol[:, gain + kt:gain + kt + 1], top, ALU.mult, ALU.subtract)
                    ins.then_inc(S["hT_lo_done"], 1)

            def post(n, src):
                g = n if n < 4 else n + 1
                dve.wait_ge(S["post_sq"], 4 * n + 4)
                v = sums[:, 4:8].rearrange("p (t h) -> p t h", h=2)
                link(dve.tensor_reduce(sums[:, 0:2], v, AX.X, ALU.add))
                TS(sums[:, 0:2], sums[:, 0:2], 1.0 / D, EPS, ALU.mult, ALU.add).then_inc(S["post_mean"], 1)
                dve.wait_ge(S["post_root"], n + 1)
                link(dve.reciprocal(rstd[:, 2:4], sums[:, 2:4]))
                dve.wait_ge(gb_in[g % 2], 16 * (g // 2 + 1))
                for q in range(4):
                    t, hf = q // 2, q % 2
                    cols = slice(hf * H, (hf + 1) * H)
                    ins = STT(xn[:, t, cols], src(t, hf), rstd[:, 2 + t:3 + t], gb[g % 2][:, cols], ALU.mult, ALU.mult)
                    ins.then_inc(S["post_scaled"], 1)

            dve.wait_ge(S["vcol_t"], 1)
            dve.tensor_copy(vcol[:, :], B[7][:, 0:V_N]).then_inc(S["vcol_ready"], 1)
            dve.wait_ge(S["vcol_ready"], 1)
            raw3 = vcol[:, V_LB:V_LB + 12].rearrange("p (l h) -> p l h", l=3)
            link(TT(lbt[:, 6, :], raw3[:, 0, :], raw3[:, 1, :], ALU.max))
            link(TT(lbt[:, 7, :], lbt[:, 6, :], raw3[:, 2, :], ALU.max))
            for l in range(3):
                ins = TT(lbt[:, l, :], raw3[:, l, :], lbt[:, 7, :], ALU.subtract)
            ins.then_inc(S["gates_done"], 1)
            norm(0)
            turned(0, V_GAIN["mix0"])
            dve.wait_ge(S["wdt_hi_done"], 1)
            TT(wdt_lo[:, :, :], wdt[:, :, :], wdt_hi[:, :, :].bitcast(F32), ALU.subtract).then_inc(S["wdt_lo_done"], 1)

            def lower_bounds():
                dve.wait_ge(S["logs_done"], 1)
                link(TT(lbt[:, 6, :], lbt[:, 3, :], lbt[:, 4, :], ALU.add))
                link(TT(lbt[:, 6, :], lbt[:, 6, :], lbt[:, 5, :], ALU.add))
                link(dve.reciprocal(lbt[:, 7, :], lbt[:, 6, :]))
                link(TT(lbt[:, 8, :], lbt[:, 3, :], lbt[:, 7, :], ALU.mult))
                link(TS(lbt[:, 9, :], lbt[:, 8, :], -1.0, 1.0, ALU.mult, ALU.add))

            def gates(d):
                dve.wait_ge(S["win_evac"], d + 1)
                for h in range(A_HEADS):
                    ins = TS(G[d][:, h, :], G[d][:, h, :], lbt[:, 9, h:h + 1], lbt[:, 8, h:h + 1], ALU.mult, ALU.add)
                    n = mark(ins)
                dve.wait_ge(S["dve_step"], n)
                TS(kT[d][:, :, :], G[d][:, :, :], -1.0, 1.0, ALU.mult, ALU.add).then_inc(S["gates_done"], 1)

            def scans(d):
                dve.wait_ge(S["logs_done"], 2 + d)
                dve.wait_ge(S["consts"], 1)
                if d:
                    v = PS[1][:, :, :].rearrange("p h (t c) -> p (h t) c", c=P)
                    dve.memset(v[:, :, 0:1], 0.0)
                for h in range(A_HEADS):
                    for t in range(NT):
                        if d == 0:
                            o, i_ = PS[0][:, h, t * P:(t + 1) * P], G[0][:, h, t * P:(t + 1) * P]
                        else:
                            o, i_ = PS[1][:, h, t * P + 1:(t + 1) * P], G[1][:, h, t * P:(t + 1) * P - 1]
                        n = mark(dve.tensor_tensor_scan(o, ones[:, 0:P - d], i_, 0.0, ALU.mult, ALU.add))
                dve.wait_ge(S["dve_step"], n)
                if d:
                    link(TT(btot[:, :, :], PS[1][:, :, P - 1:P], G[1][:, :, P - 1:P], ALU.add))
                dve.sem_inc(S["scans_done"], 1)

            def job_mul(j):
                d, lv = JOBS[j]
                dve.wait_ge(S["job_exp"], j + 1)
                E = EB[JBUF[j][0] % 4]
                if lv == 0:
                    E2_ = EB[JBUF[j][1] % 4]
                    eq, ek = (E, E2_) if d == 0 else (E2_, E)
                    TT(eq, eq, qT[:, :, :], ALU.mult)
                    TT(ek, ek, kT[d][:, :, :], ALU.mult).then_inc(S["job_mul"], 1)
                    return
                w = 2 * lv
                e, q_, k_ = (v.rearrange("p h (b x) -> p (h b) x", x=w) for v in (E, qT[:, :, :], kT[d][:, :, :]))
                left, right = (k_, q_) if d == 0 else (q_, k_)
                TT(e[:, :, :lv], e[:, :, :lv], left[:, :, :lv], ALU.mult)
                TT(e[:, :, lv:], e[:, :, lv:], right[:, :, lv:], ALU.mult).then_inc(S["job_mul"], 1)

            def job_evac(j):
                d, lv = JOBS[j]
                dve.wait_ge(S["job_pe"], j + 1)
                if j == 0:
                    dve.wait_ge(S["consts"], 3)
                for n, w in enumerate(JBANK[j]):
                    bank = B[4 + w % 4][:, :].rearrange("p (h t) -> p h t", h=A_HEADS)
                    if w >= 2:
                        dve.wait_ge(S["job_evac"], w - 1)
                    if lv == 128:
                        s_, t0 = (0, P) if d == 0 else (1, 0)
                        dve.tensor_copy(AT[:, :, s_, t0:t0 + P], bank).then_inc(S["job_evac"], 1)
                        continue
                    if lv == 64:
                        ks, qs = (0, 64) if d == 0 else (64, 0)
                        dve.tensor_copy(AT[ks:ks + 64, :, n, n * P + qs:n * P + qs + 64],
                                        bank[ks:ks + 64, :, qs:qs + 64]).then_inc(S["job_evac"], 1)
                        continue
                    m = hmask[(d, lv)][:, :].bitcast(I32).rearrange("p (o t) -> p o t", o=1).to_broadcast([P, A_HEADS, P])
                    own = AT[:, :, n, n * P:(n + 1) * P]
                    if (d, lv) == (1, 0):
                        link(dve.copy_predicated(AT2[:, :, :], m, bank))
                        link(TT(own, own, AT2[:, :, :], ALU.add))
                        dve.sem_inc(S["job_evac"], 1)
                    else:
                        dve.copy_predicated(own, m, bank).then_inc(S["job_evac"], 1)

            def softplus():
                dve.wait_ge(S["dt_mm"], 1)
                dve.wait_ge(S["small_in"], 16 * 4)
                b16 = dtbb.rearrange("p (o c) -> p o c", o=1).to_broadcast([P, NT, 16])
                link(TT(dts[:, 0, :, :], B[5][:, 0:2 * 16].rearrange("p (t c) -> p t c", t=NT), b16, ALU.add))
                STT(dts[:, 1, :, :], dts[:, 0, :, :], -1.0, dts[:, 0, :, :], ALU.mult, ALU.max).then_inc(S["dt_ready"], 1)

            def softplus2():
                dve.wait_ge(S["dt_done"], 1)
                TS(dts[:, 3, :, :], dts[:, 2, :, :], 1.0, None, ALU.add).then_inc(S["dt_ready"], 1)

            def softplus3():
                e = dts[:, 2, :, :]
                dve.wait_ge(S["dt_ready"], 2)
                link(TS(dts[:, 5, :, :], dts[:, 3, :, :], -1.0, 1e-30, ALU.add, ALU.max))
                link(dve.reciprocal(dts[:, 6, :, :], dts[:, 5, :, :]))
                link(TT(dts[:, 6, :, :], dts[:, 6, :, :], e, ALU.mult))
                link(TS(dts[:, 5, :, :], e, -0.5, 1.0, ALU.mult, ALU.add))
                link(TT(dts[:, 5, :, :], dts[:, 5, :, :], e, ALU.mult))
                dve.wait_ge(S["dt_done"], 3)
                link(TT(dts[:, 6, :, :], dts[:, 6, :, :], dts[:, 4, :, :], ALU.mult))
                link(TT(dts[:, 6, :, :], dts[:, 6, :, :], dts[:, 5, :, :], ALU.max))
                link(TS(dts[:, 7, :, :], dts[:, 0, :, :], 0.0, None, ALU.max))
                link(TT(dta[:, :, :], dts[:, 7, :, :], dts[:, 6, :, :], ALU.add))
                link(TS(nexpa[:, :], nexpa[:, :], -1.0, None, ALU.mult))
                n16 = nexpa[:, :].rearrange("p (o c) -> p o c", o=1).to_broadcast([P, NT, 16])
                TT(acs[:, :, :], dta[:, :, :], n16, ALU.mult).then_inc(S["dt_ready"], 1)

            def conv(b):
                dve.wait_ge(S["win_evac"], 4 + 2 * b)
                made = [0] * 4
                for j in range(B_CONV):
                    for i in range(4):
                        ct = 4 * b + i
                        src, dst = cin[:, i, j:j + SEQ], cout[:, ct, :]
                        w = vcol[:, V_CW + 8 * j + ct:V_CW + 8 * j + ct + 1]
                        if j == 0:
                            ins = TS(dst, src, w, vcol[:, V_CB + ct:V_CB + ct + 1], ALU.mult, ALU.add)
                        else:
                            dve.wait_ge(S["dve_step"], made[i])
                            ins = STT(dst, src, w, dst, ALU.mult, ALU.add)
                        if j == B_CONV - 1:
                            ins.then_inc(S["conv_done"], 1)
                        else:
                            made[i] = mark(ins)

            for c in range(9):
                ahead(U_WIN + 2 * c + SPLIT)
                if c == 1:
                    lower_bounds()
                if c == 2:
                    gates(0)
                if c == 3:
                    gates(1)
                    scans(0)
                    dve.wait_ge(S["win_evac"], 3)
                    softplus()
                if c == 4:
                    scans(1)
                if c > JOB_ROUND0:
                    for j in (2 * (c - 1 - JOB_ROUND0), 2 * (c - 1 - JOB_ROUND0) + 1):
                        job_evac(j)
                if JOB_ROUND0 <= c < 8:
                    for j in (2 * (c - JOB_ROUND0), 2 * (c - JOB_ROUND0) + 1):
                        job_mul(j)
                if c == 5:
                    softplus2()
                    conv(0)
                if c == 7:
                    softplus3()
                    conv(1)

            dve.wait_ge(S["cols_done"], 1)
            cb = B[4][:, 0:48]
            for t in range(NT):
                TS(Ccol[:, t, 0:8], cb[:, 16 * t:16 * t + 8], 1.0, None, ALU.mult)
                ins = TS(Ccol[:, t, 8:16], cb[:, 16 * t + 8:16 * t + 16], -1.0, None, ALU.mult)
            n = mark(ins)
            dve.wait_ge(S["dve_step"], n)
            TT(Cx[:, 0:8], Ccol[:, 0, 0:8], cb[:, 32:40], ALU.subtract)
            TT(Cx[:, 8:16], Ccol[:, 1, 8:16], cb[:, 40:48], ALU.subtract).then_inc(S["cols_copied"], 1)
            dve.wait_ge(S["rows_turned"], 1)
            dve.tensor_copy(csrow[:, :], B[5][0:16, 0:SEQ]).then_inc(S["rows_copied"], 1)
            dve.wait_ge(S["g_done"], 1)
            for g in range(B_GROUPS):
                bank = B[2 + g]
                TT(Gm[g][:, 0:P], bank[:, 0:P], le[:, :], ALU.mult)
                dve.tensor_copy(Gm[g][:, P:2 * P], bank[:, P:2 * P])
                TT(Gm[g][:, 2 * P:3 * P], bank[:, 3 * P:4 * P], le[:, :], ALU.mult)
                TT(Gm[g][:, 3 * P:4 * P], bank[:, 0:P], ge[:, :], ALU.mult)
                dve.tensor_copy(Gm[g][:, 4 * P:5 * P], bank[:, 2 * P:3 * P])
                TT(Gm[g][:, 5 * P:6 * P], bank[:, 3 * P:4 * P], ge[:, :], ALU.mult).then_inc(S["gm_done"], 1)
            dve.wait_ge(S["xs_turned"], 1)
            for t in range(NT):
                ins = dve.tensor_copy(xsn[:, t, :], B[6 + t][:, :])
            ins.then_inc(S["xs_copied"], 1)
            dve.wait_ge(S["xs_copied"], 1)
            for t in range(NT):
                TT(tmpn[:, t, :].rearrange("p (h c) -> p h c", c=B_HD), xsn[:, t, :].rearrange("p (h c) -> p h c", c=B_HD),
                   db.rearrange("p (h o) -> p h o", o=1).to_broadcast([P, B_HEADS, B_HD]), ALU.mult)

            dve.wait_ge(S["o_copied"], 2)
            oa = xn[:, :, 0:H]
            for t in range(NT):
                ins = TT(squ[:, t, :], xn[:, t, 0:H], xn[:, t, 0:H], ALU.mult)
            link(ins)
            link(dve.tensor_reduce(nrm[:, 0:8], squ.rearrange("p t (h c) -> p (t h) c", c=P), AX.X, ALU.add))
            TS(nrm[:, 0:8], nrm[:, 0:8], 1.0 / P, EPS, ALU.mult, ALU.add).then_inc(S["oa_done"], 1)
            dve.wait_ge(S["root_a"], 1)
            link(dve.reciprocal(nrm[:, 0:8], nrm[:, 0:8]))
            for t in range(NT):
                v = xn[:, t, 0:H].rearrange("p (h c) -> p h c", c=P)
                ins = TT(v, v, nrm[:, 4 * t:4 * t + 4].rearrange("p (h o) -> p h o", o=1).to_broadcast([P, A_HEADS, P]), ALU.mult)
                n = mark(ins)
            dve.wait_ge(S["dve_step"], n)
            for t in range(NT):
                v = xn[:, t, 0:H].rearrange("p (h c) -> p h c", c=P)
                n = mark(TT(v, v, anb.rearrange("p (o c) -> p o c", o=1).to_broadcast([P, A_HEADS, P]), ALU.mult))
            dve.wait_ge(S["dve_step"], n)
            dve.wait_ge(S["win_evac"], 8)
            for t in range(NT):
                ins = TT(xn[:, t, 0:H], xn[:, t, 0:H], vgz[:, 1, t, :], ALU.mult)
            ins.then_inc(S["mix_a"], 1)

            def exponents(h):
                dve.wait_ge(S["rbc_done"], h + 1)
                bank, L = B[2 + h % 2], Lb[h % 2]
                f, b = slice(h, h + 1), slice(8 + h, 9 + h)
                for o, c0, col in ((0, 0, Ccol[:, 0, f]), (1, P, Cx[:, f]), (2, P, Ccol[:, 1, f]),
                                   (3, 2 * P, Ccol[:, 0, b]), (4, 2 * P, Cx[:, b]), (5, 3 * P, Ccol[:, 1, b])):
                    ins = TS(L[:, o * P:(o + 1) * P], bank[:, c0:c0 + P], col, 0.0, ALU.subtract, ALU.min)
                ins.then_inc(S["rbc_used"], 1)

            def scores(h):
                dve.wait_ge(S["l_exp"], h + 1)
                if h >= 2:
                    dve.wait_ge(S["y_pe"], h - 1)
                L, W, g = Lb[h % 2], Wb[h % 2], Gm[h // (B_HEADS // B_GROUPS)]
                for c0, c1, t, k in ((0, 256, 0, h), (256, 384, 1, h), (384, 512, 0, 8 + h), (512, 768, 1, 8 + h)):
                    ins = STT(W[:, c0:c1], L[:, c0:c1], dta[:, t, k:k + 1], g[:, c0:c1], ALU.mult, ALU.mult)
                ins.then_inc(S["w_done"], 1)

            dve.wait_ge(S["gm_done"], 2)
            for h in range(B_HEADS + 1):
                if h < B_HEADS:
                    exponents(h)
                if h:
                    scores(h - 1)
            dve.wait_ge(S["y_pe"], B_HEADS)
            ob = [xn[:, t, H:D] for t in range(NT)]
            for t in range(NT):
                n = mark(TT(ob[t], B[6 + t][:, :], tmpn[:, t, :], ALU.add))
            dve.wait_ge(S["dve_step"], n)
            for t in range(NT):
                n = mark(TT(ob[t], ob[t], vgz[:, 2, t, :], ALU.mult))
            dve.wait_ge(S["dve_step"], n)
            for t in range(NT):
                n = mark(TT(squ[:, t, :], ob[t], ob[t], ALU.mult))
            dve.wait_ge(S["dve_step"], n)
            link(dve.tensor_reduce(nrm[:, 8:12], squ.rearrange("p t (g c) -> p (t g) c", g=2), AX.X, ALU.add))
            TS(nrm[:, 8:12], nrm[:, 8:12], 2.0 / H, EPS, ALU.mult, ALU.add).then_inc(S["ob_done"], 1)
            dve.wait_ge(S["root_b"], 1)
            dve.wait_ge(S["bnb_in"], 16)
            link(dve.reciprocal(nrm[:, 8:12], nrm[:, 8:12]))
            for t in range(NT):
                for g in range(B_GROUPS):
                    c = slice(g * 256, (g + 1) * 256)
                    k = 8 + 2 * t + g
                    ins = STT(ob[t][:, c], ob[t][:, c], nrm[:, k:k + 1], bnb[:, c], ALU.mult, ALU.mult)
            ins.then_inc(S["mix_b"], 1)
            turned(1)
            ahead(U_FFN + SPLIT)

            def bank_src(t, hf):
                return B[2 * hf + t][:, :]
            post(0, bank_src)
            norm(1)
            turned(2, V_GAIN["ffn0"])

            def ff_evac(c, b, loop=None):
                k = lambda v: v if loop is None else loop * 2 + v
                dve.wait_ge(S["ff_silu"], k(c + 1))
                for j in range(2):
                    ins = TT(ffs[:, j, :], ffs[:, j, :], B[2 * b + j][:, SEQ:], ALU.mult)
                ins.then_inc(S["ff_mul"], 1)
                dve.wait_ge(S["ff_hi"], k(c + 1))
                TT(ffl[b][:, :, :], ffs[:, :, :], ffh[b][:, :, :].bitcast(F32), ALU.subtract).then_inc(S["ff_lo"], 1)

            ff_evac(0, 0)
            with dve.Fori(0, (FF_STEPS - 1) // 2) as it:
                for b in range(2):
                    for m in range(3):
                        take_lo(U_FFN + 3 + 3 * b + m, it)
                    ff_evac(1 + b, (1 + b) % 2, it)
            nxt[0] = U_PLE0
            ahead(U_PLE0 + SPLIT)

            def bank_y(t, hf):
                return B[4 + 2 * t + hf][:, :]
            post(1, bank_y)
            norm(2)
            turned(3, V_GAIN["ple0"])

            def ple(n, u0, turns=None):
                dve.wait_ge(S["pT_hi_done"], n + 1)
                TT(pT_lo[n][:, :, :], B[5][:, :].rearrange("p (k t) -> p k t", k=2), pT_hi[n][:, :, :].bitcast(F32),
                   ALU.subtract).then_inc(S["pT_lo_done"], 1)
                ahead(u0 + 5, turns)
                used(dve, u0 + 4, turns)
                dve.wait_ge(S["sig_done"], 2 * n + 2)
                for q in range(4):
                    t, hf = q // 2, q % 2
                    v = gate[n][:, t, hf * H:(hf + 1) * H]
                    TT(v, v, B[4 + 2 * t + hf][:, :], ALU.mult).then_inc(S["ply_done"], 1)

            def gate_src(n):
                return lambda t, hf: gate[n][:, t, hf * H:(hf + 1) * H]

            ple(0, U_PLE0)
            ahead(U_QKV + SPLIT)
            post(2, gate_src(0))
            norm(3)
            turned(4, V_GAIN["mix1"])

            for c in range(6):
                ahead(U_QKV + 2 * c + 2 + SPLIT)
            for h in range(C_HEADS):
                dve.wait_ge(S["s_done"], h + 1)
                if h >= 2:
                    dve.wait_ge(S["e_done"], 2 * (h - 1))
                link(STT(sc[h % 2][:, :, :].rearrange("p t s -> p (t s)"), B[h % 2][:, :], C_HD ** -0.5,
                         bias[:, h, :, :].rearrange("p t s -> p (t s)"), ALU.mult, ALU.add))
                dve.tensor_reduce(nmax[:, h, :], sc[h % 2][:, :, :], AX.X, ALU.max, negate=True).then_inc(S["nm_done"], 1)
            dve.wait_ge(S["e_done"], 2 * C_HEADS)
            link(dve.reciprocal(rden[:, :, :], den[:, :, :]))
            for half in range(2):
                dve.wait_ge(S["oc_done"], 8 * half + 8)
                for t in range(NT):
                    r_ = rden[:, t, 8 * half:8 * half + 8].rearrange("p (h o) -> p h o", o=1).to_broadcast([P, 8, C_HD])
                    TT(xn[:, t, half * H:(half + 1) * H].rearrange("p (h c) -> p h c", c=C_HD),
                       B[4 + 2 * half + t][:, :].rearrange("p (h c) -> p h c", c=C_HD), r_, ALU.mult).then_inc(S["oc_norm"], 1)
            turned(5)
            ahead(U_MOE + 1)
            post(3, bank_src)
            norm(4)

            dve.wait_ge(S["xn_dve"], 2 * 4 + 2)
            dve.wait_ge(S["xn_act"], 5)
            dve.wait_ge(gb_in[0], 16 * 3)
            for t in range(NT):
                n = mark(TT(xn[:, t, :], xn[:, t, :], gb[0][:, :], ALU.mult))
            dve.wait_ge(S["dve_step"], n)
            dve.sem_inc(S["xg_ready"], 1)
            dve.wait_ge(S["xgh_done"], 1)
            TT(xg_lo[:, :, :], xn[:, :, :], xg_hi[:, :, :].bitcast(F32), ALU.subtract).then_inc(S["xgl_done"], 1)
            dve.wait_ge(S["lg_done"], 1)
            link(dve.tensor_copy(lg[:, :, :], B[5][:, 0:16].rearrange("p (t e) -> p t e", t=NT)))
            for t in range(NT):
                n = mark(dve.max(mx8[:, t, :], lg[:, t, :]))
            dve.wait_ge(S["dve_step"], n)
            TT(r1[:, 0, :, 0:1], mx8[:, :, 1:2], mx8[:, :, 0:1], ALU.subtract).then_inc(S["top_done"], 1)
            for t in range(NT):
                n = mark(dve.max_index(ix8[:, t, :], mx8[:, t, :], lg[:, t, :]))
            dve.wait_ge(S["dve_step"], n)
            link(dve.tensor_copy(ixf[:, :, :], ix8[:, :, :]))
            dve.wait_ge(S["moe_consts"], 3)
            for c in range(2):
                for t in range(NT):
                    n = mark(TS(oh[:, c, t, :], iota_f[:, 0:8], ixf[:, t, c:c + 1], None, ALU.is_equal))
            dve.wait_ge(S["dve_step"], n)
            TT(msk[:, :, :], oh[:, 0, :, :], oh[:, 1, :, :], ALU.add).then_inc(S["mask_done"], 1)
            dve.wait_ge(S["top_exp"], 1)
            link(TS(r1[:, 2, :, 0:1], r1[:, 1, :, 0:1], 1.0, None, ALU.add))
            link(dve.reciprocal(r1[:, 3, :, 0:1], r1[:, 2, :, 0:1]))
            link(TT(r1[:, 4, :, 0:1], r1[:, 3, :, 0:1], r1[:, 1, :, 0:1], ALU.mult))
            for t in range(NT):
                link(TS(r1[:, 5, t, :], oh[:, 1, t, :], r1[:, 4, t, 0:1], None, ALU.mult))
                link(STT(gat[:, t, 0:8], oh[:, 0, t, :], r1[:, 3, t, 0:1], r1[:, 5, t, :], ALU.mult, ALU.add))
            dve.wait_ge(S["pos_done"], 1)
            pos = B[4][:, 0:16].rearrange("p (t e) -> p t e", t=NT)
            link(TS(r1[:, 6, :, :], pos, 1.0, None, ALU.add))
            link(TT(r1[:, 6, :, :], r1[:, 6, :, :], msk[:, :, :], ALU.mult))
            link(TS(posx[:, :, 0:8], r1[:, 6, :, :], -1.0, None, ALU.add))
            link(dve.tensor_copy(cnt[:, :], B[4][:, 16:24]))
            link(TS(flag[:, :], cnt[:, :], float(P), None, ALU.is_gt))
            link(dve.memset(fpos[:, 0:1], 0.0))
            link(dve.tensor_tensor_scan(fpos[:, 1:9], ones[:, 0:8], flag[:, :], 0.0, ALU.mult, ALU.add))
            link(TS(r1[:, 7, :, :], msk[:, :, :], -float(P), None, ALU.mult))
            link(TT(r1[:, 7, :, :], r1[:, 7, :, :], r1[:, 6, :, :], ALU.add))
            link(dve.memset(posx[:, :, 8:12], -1.0))
            link(dve.memset(gat[:, :, 8:12], 0.0))
            for k in range(3):
                link(TS(ohx[:, k, :], fpos[:, 0:8], float(k), None, ALU.is_equal))
                link(TT(ohx[:, k, :], ohx[:, k, :], flag[:, :], ALU.mult))
                o8 = ohx[:, k, :]
                for t in range(NT):
                    link(TT(r1[:, 5, t, :], o8, r1[:, 7, t, :], ALU.mult))
                    link(dve.tensor_reduce(posx[:, t, 8 + k:9 + k], r1[:, 5, t, :], AX.X, ALU.add))
                    link(TS(posx[:, t, 8 + k:9 + k], posx[:, t, 8 + k:9 + k], -1.0, None, ALU.add))
                    link(TT(r1[:, 5, t, :], o8, gat[:, t, 0:8], ALU.mult))
                    link(dve.tensor_reduce(gat[:, t, 8 + k:9 + k], r1[:, 5, t, :], AX.X, ALU.add))
                link(TT(r1[:, 5, 0, :], o8, iota_f[:, 0:8], ALU.mult))
                link(dve.tensor_reduce(itf[:, 8 + k:9 + k], r1[:, 5, 0, :], AX.X, ALU.add))
            link(TS(itf[:, 12:13], fpos[:, 8:9], float(N_EXPERTS), None, ALU.add))
            link(dve.tensor_copy(items[0:1, :], itf[0:1, :]))
            dve.sem_inc(S["items_ready"], 1)
            n_items = dve.value_load(items[0:1, 12:13], min_val=N_EXPERTS, max_val=MAX_ITEMS)

            def build_sel(i):
                for t in range(NT):
                    TS(sel[:, t, :], iota_f[:, :], posx[:, t, bass.ds(i, 1)], None, ALU.is_equal)
                dve.tensor_copy(gcol[:, :, :], gat[:, :, bass.ds(i, 1)]).then_inc(S["sel_built"], 1)

            def gather_evac(k):
                dve.wait_ge(S["geh"], k)
                for b in range(2):
                    ins = TT(he_lo[:, 4 * b:4 * b + 4, :], B[5 + b][:, :].rearrange("p (k s) -> p k s", k=4),
                             he_hi[:, 4 * b:4 * b + 4, :].bitcast(F32), ALU.subtract)
                ins.then_inc(S["gel"], 1)

            def product(k, u, turns):
                dve.wait_ge(S["esilu"], k)
                used(dve, u + 3, turns)
                TT(ea[:, :], es[:, :], B[1][:, :], ALU.mult).then_inc(S["emul"], 1)

            def turned_lo(u):
                dve.wait_ge(S["ehi"], u)
                TT(eT_lo[:, :, :], B[4][:, :].rearrange("p (k s) -> p k s", k=4), eT_hi[:, :, :].bitcast(F32),
                   ALU.subtract).then_inc(S["elo"], 1)

            def y_low(i):
                dve.wait_ge(S["yhi"], i + 1)
                for hf in range(2):
                    c = slice(hf * H, (hf + 1) * H)
                    ins = STT(y_lo[:, c], B[2 + hf][:, :], gslot[:, 0:1], y_hi[:, c].bitcast(F32), ALU.mult, ALU.subtract)
                ins.then_inc(S["ylo"], 1)

            COMB = [B[5], B[6], B[7], B[3]]

            def add_item(i, s=None):
                dve.wait_ge(S["comb_done"], i + 2)
                for q in range(4):
                    t, hf = q // 2, q % 2
                    v = acc[:, t, hf * H:(hf + 1) * H]
                    ins = TT(v, v, COMB[q][:, :], ALU.add)
                    if s:
                        ins.then_inc(s, 1)
                return ins

            dve.memset(B[2][:, :], 0.0)
            dve.memset(B[3][:, :], 0.0)
            dve.memset(gslot[:, :], 0.0).then_inc(S["selT_copied"], 1)
            build_sel(0)
            gather_evac(1)
            dve.wait_ge(S["moe_init"], 3)
            with dve.Fori(0, n_items) as i:
                turns = i * FE_STEPS
                take_lo(U_MOE + 1, turns)
                take_lo(U_MOE + 2, turns)
                y_low(i)
                take_lo(U_MOE + 3, turns)
                take_lo(U_MOE + 4, turns)
                product(turns + 1, U_MOE, turns)
                add_item(i).then_inc(S["comb_added"], 1)
                dve.wait_ge(S["selT_done"], i + 1)
                dve.tensor_copy(selT[:, :], B[2][:, 0:SEQ])
                dve.tensor_copy(gslot[:, :], B[2][:, SEQ:SEQ + 1]).then_inc(S["selT_copied"], 1)
                build_sel(i + 1)
                with dve.Fori(1, FE_STEPS) as f:
                    done = turns + f
                    take_lo(U_STEP + 1, done)
                    take_lo(U_STEP + 2, done)
                    turned_lo(done)
                    for k in range(3, 7):
                        take_lo(U_STEP + k, done)
                    product(done + 1, U_STEP, done)
                take_lo(U_TAIL + 1, turns + (FE_STEPS - 1))
                turned_lo(turns + FE_STEPS)
                gather_evac(i + 2)
                take_lo(U_TAIL + 2, turns + (FE_STEPS - 1))
            y_low(n_items + 0)
            all_turns = n_items * FE_STEPS
            nxt[0] = U_MOE + 1
            ahead(U_MOE + SPLIT, all_turns)
            add_item(n_items + 0, S["moe_acc"])
            post(4, lambda t, hf: acc[:, t, hf * H:(hf + 1) * H])
            norm(5)
            turned(6, V_GAIN["ple1"])
            ple(1, U_MOE, all_turns)
            post(5, gate_src(1))

        @block.tensor
        def _(pe):
            def mm(o, l, r, first, last=False):
                return pe.matmul(o, l, r, start=first, stop=last, skip_group_check=True)

            def mm3(o, l, r, first, last=False):
                mm(o, l[0], r[0], first)
                mm(o, l[0], r[1], False)
                return mm(o, l[1], r[0], False, last)

            def unit_ready(u, turns=None):
                pe.wait_ge(S["lo_ready"], unit_count(u + 1, turns))

            def parts(u, k):
                return views(hi[u % SPLIT], k), views(lo[u % SPLIT], k)

            def turn(m, src_ready, n_banks=2):
                src_ready()
                for j in range(4):
                    if j >= 2 or m:
                        pe.wait_ge(S["hT_lo_done"], 4 * m + j - 1)
                    for b in range(2):
                        for t in range(NT):
                            kt = 2 * j + b
                            ins = pe.transpose(B[6 + j % 2][:, b * SEQ + t * P:b * SEQ + (t + 1) * P],
                                               xn[:, t, kt * P:(kt + 1) * P], ident[:, :])
                    ins.then_inc(S["turned"], 1)

            def normed(n):
                def w():
                    pe.wait_ge(S["xn_dve"], 2 * n + 2)
                    pe.wait_ge(S["xn_act"], n + 1)
                return w

            def weights_still(u, hf, banks):
                w = parts(u, 4)
                for ct in range(4):
                    for kk in range(4):
                        o = banks[ct // 2][:, (ct % 2) * SEQ:(ct % 2 + 1) * SEQ]
                        l = [v[:, kk, ct * P:(ct + 1) * P] for v in w]
                        r = [hT_hi[:, 4 * hf + kk, :], hT_lo[:, 4 * hf + kk, :]]
                        ins = mm3(o, l, r, hf == 0 and kk == 0 and ct % 2 == 0, hf == 1 and kk == 3)
                return ins

            def tokens_still(u, k, kt0, outs, src, first, last, n_cols=H):
                w = parts(u, k)
                for bank, t, c0 in outs:
                    for kk in range(k):
                        l = [v[:, kt0 + kk, t * P:(t + 1) * P] for v in src]
                        r = [v[:, kk, c0:c0 + n_cols] for v in w]
                        ins = mm3(bank[:, 0:n_cols], l, r, first and kk == 0, last and kk == k - 1)
                return ins

            hT = (hT_hi[:, :, :], hT_lo[:, :, :])

            pe.wait_ge(S["ident_ready"], 1)
            pe.wait_ge(S["vrow_in"], 16 * 8)
            pe.transpose(B[7][:, 0:V_N], vrow, ident[0:V_N, 0:V_N]).then_inc(S["vcol_t"], 1)
            pe.wait_ge(S["vcol_ready"], 1)
            turn(0, normed(0))

            def job(j):
                d, lv = JOBS[j]
                pe.wait_ge(S["job_mul"], j + 1)
                E = EB[JBUF[j][0] % 4]
                for n, w in enumerate(JBANK[j]):
                    if w >= 4:
                        pe.wait_ge(S["job_evac"], w - 3)
                    bank = B[4 + w % 4]
                    own = slice(n * P, (n + 1) * P)
                    for h in range(A_HEADS):
                        if lv == 0:
                            eq, ek = (E, EB[JBUF[j][1] % 4]) if d == 0 else (EB[JBUF[j][1] % 4], E)
                            l, r = ek[:, h, own], eq[:, h, own]
                        elif lv < 128:
                            l = r = E[:, h, own]
                        else:
                            l, r = (E[:, h, 0:P], E[:, h, P:]) if d == 0 else (E[:, h, P:], E[:, h, 0:P])
                        ins = mm(bank[:, h * P:(h + 1) * P], l, r, h == 0, True)
                ins.then_inc(S["job_pe"], 1)

            pe.wait_ge(S["hT_lo_done"], 4)
            for c, (name, _) in enumerate(WIN_GROUPS):
                still = name not in ("v", "g", "z")
                banks = [B[2 * (c % 2)], B[2 * (c % 2) + 1]]
                if c >= 2:
                    pe.wait_ge(S["win_evac"], c - 1)
                for hf in range(2):
                    u = U_WIN + 2 * c + hf
                    unit_ready(u)
                    if still:
                        ins = weights_still(u, hf, banks)
                    else:
                        ins = tokens_still(u, 4, 4 * hf, [(banks[t], t, 0) for t in range(NT)], hT, hf == 0, hf == 1)
                    ins.then_inc(S["unit_used"], 1)
                if c == 2:
                    pe.wait_ge(S["wdt_lo_done"], 1)
                    for t in range(NT):
                        for kt in range(KT):
                            l = [v[:, kt, t * P:(t + 1) * P] for v in hT]
                            ins = mm3(B[5][:, t * 16:(t + 1) * 16], l, [wdt_hi[:, kt, :], wdt_lo[:, kt, :]],
                                      t == 0 and kt == 0, kt == KT - 1)
                    ins.then_inc(S["dt_mm"], 1)
                if c >= JOB_ROUND0:
                    if c == JOB_ROUND0:
                        pe.wait_ge(S["dt_ready"], 1)
                    for j in (2 * (c - JOB_ROUND0), 2 * (c - JOB_ROUND0) + 1):
                        job(j)

            pe.wait_ge(S["job_evac"], JBANK[-1][-1] + 1)
            pe.wait_ge(S["win_evac"], 7)
            for t in range(NT):
                for h in range(A_HEADS):
                    for s_ in range(NT):
                        ins = mm(B[t][:, h * P:(h + 1) * P], AT[:, h, s_, t * P:(t + 1) * P],
                                 vgz[:, 0, s_, h * P:(h + 1) * P], h == 0 and s_ == 0, s_ == NT - 1)
            ins.then_inc(S["o_done"], 1)

            pe.wait_ge(S["dt_ready"], 3)
            for t in range(NT):
                mm(B[4][:, 16 * t:16 * t + 8], le[:, :], acs[:, t, 0:8], t == 0, True)
                mm(B[4][:, 16 * t + 8:16 * t + 16], lt[:, :], acs[:, t, 8:16], False, True)
            mm(B[4][:, 32:48], ones[:, :], acs[:, 0, :], False, True).then_inc(S["cols_done"], 1)
            pe.wait_ge(S["conv_silu"], 2)
            pe.wait_ge(S["win_evac"], 8)
            for g in range(B_GROUPS):
                for s_ in range(NT):
                    ins = mm(B[2 + g][:, s_ * SEQ:(s_ + 1) * SEQ], cout[:, 4 + g, s_ * P:(s_ + 1) * P], cout[:, 6 + g, :],
                             s_ == 0, True)
            ins.then_inc(S["g_done"], 1)
            for t in range(NT):
                for ct in range(4):
                    ins = pe.transpose(B[6 + t][:, ct * P:(ct + 1) * P], cout[:, ct, t * P:(t + 1) * P], ident[:, :])
            ins.then_inc(S["xs_turned"], 1)
            pe.wait_ge(S["cols_copied"], 1)
            for t in range(NT):
                ins = pe.transpose(B[5][0:16, t * P:(t + 1) * P], Ccol[:, t, :], ident[:, :])
            ins.then_inc(S["rows_turned"], 1)

            def rbc(h):
                if h >= 2:
                    pe.wait_ge(S["rbc_used"], h - 1)
                for d in range(2):
                    k = 8 * d + h
                    ins = mm(B[2 + h % 2][:, d * SEQ:(d + 1) * SEQ], ident[0:16, k:k + 1].to_broadcast([16, P]),
                             csrow[:, :], d == 0, True)
                ins.then_inc(S["rbc_done"], 1)

            pe.wait_ge(S["rows_copied"], 1)
            pe.wait_ge(S["gm_done"], 2)
            rbc(0)
            rbc(1)
            pe.wait_ge(S["xs_copied"], 1)
            for h in range(B_HEADS):
                pe.wait_ge(S["w_done"], h + 1)
                W = Wb[h % 2]
                for t, blocks in ((0, ((0, 0), (3, 0), (4, 1))), (1, ((1, 0), (2, 1), (5, 1)))):
                    for n, (blk, s_) in enumerate(blocks):
                        ins = mm(B[6 + t][:, h * B_HD:(h + 1) * B_HD], W[:, blk * P:(blk + 1) * P],
                                 xsn[:, s_, h * B_HD:(h + 1) * B_HD], h == 0 and n == 0, n == 2)
                ins.then_inc(S["y_pe"], 1)
                if h + 2 < B_HEADS:
                    rbc(h + 2)

            def mixed():
                pe.wait_ge(S["mix_a"], 1)
                pe.wait_ge(S["mix_b"], 1)
            turn(1, mixed)

            def square(u0, m):
                pe.wait_ge(S["hT_lo_done"], 4 * m + 4)
                for c in range(2):
                    for hf in range(2):
                        u = u0 + 2 * c + hf
                        unit_ready(u)
                        tokens_still(u, 4, 4 * hf, [(B[2 * c + t], t, 0) for t in range(NT)], hT,
                                     hf == 0, hf == 1).then_inc(S["unit_used"], 1)

            square(U_WOUT0, 1)
            turn(2, normed(1))

            pe.wait_ge(S["hT_lo_done"], 12)
            def ff_up(u, m, b, turns):
                unit_ready(u, turns)
                w = parts(u, KT)
                for j in range(2):
                    for kt in range(KT):
                        l = [v[:, kt, j * P:(j + 1) * P] for v in w]
                        ins = mm3(B[2 * b + j][:, m * SEQ:(m + 1) * SEQ], l, [hT_hi[:, kt, :], hT_lo[:, kt, :]],
                                  m == 0 and kt == 0, kt == KT - 1)
                ins.then_inc(S["unit_used"], 1)

            def ff_down(u, b, turns, first):
                unit_ready(u, turns)
                w = parts(u, 2)
                for t in range(NT):
                    for hf in range(2):
                        for j in range(2):
                            l = [ffh[b][:, j, t * P:(t + 1) * P], ffl[b][:, j, t * P:(t + 1) * P]]
                            ins = mm3(B[4 + 2 * t + hf][:, :], l, [v[:, j, hf * H:(hf + 1) * H] for v in w],
                                      first and j == 0)
                return ins.then_inc(S["unit_used"], 1)

            def ff_step(c, b, loop=None, first=False):
                k = lambda v: v if loop is None else loop * 2 + v
                base = U_FFN + 2 + 3 * (c - 1)
                for m in range(2):
                    ff_up(base + m, m, b, loop)
                pe.wait_ge(S["ff_lo"], k(c))
                ff_down(base + 2, 1 - b, loop, first)

            for m in range(2):
                ff_up(U_FFN + m, m, 0, None)
            ff_step(1, 1, None, True)
            ff_step(2, 0)
            with pe.Fori(1, (FF_STEPS - 1) // 2) as it:
                ff_step(1, 1, it)
                ff_step(2, 0, it)
            pe.wait_ge(S["ff_lo"], FF_STEPS)
            ff_down(U_PLE0 - 1, 0, None, False)
            turn(3, normed(2))

            def ple(n, u0, m, turns=None):
                pe.wait_ge(S["p_in"], 16 * (n + 1))
                for k in range(2):
                    for t in range(NT):
                        ins = pe.transpose(B[5][:, k * SEQ + t * P:k * SEQ + (t + 1) * P],
                                           pin[n][:, t, k * P:(k + 1) * P], ident[:, :])
                ins.then_inc(S["p_turned"], 1)
                pe.wait_ge(S["hT_lo_done"], 4 * m + 4)
                for c in range(2):
                    for hf in range(2):
                        u = u0 + 2 * c + hf
                        unit_ready(u, turns)
                        tokens_still(u, 4, 4 * hf, [(B[2 * c + t], t, 0) for t in range(NT)], hT,
                                     hf == 0, hf == 1).then_inc(S["unit_used"], 1)
                u = u0 + 4
                unit_ready(u, turns)
                pe.wait_ge(S["pT_lo_done"], n + 1)
                outs = [(B[4 + 2 * t + hf], t, hf * H) for t in range(NT) for hf in range(2)]
                tokens_still(u, 2, 0, outs, (pT_hi[n][:, :, :], pT_lo[n][:, :, :]), True, True).then_inc(S["unit_used"], 1)

            ple(0, U_PLE0, 3)
            turn(4, normed(3))

            pe.wait_ge(S["hT_lo_done"], 20)
            for c in range(6):
                banks = [B[2 * (c % 2)], B[2 * (c % 2) + 1]]
                if c >= 2:
                    pe.wait_ge(S["qkv_evac"], c - 1)
                for hf in range(2):
                    u = U_QKV + 2 * c + hf
                    unit_ready(u)
                    if c < 4:
                        ins = weights_still(u, hf, banks)
                    else:
                        ins = tokens_still(u, 4, 4 * hf, [(banks[t], t, 0) for t in range(NT)], hT, hf == 0, hf == 1)
                    ins.then_inc(S["unit_used"], 1)
            pe.wait_ge(S["qkv_evac"], 6)

            def attn_scores(h):
                if h >= 2:
                    pe.wait_ge(S["nm_done"], h - 1)
                p0, kt = C_HD * (h % 2), h // 2
                for t in range(NT):
                    ins = mm(B[h % 2][:, t * SEQ:(t + 1) * SEQ], qcT[p0:p0 + C_HD, kt, t * P:(t + 1) * P],
                             kcT[p0:p0 + C_HD, kt, :], t == 0, True)
                ins.then_inc(S["s_done"], 1)

            def attn_turn(h):
                pe.wait_ge(S["e_done"], 2 * h + 2)
                if h >= 2:
                    pe.wait_ge(S["pt_copied"], h - 1)
                for s_ in range(NT):
                    for t in range(NT):
                        ins = pe.transpose(B[2 + h % 2][:, s_ * SEQ + t * P:s_ * SEQ + (t + 1) * P],
                                           pr[h % 2][:, t, s_ * P:(s_ + 1) * P], ident[:, :])
                ins.then_inc(S["pt_done"], 1)

            def attn_out(h):
                pe.wait_ge(S["pt_copied"], h + 1)
                for t in range(NT):
                    for s_ in range(NT):
                        ins = mm(B[4 + 2 * (h // 8) + t][:, (h % 8) * C_HD:(h % 8 + 1) * C_HD],
                                 prT[h % 2][:, s_, t * P:(t + 1) * P], vc[:, s_, h * C_HD:(h + 1) * C_HD],
                                 h % 8 == 0 and s_ == 0, s_ == NT - 1)
                ins.then_inc(S["oc_done"], 1)

            for i in range(C_HEADS + 3):
                if i < C_HEADS:
                    attn_scores(i)
                if 2 <= i < C_HEADS + 2:
                    attn_turn(i - 2)
                if i >= 3:
                    attn_out(i - 3)
            turn(5, lambda: pe.wait_ge(S["oc_norm"], 4))
            square(U_WOUT1, 5)

            pe.wait_ge(S["xg_ready"], 1)
            for j in range(4):
                if j >= 2:
                    pe.wait_ge(S["hF_copied"], j - 1)
                for b in range(2):
                    for t in range(NT):
                        kt = 2 * j + b
                        ins = pe.transpose(B[6 + j % 2][:, b * SEQ + t * P:b * SEQ + (t + 1) * P],
                                           xn[:, t, kt * P:(kt + 1) * P], ident[:, :])
                ins.then_inc(S["hF_turned"], 1)
            pe.wait_ge(S["hF_copied"], 4)
            pe.wait_ge(S["wr_in"], 16)
            for t in range(NT):
                for kt in range(KT):
                    ins = mm(B[5][:, t * 8:t * 8 + 8], hF[:, kt, t * P:(t + 1) * P], wr[:, kt, :],
                             t == 0 and kt == 0, kt == KT - 1)
            ins.then_inc(S["lg_done"], 1)
            pe.wait_ge(S["mask_done"], 1)
            mm(B[4][:, 0:8], lt[:, :], msk[:, 0, :], True, True)
            mm(B[4][:, 8:16], lt[:, :], msk[:, 1, :], False)
            mm(B[4][:, 8:16], ones[:, :], msk[:, 0, :], False, True)
            mm(B[4][:, 16:24], ones[:, :], msk[:, 0, :], False)
            mm(B[4][:, 16:24], ones[:, :], msk[:, 1, :], False, True).then_inc(S["pos_done"], 1)
            pe.wait_ge(S["items_ready"], 1)
            n_items = pe.value_load(items[0:1, 12:13], min_val=N_EXPERTS, max_val=MAX_ITEMS)

            def gather(k):
                pe.wait_ge(S["sel_built"], k)
                for kt in range(KT):
                    for t in range(NT):
                        for n, v in enumerate((xg_hi, xg_lo)):
                            ins = mm(B[5 + kt // 4][:, (kt % 4) * P:(kt % 4 + 1) * P], v[:, t, kt * P:(kt + 1) * P],
                                     sel[:, t, :], kt % 4 == 0 and t == 0 and n == 0, t == NT - 1 and n == 1)
                ins.then_inc(S["gath_done"], 1)

            he = (he_hi[:, :, :], he_lo[:, :, :])

            def gate_up(u, turns):
                for m in range(2):
                    for hf in range(2):
                        unit_ready(u + 2 * m + hf, turns)
                        w = parts(u + 2 * m + hf, 4)
                        for kk in range(4):
                            ins = mm3(B[m][:, :], [v[:, 4 * hf + kk, :] for v in he], [v[:, kk, :] for v in w],
                                      hf == 0 and kk == 0, hf == 1 and kk == 3)
                        ins.then_inc(S["unit_used"], 1)

            def turn_product(k):
                pe.wait_ge(S["emul"], k)
                for j in range(4):
                    ins = pe.transpose(B[4][:, j * P:(j + 1) * P], ea[:, j * P:(j + 1) * P], ident[:, :])
                ins.then_inc(S["eturned"], 1)

            def down(u, turns, k, first=False):
                pe.wait_ge(S["elo"], k)
                for n in range(2):
                    unit_ready(u + n, turns)
                    w = parts(u + n, 2)
                    for hf in range(2):
                        for kk in range(2):
                            l = [v[:, 2 * n + kk, :] for v in (eT_hi, eT_lo)]
                            ins = mm3(B[2 + hf][:, :], l, [v[:, kk, hf * H:(hf + 1) * H] for v in w], first and n == 0 and kk == 0)
                    ins.then_inc(S["unit_used"], 1)

            COMB = [B[5], B[6], B[7], B[3]]

            def combine(i):
                pe.wait_ge(S["ylo"], i + 1)
                for q in range(4):
                    t, hf = q // 2, q % 2
                    for n, v in enumerate((y_hi, y_lo)):
                        ins = mm(COMB[q][:, :], selT[:, t * P:(t + 1) * P], v[:, hf * H:(hf + 1) * H], n == 0, n == 1)
                ins.then_inc(S["comb_done"], 1)

            gather(1)
            pe.sem_inc(S["comb_done"], 1)
            pe.wait_ge(S["moe_init"], 3)
            with pe.Fori(0, n_items) as i:
                turns = i * FE_STEPS
                pe.wait_ge(S["gel"], i + 1)
                gate_up(U_MOE, turns)
                combine(i)
                for t in range(NT):
                    pe.transpose(B[2][:, t * P:(t + 1) * P], sel[:, t, :].bitcast(F32), ident[:, :])
                for t in range(NT):
                    ins = mm(B[2][:, SEQ:SEQ + 1], sel[:, t, :].bitcast(F32), gcol[:, t, :], False if t else True, t == 1)
                ins.then_inc(S["selT_done"], 1)
                turn_product(turns + 1)
                gate_up(U_MOE + 4, turns)
                pe.wait_ge(S["selT_copied"], i + 2)
                down(U_MOE + 8, turns, turns + 1, True)
                with pe.Fori(2, FE_STEPS) as f:
                    done = turns + f
                    turn_product(done)
                    gate_up(U_STEP, done)
                    down(U_STEP + 4, done, done)
                turn_product(turns + FE_STEPS)
                gather(i + 2)
                down(U_TAIL, turns + (FE_STEPS - 1), turns + FE_STEPS)
            combine(n_items + 0)
            all_turns = n_items * FE_STEPS
            turn(6, normed(5))
            ple(1, U_MOE, 6, all_turns)


_INS = ["x", "p", "hgrn_lb_raw", "e_norm_mix_pre", "e_w_in", "e_conv_w", "e_conv_b", "e_A_log", "e_dt_bias", "e_D",
        "e_a_norm", "e_b_norm", "e_w_out", "e_norm_mix_post", "e_norm_ffn_pre", "e_w_ffn_gate", "e_w_ffn_up",
        "e_w_ffn_down", "e_norm_ffn_post", "o_norm_mix_pre", "o_w_qkv", "o_rpb", "o_w_out", "o_norm_mix_post",
        "o_norm_ffn_pre", "o_w_router", "o_w_exp_gate", "o_w_exp_up", "o_w_exp_down", "o_norm_ffn_post",
        "ple_norm_in", "ple_w_gate", "ple_w_proj", "ple_norm_post"]


def kernel(**inputs):
    import concourse.bacc as bacc
    from concourse.bass_utils import run_bass_kernel_spmd

    nc = bacc.Bacc("TRN2", target_bir_lowering=False, num_devices=1)
    arrays, args = {}, {}
    for name in _INS:
        v = np.ascontiguousarray(inputs[name])
        arrays[f"in_{name}"] = v
        args[name] = nc.dram_tensor(f"in_{name}", v.shape, mybir.dt.from_np(v.dtype), kind="ExternalInput").ap()
    out = nc.dram_tensor("out", (1, SEQ, D), F32, kind="ExternalOutput").ap()
    trunk(nc, args, out)
    r = run_bass_kernel_spmd(nc, [arrays], core_ids=[0])
    return r.results[0]["out"]
```

```python
from contextlib import ExitStack

import concourse.bass as bass
import numpy as np
from concourse import mybir

P = 128
SEQ = 256
NT = SEQ // P
D = 1024
KT = D // P
GRID_W = 64
EPS = 1e-6
A_HEADS, A_DK = 4, 128
B_HEADS, B_HD, B_GROUPS, B_CONV = 8, 64, 2, 5
C_HEADS, C_HD = 16, 64
NA_ROWS, NA_COLS = 8, 16
RPB_W = 2 * NA_COLS - 1
RPB_H = (2 * NA_ROWS - 1) * RPB_W
D_FF = 2816
N_EXPERTS, D_FFE = 8, 3584
WIN = 3 * RPB_W + GRID_W
P_DIM = 256
H = 512
UNIT = 2048
RAW, SPLIT = 6, 3
FF_STEP = 256
FF_STEPS = D_FF // FF_STEP
FE_STEPS = D_FFE // H
MAX_ITEMS = N_EXPERTS + 3
NEG = -1e30

F32 = mybir.dt.float32
F32R = mybir.dt.float32r
I32 = mybir.dt.int32
U32 = mybir.dt.uint32
ALU = mybir.AluOpType
ACT = mybir.ActivationFunctionType
AX = mybir.AxisListType

U_WIN = 0
U_WOUT0 = U_WIN + 16
U_FFN = U_WOUT0 + 4
U_PLE0 = U_FFN + 3 * FF_STEPS
U_QKV = U_PLE0 + 5
U_WOUT1 = U_QKV + 12
U_MOE = U_WOUT1 + 4
U_STEP = U_MOE + 4 - RAW
U_TAIL = U_MOE + 4

V_GAIN = {"mix0": 0, "ffn0": 8, "ple0": 16, "mix1": 24, "ple1": 32}
V_LB = 40
V_CW = 52
V_CB = 92
V_N = 100

QUARTERS = [(t, hf) for hf in range(2) for t in range(NT)]

WIN_GROUPS = [("ff", 512), ("fb", 1024), ("q", 0), ("xs", 3072), ("v", 1536),
              ("bc", 3584), ("g", 2048), ("z", 2560)]
DT_COL = 4096

JOBS = [(d, lv) for d in (0, 1) for lv in (0, 16, 32, 64, 128)]
JOB_ROUND0 = 3


def job_buffers():
    out, w = [], 0
    for _, lv in JOBS:
        n = 2 if lv == 0 else 1
        out.append(list(range(w, w + n)))
        w += n
    return out


def job_banks():
    out, w = [], 0
    for _, lv in JOBS:
        n = 1 if lv == 128 else 2
        out.append(list(range(w, w + n)))
        w += n
    return out


JBUF, JBANK = job_buffers(), job_banks()
JOB_OF_BUF = {w: j for j, ws in enumerate(JBUF) for w in ws}


def trunk(nc, a, out):
    ctx = ExitStack()
    with ctx:
        def sb(name, shape, dt=F32, stack=None):
            return (stack or ctx).enter_context(nc.sbuf_tensor(name, shape, dt))

        raw = [sb(f"raw{i}", [P, UNIT]) for i in range(RAW)]
        hi = [sb(f"hi{i}", [P, UNIT], F32R) for i in range(SPLIT)]
        lo = [sb(f"lo{i}", [P, UNIT], F32R) for i in range(SPLIT)]
        x = sb("x", [P, NT, D])
        xn = sb("xn", [P, NT, D])
        hT_hi = sb("hT_hi", [P, KT, SEQ], F32R)
        hT_lo = sb("hT_lo", [P, KT, SEQ], F32R)
        gb = [sb(f"gb{i}", [P, D]) for i in range(2)]
        ident = sb("ident", [P, P])
        ones = sb("ones", [P, P])
        ident_r = sb("ident_r", [P, 16], F32R)
        le_ge = sb("le_ge", [P, NT, P])
        le = le_ge[:, 0, :]
        ge = le_ge[:, 1, :]
        lt = sb("lt", [P, P])
        vcol = sb("vcol", [P, V_N])
        sums = sb("sums", [P, 4])
        sums_e = sb("sums_e", [P, NT])
        root = sb("root", [P, NT + 1])
        rstd = sb("rstd", [P, NT])

        s0 = ExitStack()
        vrow = xn[0:V_N, 0, 0:P]
        qT = sb("qT", [P, A_HEADS, SEQ], F32, s0)
        kT = [sb(f"kT{d}", [P, A_HEADS, SEQ], F32, s0) for d in (0, 1)]
        G = [sb(f"G{d}", [P, A_HEADS, SEQ], F32, s0) for d in (0, 1)]
        PS = [sb(f"PS{d}", [P, A_HEADS, SEQ], F32, s0) for d in (0, 1)]
        E2 = sb("E2", [P, A_HEADS, SEQ], F32, s0)
        cout = sb("cout", [P, 8, SEQ], F32, s0)
        diags = [cout[:, 0:1, :].rearrange("p o (t s) -> p (o t) s", t=NT)] + [le_ge[:, :, :]] * 5
        gb1_as_e = gb[1][:, :].rearrange("p (h t) -> p h t", h=A_HEADS)
        EB = [G[0][:, :, :], E2[:, :, :], gb1_as_e, G[1][:, :, :]]
        AT = xn[:, :, :].rearrange("p a d -> p (a d)").rearrange("p (h s t) -> p h s t", h=A_HEADS, s=NT)
        AT2 = sb("AT2", [P, A_HEADS, P], F32, s0)
        btot = sb("btot", [P, A_HEADS, 1], F32, s0)
        hmask = {(d, lv): sb(f"hmask{d}_{lv}", [P, P], F32, s0) for d, lv in JOBS if lv < 64}
        cin = sb("cin", [P, 4, SEQ + 4], F32, s0)
        vgz = sb("vgz", [P, 3, NT, H], F32, s0)
        wdt = sb("wdt", [P, KT, 16], F32, s0)
        wdt_hi = sb("wdt_hi", [P, KT, 16], F32R, s0)
        wdt_lo = sb("wdt_lo", [P, KT, 16], F32R, s0)
        lbt = sb("lbt", [P, 10, 4], F32, s0)
        smallb = sb("smallb", [P, 16 + 16 + 8 + 128], F32, s0)
        dtbb, alogb, db = smallb[:, 0:16], smallb[:, 16:32], smallb[:, 32:40]
        anb = smallb[:, 40:168]
        bnb = AT2[:, :, :].rearrange("p h t -> p (h t)")
        dts = sb("dts", [P, 8, NT, 16], F32, s0)
        dta = sb("dta", [P, NT, 16], F32, s0)
        nexpa = sb("nexpa", [P, 16], F32, s0)
        acs = sb("acs", [P, NT, 16], F32, s0)
        Ccol = sb("Ccol", [P, NT, 16], F32, s0)
        Cx = sb("Cx", [P, 16], F32, s0)
        nrm = sb("nrm", [P, 12], F32, s0)
        cs_hi_t = sb("cs_hi", [16, SEQ], F32R, s0)
        cs_lo_t = sb("cs_lo", [16, SEQ], F32R, s0)
        cs_hi, cs_lo = cs_hi_t[:, :], cs_lo_t[:, :]
        epsc = sb("epsc", [P, 1], F32, s0)
        flat = lambda v: v.rearrange("p h t -> p (h t)")
        Gm = [flat(EB[0]), flat(EB[1])]
        Lb = [gb[1][:, :], flat(EB[3])]
        Wb = [flat(kT[0][:, :, :]), flat(kT[1][:, :, :])]
        xsn = flat(PS[0][:, :, :]).rearrange("p (t c) -> p t c", t=NT)
        tmpn = flat(PS[1][:, :, :]).rearrange("p (t c) -> p t c", t=NT)
        squ = flat(qT[:, :, :]).rearrange("p (t c) -> p t c", t=NT)
        s0.close()

        s1 = ExitStack()
        ffs = sb("ffs", [P, 2, SEQ], F32, s1)
        ffh = [sb(f"ffh{i}", [P, 2, SEQ], F32R, s1) for i in range(2)]
        ffl = [sb(f"ffl{i}", [P, 2, SEQ], F32R, s1) for i in range(2)]
        sb("space1", [P, 640], F32, s1)
        bias = sb("bias", [P, C_HEADS, NT, SEQ], F32, s1)
        s1w = ExitStack()
        win = sb("win", [P, NT, C_HEADS, WIN], F32, s1w)
        tab = sb("tab", [C_HEADS, RPB_H], F32, s1w)
        tab_r = sb("tab_r", [C_HEADS, RPB_H], F32, s1w)
        s1w.close()
        pin = [sb("pin0", [P, NT, P_DIM], F32, s1w)]
        pT_hi = [sb("pT_hi0", [P, 2, SEQ], F32R, s1w)]
        pT_lo = [sb("pT_lo0", [P, 2, SEQ], F32R, s1w)]
        gate = [sb("gate0", [P, NT, D], F32, s1w)]
        s1w.close()
        qcT = sb("qcT", [P, KT, SEQ], F32, s1w)
        kcT = sb("kcT", [P, KT, SEQ], F32, s1w)
        vc = sb("vc", [P, NT, D], F32, s1w)
        s1w.close()
        s1.close()
        s3 = ExitStack()
        sc = [sb(f"sc{i}", [P, NT, SEQ], F32, s3) for i in range(2)]
        pr = [sb(f"pr{i}", [P, NT, SEQ], F32, s3) for i in range(2)]
        prT = [sb(f"prT{i}", [P, NT, SEQ], F32, s3) for i in range(2)]
        nmax = sb("nmax", [P, C_HEADS, NT], F32, s3)
        den = sb("den", [P, NT, C_HEADS], F32, s3)
        rden = sb("rden", [P, NT, C_HEADS], F32, s3)
        s3.close()

        s4 = ExitStack()
        pin.append(sb("pin1", [P, NT, P_DIM], F32, s4))
        pT_hi.append(sb("pT_hi1", [P, 2, SEQ], F32R, s4))
        pT_lo.append(sb("pT_lo1", [P, 2, SEQ], F32R, s4))
        hF = sb("hF", [P, KT, SEQ], F32, s4)
        gate.append(hF[:, :, :].rearrange("p k t -> p (k t)").rearrange("p (t d) -> p t d", t=NT))
        wr = sb("wr", [P, KT, N_EXPERTS], F32, s4)
        xg_hi = sb("xg_hi", [P, NT, D], F32R, s4)
        xg_lo = sb("xg_lo", [P, NT, D], F32R, s4)
        he_hi = sb("he_hi", [P, KT, P], F32R, s4)
        he_lo = sb("he_lo", [P, KT, P], F32R, s4)
        acc = sb("acc", [P, NT, D], F32, s4)
        es = sb("es", [P, H], F32, s4)
        ea = sb("ea", [P, H], F32, s4)
        eT_hi = sb("eT_hi", [P, 4, P], F32R, s4)
        eT_lo = sb("eT_lo", [P, 4, P], F32R, s4)
        y_hi = sb("y_hi", [P, D], F32R, s4)
        y_lo = sb("y_lo", [P, D], F32R, s4)
        sel = sb("sel", [P, NT, P], F32R, s4)
        selT = sb("selT", [P, SEQ], F32R, s4)
        gcol = sb("gcol", [P, NT, 1], F32, s4)
        gslot = sb("gslot", [P, 1], F32, s4)
        iota_f = sb("iota_f", [P, P], F32, s4)
        lg = sb("lg", [P, NT, 8], F32, s4)
        mx8 = sb("mx8", [P, NT, 8], F32, s4)
        ix8 = sb("ix8", [P, NT, 8], U32, s4)
        ixf = sb("ixf", [P, NT, 8], F32, s4)
        oh = sb("oh", [P, NT, 2, 8], F32, s4)
        msk = sb("msk", [P, NT, 8], F32, s4)
        gat = sb("gat", [P, NT, 12], F32, s4)
        posx = sb("posx", [P, NT, 12], F32, s4)
        r1 = sb("r1", [P, 8, NT, 8], F32, s4)
        r3 = sb("r3", [P, 2, NT, 3, 8], F32, s4)
        flag = sb("flag", [P, 8], F32, s4)
        fpos = sb("fpos", [P, 9], F32, s4)
        ohx = sb("ohx", [P, 3, 8], F32, s4)
        itf = sb("itf", [P, 16], F32, s4)
        items = sb("items", [1, 16], I32, s4)
        s4.close()

        B = [ctx.enter_context(nc.psum_tensor(f"bank{i}", [P, H], F32)) for i in range(8)]

        Y_BANKS = [[B[6], B[7]], [B[4], B[5]]]
        TURN_BANKS = {1: [B[0], B[1], B[6], B[7]]}

        def turn_bank(m, j):
            return TURN_BANKS.get(m, [B[6], B[7], B[6], B[7]])[j]

        P_BANK = [B[2], B[4]]
        PROJ_BANKS = [[B[0], B[1], B[2], B[3]], [B[0], B[1], B[2], B[4]]]
        GATE_BANKS = [[B[4], B[5], B[6], B[7]], [B[3], B[5], B[6], B[7]]]

        def sem(name):
            return ctx.enter_context(nc.semaphore(name))

        S = {}
        for n in (
                "act_step bnb_in cols_copied cols_done comb_added comb_done consts conv_done conv_silu "
                "cs_hi_done diag_ready dt_done dt_mm dt_ready dve_step dxs_done e_done ehi "
                "elo emul eps_added esilu eturned ff_hi ff_lo ff_mul ff_quarter "
                "ff_silu first_gated g_done gates_done gath_done geh gel gm_done hF_copied "
                "hF_turned hT_hi_done hT_lo_done hi_ready ident_ready inverse_a items_ready job_evac job_exp "
                "job_mul job_pe job_sub l_exp lg_done lo_ready logs_done mask_done mix_a "
                "mix_b moe_acc moe_consts moe_init nm_done o_copied o_done oc_done oc_norm "
                "out_done pT_hi_done pT_lo_done p_in p_turned ply_done pool_step pos_done pt_copied "
                "pt_done qkv_evac rbc_done rbc_used root_a root_b root_done rows_copied rows_turned "
                "s_done scans_done second_gated selT_copied selT_done sel_built sig_done small_in sq_done "
                "tab_in tab_out top_done top_exp turned unit_used vcol_ready vcol_t vrow_in "
                "w_done wdt_hi_done wdt_in wdt_lo_done win_evac win_in win_masked wr_in x_in "
                "x_ready xg_ready xgh_done xgl_done xs_copied xs_turned y_copied y_pe yhi "
                "ylo "
        ).split():
            S[n] = sem(n)
        raw_in = [sem(f"raw_in{i}") for i in range(RAW)]
        gb_in = [sem(f"gb_in{i}") for i in range(2)]

        block = ctx.enter_context(nc.Block())

        def unit_count(u, turns):
            return u if turns is None else turns * RAW + u

        def used(eng, u, turns=None):
            eng.wait_ge(S["unit_used"], unit_count(u + 1, turns))

        def views(t, k):
            return t[:, :].rearrange("p (k n) -> p k n", k=k)

        def rows(w, k0, k, c0, c):
            return w[k0 * P:(k0 + k) * P, c0:c0 + c].rearrange("(k p) n -> p k n", p=P)

        e_w_in, e_w_out, o_w_qkv, o_w_out = a["e_w_in"][0], a["e_w_out"][0], a["o_w_qkv"][0], a["o_w_out"][0]
        w_g, w_u, w_d = a["e_w_ffn_gate"][0], a["e_w_ffn_up"][0], a["e_w_ffn_down"][0]
        x_in_d, out_d = a["x"][0], out[0]
        rev = nc.dram_tensor("rpb_reversed", (C_HEADS, RPB_H), F32, kind="Internal").ap()

        @block.sync
        def _(sp):
            def load(u, src, k, turns=None):
                if u >= RAW:
                    sp.wait_ge(S["lo_ready"], unit_count(u - RAW + 1, turns))
                sp.dma_start(views(raw[u % RAW], k), src).then_inc(raw_in[u % RAW], 16)

            for t in range(NT):
                sp.dma_start(x[:, t, :], x_in_d[t * P:(t + 1) * P, :]).then_inc(S["x_in"], 16)
            n = 0
            for name in ("e_norm_mix_pre", "e_norm_ffn_pre"):
                sp.dma_start(vrow[n:n + 8, :], a[name][0].rearrange("(k p) -> k p", p=P)).then_inc(S["vrow_in"], 16)
                n += 8
            sp.dma_start(vrow[n:n + 8, :], a["ple_norm_in"][0].rearrange("(k p) -> k p", p=P)).then_inc(S["vrow_in"], 16)
            n += 8
            sp.dma_start(vrow[n:n + 8, :], a["o_norm_mix_pre"][0].rearrange("(k p) -> k p", p=P)).then_inc(S["vrow_in"], 16)
            n += 8
            sp.dma_start(vrow[n:n + 8, :], a["ple_norm_in"][1].rearrange("(k p) -> k p", p=P)).then_inc(S["vrow_in"], 16)
            n += 8
            sp.dma_start(vrow[n:n + 12, :], a["hgrn_lb_raw"].rearrange("l (h p) -> (l h) p", p=P)).then_inc(S["vrow_in"], 16)
            n += 12
            sp.dma_start(vrow[n:n + 40, :], a["e_conv_w"][0].rearrange("j (c p) -> (j c) p", p=P)).then_inc(S["vrow_in"], 16)
            n += 40
            sp.dma_start(vrow[n:n + 8, :], a["e_conv_b"][0].rearrange("(c p) -> c p", p=P)).then_inc(S["vrow_in"], 16)
            for c, (_, col) in enumerate(WIN_GROUPS):
                for hf in range(2):
                    load(U_WIN + 2 * c + hf, rows(e_w_in, 4 * hf, 4, col, H), 4)
            def square(w, u0, cols):
                for c in range(cols):
                    for hf in range(2):
                        load(u0 + 2 * c + hf, rows(w, 4 * hf, 4, c * H, H), 4)
            for hf in range(2):
                for c in range(2):
                    load(U_WOUT0 + 2 * hf + c, rows(e_w_out, 4 * hf, 4, c * H, H), 4)
            for m, w in enumerate((w_g, w_u)):
                load(U_FFN + m, rows(w, 0, KT, 0, FF_STEP), KT)
            with sp.Fori(0, (FF_STEPS - 1) // 2) as it:
                for b in range(2):
                    for m, w in enumerate((w_g, w_u)):
                        src = w[:, bass.ds(it * (2 * FF_STEP) + (b + 1) * FF_STEP, FF_STEP)].rearrange("(k p) n -> p k n", p=P)
                        load(U_FFN + 2 + 3 * b + m, src, KT, it)
                    src = w_d[bass.ds(it * (2 * FF_STEP) + b * FF_STEP, FF_STEP), :].rearrange("(k p) n -> p k n", p=P)
                    load(U_FFN + 2 + 3 * b + 2, src, 2, it)
            load(U_PLE0 - 1, rows(w_d, 2 * (FF_STEPS - 1), 2, 0, D), 2)
            def ple(u0, li, turns=None):
                load(u0, rows(a["ple_w_proj"][li], 0, 2, 0, D), 2, turns)
                for c in range(2):
                    for hf in range(2):
                        load(u0 + 1 + 2 * c + hf, rows(a["ple_w_gate"][li], 4 * hf, 4, c * H, H), 4, turns)
            ple(U_PLE0, 0)
            square(o_w_qkv, U_QKV, 6)
            square(o_w_out, U_WOUT1, 2)

            def gu(e, f, u, turns):
                for m, name in enumerate(("o_w_exp_gate", "o_w_exp_up")):
                    w = a[name][0]
                    for hf in range(2):
                        src = w[bass.ds(e, 1), hf * H:(hf + 1) * H, bass.ds(f * H, H)] \
                            .rearrange("e (k p) n -> p (e k) n", p=P)
                        load(u + 2 * m + hf, src, 4, turns)

            def dn(e, f, u, turns):
                w = a["o_w_exp_down"][0]
                for hf in range(2):
                    src = w[bass.ds(e, 1), bass.ds(f * H + hf * 256, 256), :] \
                        .rearrange("e (k p) n -> p (e k) n", p=P)
                    load(u + hf, src, 2, turns)

            def item(e, turns):
                gu(e, 0, U_MOE, turns)
                with sp.Fori(1, FE_STEPS) as f:
                    gu(e, f, U_MOE + 4 - RAW, turns + f)
                    dn(e, f - 1, U_MOE + 8 - RAW, turns + f)
                dn(e, FE_STEPS - 1, U_MOE + 4, turns + (FE_STEPS - 1))

            with sp.Fori(0, 1) as zero:
                item(zero, zero * FE_STEPS)
            sp.wait_ge(S["items_ready"], 1)
            n_items = sp.value_load(items[0:1, 12:13], min_val=N_EXPERTS, max_val=MAX_ITEMS)
            with sp.Fori(1, n_items) as i:
                e = sp.value_load(items[0:1, bass.ds(i, 1)], min_val=0, max_val=N_EXPERTS - 1)
                item(e, i * FE_STEPS)
            ple(U_MOE, 1, n_items * FE_STEPS)
            for k, (t, hf) in enumerate(QUARTERS):
                sp.wait_ge(S["x_ready"], 5 * 4 + k + 1)
                cols = slice(hf * H, (hf + 1) * H)
                sp.dma_start(out_d[t * P:(t + 1) * P, cols], x[:, t, cols]).then_inc(S["out_done"], 16)
            sp.wait_ge(S["out_done"], 16 * 4)

        @block.gpsimd
        def _(pool):
            steps = [0]

            def link(ins):
                steps[0] += 1
                ins.then_inc(S["pool_step"], 1)
                pool.wait_ge(S["pool_step"], steps[0])

            def keep(t, pattern, base, cm):
                link(pool.affine_select(out=t, in_=t, compare_op=ALU.is_ge, fill=0.0, base=base,
                                        pattern=pattern, channel_multiplier=cm))

            def bcast(dst, src, n, s):
                pool.dma_start(dst, src.partition_broadcast(P)).then_inc(S[s], 16)

            pool.memset(ones[:, :], 1.0).then_inc(S["consts"], 1)
            link(pool.memset(ident[:, :], 0.0))
            pool.affine_select(out=ident[:, :], in_=ident[:, :], compare_op=ALU.not_equal, fill=1.0, base=0,
                               pattern=[[-1, P]], channel_multiplier=1).then_inc(S["ident_ready"], 1)
            gains = [a["e_norm_mix_post"][0], a["e_norm_ffn_post"][0], a["ple_norm_post"][0], a["o_norm_mix_post"][0],
                     a["o_norm_ffn_pre"][0], a["o_norm_ffn_post"][0], a["ple_norm_post"][1]]

            def load_gain(n):
                if n in (2, 3, 4, 5):
                    pool.wait_ge(S["x_ready"], 4 * (n - 1))
                elif n == 6:
                    pool.wait_ge(S["xg_ready"], 4)
                pool.dma_start(gb[n % 2][:, :], gains[n].partition_broadcast(P)).then_inc(gb_in[n % 2], 16)

            bcast(dtbb, a["e_dt_bias"][0].rearrange("a h -> (a h)"), 16, "small_in")
            bcast(alogb, a["e_A_log"][0].rearrange("a h -> (a h)"), 16, "small_in")
            bcast(db, a["e_D"][0], 8, "small_in")
            bcast(anb, a["e_a_norm"][0], 128, "small_in")
            pool.dma_start(wdt[:, :, :], rows(e_w_in, 0, KT, DT_COL, 16)).then_inc(S["wdt_in"], 16)
            load_gain(0)
            for t, pat, cm, base in ((le, 1, -1, 0), (ge, -1, 1, 0), (lt, 1, -1, -1)):
                link(pool.memset(t[:, :], 1.0))
                keep(t[:, :], [[pat, P]], base, cm)
            for d, lv in JOBS:
                if lv >= 64:
                    continue
                m = hmask[(d, lv)]
                if lv == 0:
                    link(pool.memset(m[:, :], 1.0))
                    v = m[:, :].rearrange("p (b x) -> p b x", x=16)
                    nb = P // 16
                    if d == 0:
                        keep(v, [[-16, nb], [0, 16]], 0, 1)
                        keep(v, [[16, nb], [1, 16]], 0, -1)
                    else:
                        keep(v, [[16, nb], [0, 16]], 15, -1)
                        keep(v, [[-16, nb], [-1, 16]], 0, 1)
                else:
                    nb = P // (2 * lv)
                    link(pool.memset(m[:, :], 0.0))
                    v = m[:, :].rearrange("p (b x) -> p b x", x=2 * lv)
                    w = v[:, :, lv:] if d == 0 else v[:, :, :lv]
                    link(pool.memset(w, 1.0))
                    off = 0 if d == 0 else lv
                    keep(w, [[-2 * lv, nb], [0, lv]], -off, 1)
                    keep(w, [[2 * lv, nb], [0, lv]], off + lv - 1, -1)
            pool.memset(epsc[:, :], EPS)
            pool.memset(cin[:, :, 0:2], 0.0)
            link(pool.memset(cin[:, :, SEQ + 2:], 0.0))
            pool.memset(AT2[:, :, :], 0.0).then_inc(S["consts"], 1)
            pool.wait_ge(S["vcol_t"], 1)
            pool.memset(AT, 0.0).then_inc(S["consts"], 1)

            pool.wait_ge(S["scans_done"], 1)
            for j, (d, lv) in enumerate(JOBS):
                if j == 2:
                    pool.wait_ge(S["scans_done"], 2)
                Y = PS[d]
                last = max(JBUF[j])
                if last >= 4:
                    pool.wait_ge(S["job_pe"], JOB_OF_BUF[last - 4] + 1)
                E = EB[JBUF[j][0] % 4]
                if lv == 0:
                    y = Y[:, :, :].rearrange("p h (b x) -> p (h b) x", x=16)
                    e = E.rearrange("p h (b x) -> p (h b) x", x=16)
                    pool.tensor_tensor(e, y, y[:, :, 7:8].to_broadcast([P, A_HEADS * SEQ // 16, 16]),
                                       ALU.subtract).then_inc(S["job_sub"], 1)
                elif lv < 128:
                    nb = A_HEADS * SEQ // (2 * lv)
                    y = Y[:, :, :].rearrange("p h (b x) -> p (h b) x", x=2 * lv)
                    e = E.rearrange("p h (b x) -> p (h b) x", x=2 * lv)
                    at = lv - 1 if d == 0 else lv
                    ref = y[:, :, at:at + 1].to_broadcast([P, nb, lv])
                    pool.tensor_tensor(e[:, :, :lv], ref, y[:, :, :lv], ALU.subtract)
                    pool.tensor_tensor(e[:, :, lv:], y[:, :, lv:], ref, ALU.subtract).then_inc(S["job_sub"], 1)
                else:
                    ref = (PS[0][:, :, P - 1:P] if d == 0 else btot[:, :, :]).to_broadcast([P, A_HEADS, P])
                    pool.tensor_tensor(E[:, :, 0:P], ref, Y[:, :, 0:P], ALU.subtract).then_inc(S["job_sub"], 1)

            pool.wait_ge(S["job_evac"], JBANK[5][-1] + 1)
            bcast(bnb, a["e_b_norm"][0], 512, "bnb_in")

            pool.wait_ge(S["win_evac"], 7)
            pool.wait_ge(S["small_in"], 16 * 4)
            for t in range(NT):
                v = vgz[:, 1, t, :].rearrange("p (h c) -> p h c", c=P)
                ins = pool.tensor_tensor(v, v, anb.rearrange("p (o c) -> p o c", o=1).to_broadcast([P, A_HEADS, P]), ALU.mult)
            link(ins)
            for t in range(NT):
                pool.wait_ge(S["o_copied"], t + 1)
                pool.tensor_tensor(xn[:, t, 0:H], xn[:, t, 0:H], vgz[:, 1, t, :], ALU.mult).then_inc(S["mix_a"], 1)
            pool.wait_ge(S["xs_copied"], 1)
            for t in range(NT):
                pool.tensor_tensor(tmpn[:, t, :].rearrange("p (h c) -> p h c", c=B_HD),
                                   xsn[:, t, :].rearrange("p (h c) -> p h c", c=B_HD),
                                   db.rearrange("p (h o) -> p h o", o=1).to_broadcast([P, B_HEADS, B_HD]),
                                   ALU.mult).then_inc(S["dxs_done"], 1)
            pool.wait_ge(S["dxs_done"], 2)
            ob = [xn[:, t, H:H + 256] for t in range(NT)]
            for t in range(NT):
                pool.wait_ge(S["y_copied"], t + 1)
                link(pool.tensor_tensor(ob[t], ob[t], tmpn[:, t, 0:256], ALU.add))
                pool.tensor_tensor(ob[t], ob[t], vgz[:, 2, t, 0:256], ALU.mult).then_inc(S["first_gated"], 1)
            pool.wait_ge(S["x_ready"], 4)
            pool.dma_start(tab[:, :], a["o_rpb"][0].rearrange("h r c -> h (r c)")).then_inc(S["tab_in"], 16)
            pool.wait_ge(S["tab_in"], 16)
            whole = tab[:, :]
            backwards = bass.AP(tensor=whole.tensor, offset=whole.offset + RPB_H - 1,
                                ap=[list(whole.ap[0]), [-1, RPB_H]])
            link(pool.tensor_copy(tab_r[:, :], backwards))
            pool.dma_start(rev, tab_r[:, :]).then_inc(S["tab_out"], 16)
            pool.wait_ge(S["tab_out"], 16)
            for r in range(SEQ // GRID_W):
                src = bass.AP(tensor=rev.tensor,
                              offset=RPB_H - 1 - (NA_ROWS - 1 - r) * RPB_W - (NA_COLS - 1) - (WIN - 1),
                              ap=[[1, GRID_W], [RPB_H, C_HEADS], [1, WIN]])
                pool.dma_start(win[(r % 2) * GRID_W:(r % 2 + 1) * GRID_W, r // 2, :, :], src).then_inc(S["win_in"], 16)
            def load_p(li):
                pool.dma_start(pin[li][:, :, :], a["p"][li, 0].rearrange("(t p) n -> p t n", p=P)).then_inc(S["p_in"], 16)
            load_gain(1)
            load_gain(2)
            pool.wait_ge(S["win_in"], 16 * 4)
            for t in range(NT):
                for h in range(C_HEADS):
                    base_ap = win[:, t, h, :]
                    src = bass.AP(tensor=base_ap.tensor, offset=base_ap.offset + WIN - 1,
                                  ap=[list(base_ap.ap[0]), [-RPB_W, 4], [-1, GRID_W]])
                    ins = pool.tensor_copy(bias[:, h, t, :].rearrange("p (r c) -> p r c", c=GRID_W), src)
            link(ins)
            for r in range(2):
                v = bias[r * GRID_W:(r + 1) * GRID_W, :, :, :].rearrange("p h t (r c) -> p (h t r) c", c=GRID_W)
                link(pool.affine_select(out=v[:, :, NA_COLS:], in_=v[:, :, NA_COLS:], compare_op=ALU.is_ge, fill=NEG,
                                        base=NA_COLS // 2 - 1 - NA_COLS,
                                        pattern=[[0, C_HEADS * NT * 4], [-1, GRID_W - NA_COLS]], channel_multiplier=1))
                ins = pool.affine_select(out=v[:, :, :GRID_W - NA_COLS], in_=v[:, :, :GRID_W - NA_COLS],
                                         compare_op=ALU.is_ge, fill=NEG, base=NA_COLS // 2,
                                         pattern=[[0, C_HEADS * NT * 4], [1, GRID_W - NA_COLS]], channel_multiplier=-1)
                ins.then_inc(S["win_masked"], 1)
            pool.wait_ge(S["win_masked"], 2)
            load_p(0)
            load_gain(3)
            load_gain(4)
            load_gain(5)
            load_p(1)
            pool.dma_start(wr[:, :, :], a["o_w_router"][0].rearrange("(k p) e -> p k e", p=P)).then_inc(S["wr_in"], 16)
            pool.iota(iota_f[:, :], pattern=[[1, P]], base=0, channel_multiplier=0,
                      allow_small_or_imprecise_dtypes=True).then_inc(S["moe_consts"], 1)
            pool.iota(itf[:, :], pattern=[[1, 16]], base=0, channel_multiplier=0,
                      allow_small_or_imprecise_dtypes=True).then_inc(S["moe_consts"], 1)
            pool.memset(acc[:, :, :], 0.0).then_inc(S["moe_consts"], 1)
            pool.memset(y_hi[:, :].bitcast(F32), 0.0).then_inc(S["moe_init"], 1)
            pool.memset(y_lo[:, :].bitcast(F32), 0.0).then_inc(S["moe_init"], 1)
            pool.memset(selT[:, :].bitcast(F32), 0.0).then_inc(S["moe_init"], 1)
            load_gain(6)
            pool.wait_ge(S["xgh_done"], 1)
            pool.tensor_tensor(xg_lo[:, :, :], xn[:, :, :], xg_hi[:, :, :].bitcast(F32), ALU.subtract).then_inc(S["xgl_done"], 1)

        @block.scalar
        def _(act):
            steps = [0]
            A = act.activation

            def link(ins):
                steps[0] += 1
                ins.then_inc(S["act_step"], 1)
                act.wait_ge(S["act_step"], steps[0])

            def round_hi(u, turns=None):
                act.wait_ge(raw_in[u % RAW], 16 * (u // RAW + 1) if turns is None else turns * 16 + 16 * (u // RAW + 1))
                if u >= SPLIT:
                    act.wait_ge(S["unit_used"], unit_count(u - SPLIT + 1, turns))
                A(hi[u % SPLIT][:, :], raw[u % RAW][:, :], ACT.Copy).then_inc(S["hi_ready"], 1)

            def roots(r, src, ready, junk=lambda t, hf: xn[:, t, hf * H:(hf + 1) * H], between=None):
                A(root[:, NT:], ones[:, 0:1], ACT.Sqrt)
                for k, (t, hf) in enumerate(QUARTERS):
                    ready(k)
                    A(junk(t, hf), src(t, hf), ACT.Square, scale=D ** -0.5,
                      accum_out=sums[:, k:k + 1]).then_inc(S["sq_done"], 1)
                act.wait_ge(S["sq_done"], 4 * r + 4)
                act.wait_ge(S["eps_added"], r + 1)
                for t in range(NT):
                    ins = A(root[:, t:t + 1], sums[:, 2 + t:3 + t], ACT.Sqrt, bias=sums_e[:, t:t + 1])
                ins.then_inc(S["root_done"], 1)

            def norm(n):
                roots(2 * n, lambda t, hf: x[:, t, hf * H:(hf + 1) * H],
                      lambda k: act.wait_ge(S["x_ready"], 4 * (n - 1) + k + 1))

            def post(n, src, ready):
                roots(2 * n + 1, src, ready)

            def turned(m, gain=None, js=range(4)):
                for j in js:
                    act.wait_ge(S["turned"], 4 * m + j + 1)
                    for b in range(2):
                        kt = 2 * j + b
                        sc_ = 1.0 if gain is None else vcol[:, gain + kt:gain + kt + 1]
                        ins = A(hT_hi[:, kt, :], turn_bank(m, j)[:, b * SEQ:(b + 1) * SEQ], ACT.Copy, scale=sc_)
                    ins.then_inc(S["hT_hi_done"], 1)

            act.wait_ge(S["consts"], 1)
            roots(0, lambda t, hf: x[:, t, hf * H:(hf + 1) * H], lambda k: act.wait_ge(S["x_in"], 16 * NT),
                  lambda t, hf: vgz[:, hf, t, :])
            round_hi(0)
            act.wait_ge(S["vcol_ready"], 1)
            turned(0, V_GAIN["mix0"])
            act.wait_ge(S["ident_ready"], 1)
            A(ident_r[:, :], ident[:, 0:16], ACT.Copy)
            act.wait_ge(S["wdt_in"], 16)
            A(wdt_hi[:, :, :], wdt[:, :, :], ACT.Copy).then_inc(S["wdt_hi_done"], 1)

            def evac_group(c):
                name = WIN_GROUPS[c][0]
                used(act, U_WIN + 2 * c + 1)
                for b in range(2):
                    bank = B[2 * (c % 2) + b]
                    if name in ("ff", "fb"):
                        g = G[0] if name == "ff" else G[1]
                        ins = A(g[:, 2 * b:2 * b + 2, :], bank[:, :].rearrange("p (h t) -> p h t", h=2), ACT.Sigmoid)
                    elif name == "q":
                        ins = A(qT[:, 2 * b:2 * b + 2, :], bank[:, :].rearrange("p (h t) -> p h t", h=2), ACT.Silu)
                    elif name in ("xs", "bc"):
                        if name == "bc":
                            act.wait_ge(S["conv_done"], 4)
                        ins = A(cin[:, 2 * b:2 * b + 2, 2:2 + SEQ], bank[:, :].rearrange("p (h t) -> p h t", h=2), ACT.Copy)
                    else:
                        k = ("v", "g", "z").index(name)
                        ins = A(vgz[:, k, b, :], bank[:, :], ACT.Silu if k else ACT.Copy)
                ins.then_inc(S["win_evac"], 1)

            def job_exp(j):
                d, lv = JOBS[j]
                act.wait_ge(S["job_sub"], j + 1)
                E = EB[JBUF[j][0] % 4]
                if lv == 0:
                    link(A(EB[JBUF[j][1] % 4], E, ACT.Exp, scale=-1.0))
                    A(E, E, ACT.Exp).then_inc(S["job_exp"], 1)
                elif lv < 128:
                    A(E, E, ACT.Exp).then_inc(S["job_exp"], 1)
                else:
                    A(E[:, :, P:], PS[d][:, :, P:], ACT.Exp)
                    A(E[:, :, 0:P], E[:, :, 0:P], ACT.Exp).then_inc(S["job_exp"], 1)

            def softplus_exps():
                act.wait_ge(S["dt_ready"], 1)
                A(dts[:, 2, :, :], dts[:, 1, :, :], ACT.Exp, scale=-1.0).then_inc(S["dt_done"], 1)
                act.wait_ge(S["small_in"], 16 * 4)
                A(nexpa[:, :], alogb, ACT.Exp).then_inc(S["dt_done"], 1)

            def softplus_log():
                act.wait_ge(S["dt_ready"], 2)
                A(dts[:, 4, :, :], dts[:, 3, :, :], ACT.Ln).then_inc(S["dt_done"], 1)

            nxt = [1]

            def ahead(end, turns=None):
                while nxt[0] < end:
                    round_hi(nxt[0], turns)
                    nxt[0] += 1

            for c in range(9):
                ahead(min(U_WIN + 2 * c + SPLIT, U_WOUT0))
                if c:
                    evac_group(c - 1)
                if c == 1:
                    act.wait_ge(S["gates_done"], 1)
                    A(lbt[:, 3:6, :], lbt[:, 0:3, :], ACT.Exp).then_inc(S["logs_done"], 1)
                if c == 3:
                    for d in (0, 1):
                        act.wait_ge(S["gates_done"], 2 + d)
                        A(G[d][:, :, :], G[d][:, :, :], ACT.Ln).then_inc(S["logs_done"], 1)
                if JOB_ROUND0 <= c < 8:
                    for j in (2 * (c - JOB_ROUND0), 2 * (c - JOB_ROUND0) + 1):
                        job_exp(j)
                if c == 4:
                    softplus_exps()
                if c == 6:
                    softplus_log()
            act.wait_ge(S["rows_turned"], 1)
            A(cs_hi, B[1][0:16, 0:SEQ], ACT.Copy).then_inc(S["cs_hi_done"], 1)
            for b in range(2):
                act.wait_ge(S["conv_done"], 4 * b + 4)
                A(cout[:, 4 * b:4 * b + 4, :], cout[:, 4 * b:4 * b + 4, :], ACT.Silu).then_inc(S["conv_silu"], 1)
            A(root[:, NT:], ones[:, 0:1], ACT.Sqrt)
            act.wait_ge(S["o_done"], 1)
            for t in range(NT):
                for h in range(A_HEADS):
                    c = slice(h * P, (h + 1) * P)
                    ins = A(squ[:, t, c], B[t][:, c], ACT.Square, accum_out=nrm[:, 4 * t + h:4 * t + h + 1])
            link(ins)
            A(nrm[:, 0:8], nrm[:, 0:8], ACT.Sqrt, scale=1.0 / P, bias=epsc[:, :]).then_inc(S["root_a"], 1)
            A(root[:, NT:], ones[:, 0:1], ACT.Exp)
            act.wait_ge(S["inverse_a"], 1)
            for t in range(NT):
                for h in range(A_HEADS):
                    c = slice(h * P, (h + 1) * P)
                    ins = A(xn[:, t, c], B[t][:, c], ACT.Copy, scale=nrm[:, 4 * t + h:4 * t + h + 1])
                ins.then_inc(S["o_copied"], 1)

            def group_squares(g):
                for t in range(NT):
                    act.wait_ge(S["second_gated" if g else "first_gated"], t + 1)
                    k = 8 + 2 * t + g
                    ins = A(squ[:, t, g * 256:(g + 1) * 256], xn[:, t, H + g * 256:H + (g + 1) * 256], ACT.Square,
                            accum_out=nrm[:, k:k + 1])
                return ins

            for h in range(B_HEADS):
                act.wait_ge(S["rbc_used"], h + 1)
                A(Lb[h % 2][:, 0:768], Lb[h % 2][:, 0:768], ACT.Exp).then_inc(S["l_exp"], 1)
                if 1 <= h <= 3:
                    ahead(U_WOUT0 + h)
                if h == 4:
                    turned(1, None, (0, 1))
                if h == 5:
                    act.wait_ge(S["y_pe"], 4)
                    for t in range(NT):
                        A(xn[:, t, H:H + 256], Y_BANKS[0][t][:, 0:256], ACT.Copy).then_inc(S["y_copied"], 1)
                if h == 7:
                    group_squares(0)
            A(root[:, NT:], ones[:, 0:1], ACT.Sqrt)
            link(group_squares(1))
            A(nrm[:, 8:12], nrm[:, 8:12], ACT.Sqrt, scale=2.0 / H, bias=epsc[:, :]).then_inc(S["root_b"], 1)
            ahead(U_WOUT0 + 4)
            turned(1, None, (2, 3))
            ahead(U_FFN + SPLIT)

            def bank_src(t, hf):
                return B[2 * hf + t][:, :]
            post(0, bank_src, lambda k: used(act, U_WOUT0 + (2 if k < 2 else 3)))
            norm(1)
            turned(2, V_GAIN["ffn0"])

            def ff_evac(c, b, loop=None):
                k = lambda v: v if loop is None else loop * 2 + v
                used(act, U_FFN + 1 if c == 0 else U_FFN + 3 * c, loop)
                for j in range(2):
                    ins = A(ffs[:, j, :], B[2 * b + j][:, 0:SEQ], ACT.Silu)
                ins.then_inc(S["ff_silu"], 1)
                act.wait_ge(S["ff_mul"], k(c + 1))
                A(ffh[b][:, :, :], ffs[:, :, :], ACT.Copy).then_inc(S["ff_hi"], 1)

            ff_evac(0, 0)
            with act.Fori(0, (FF_STEPS - 1) // 2) as it:
                for b in range(2):
                    for m in range(3):
                        round_hi(U_FFN + 3 + 3 * b + m, it)
                    ff_evac(1 + b, (1 + b) % 2, it)

            def p_turned_hi(n):
                act.wait_ge(S["p_turned"], n + 1)
                A(pT_hi[n][:, :, :], P_BANK[n][:, :].rearrange("p (k t) -> p k t", k=2), ACT.Copy).then_inc(S["pT_hi_done"], 1)

            nxt[0] = U_PLE0
            p_turned_hi(0)
            ahead(U_PLE0 + SPLIT)

            def bank_y(t, hf):
                return B[4 + 2 * t + hf][:, :]
            post(1, bank_y, lambda k: act.wait_ge(S["ff_quarter"], k + 1) if k < 3 else used(act, U_PLE0 - 1))
            norm(2)
            turned(3, V_GAIN["ple0"])

            def ple(n, u0, turns=None):
                ahead(u0 + 5, turns)
                for k, (t, hf) in enumerate(QUARTERS):
                    used(act, u0 + 2 + 2 * hf, turns)
                    A(gate[n][:, t, hf * H:(hf + 1) * H], GATE_BANKS[n][k][:, :], ACT.Sigmoid).then_inc(S["sig_done"], 1)
                    if k == 1 and n == 0:
                        ahead(U_QKV + 1)
                post(2 if n == 0 else 5, lambda t, hf: gate[n][:, t, hf * H:(hf + 1) * H],
                     lambda k: act.wait_ge(S["ply_done"], 4 * n + k + 1))

            ple(0, U_PLE0)
            norm(3)
            ahead(U_QKV + SPLIT)
            turned(4, V_GAIN["mix1"])

            def qkv_evac(c):
                used(act, U_QKV + 2 * c + 1)
                for b in range(2):
                    bank = B[2 * (c % 2) + b]
                    if c < 4:
                        dst = qcT if c < 2 else kcT
                        k0 = 4 * (c % 2) + 2 * b
                        ins = A(dst[:, k0:k0 + 2, :], bank[:, :].rearrange("p (k t) -> p k t", k=2), ACT.Copy)
                    else:
                        ins = A(vc[:, b, (c - 4) * H:(c - 3) * H], bank[:, :], ACT.Copy)
                ins.then_inc(S["qkv_evac"], 1)

            for c in range(6):
                ahead(U_QKV + 2 * c + 2 + SPLIT)
                qkv_evac(c)
            for i in range(C_HEADS + 1):
                if i < C_HEADS:
                    act.wait_ge(S["nm_done"], i + 1)
                    if i >= 2:
                        act.wait_ge(S["pt_done"], i - 1)
                    for t in range(NT):
                        ins = A(pr[i % 2][:, t, :], sc[i % 2][:, t, :], ACT.Exp, bias=nmax[:, i, t:t + 1],
                                accum_out=den[:, t, i:i + 1])
                        ins.then_inc(S["e_done"], 1)
                if i:
                    h = i - 1
                    act.wait_ge(S["pt_done"], h + 1)
                    if h >= 2:
                        act.wait_ge(S["oc_done"], h - 1)
                    A(prT[h % 2][:, :, :], B[2 + h % 2][:, :].rearrange("p (s t) -> p s t", s=NT),
                      ACT.Copy).then_inc(S["pt_copied"], 1)
            turned(5)
            ahead(U_MOE + 1)
            post(3, bank_src, lambda k: used(act, U_WOUT1 + (1 if k < 2 else 3)))
            norm(4)

            for j in range(4):
                act.wait_ge(S["hF_turned"], j + 1)
                A(hF[:, 2 * j:2 * j + 2, :], B[6 + j % 2][:, :].rearrange("p (k t) -> p k t", k=2),
                  ACT.Copy).then_inc(S["hF_copied"], 1)
            act.wait_ge(S["xg_ready"], 4)
            A(xg_hi[:, :, :], xn[:, :, :], ACT.Copy).then_inc(S["xgh_done"], 1)
            act.wait_ge(S["top_done"], 1)
            A(r1[:, 1, :, 0:1], r1[:, 0, :, 0:1], ACT.Exp).then_inc(S["top_exp"], 1)

            def gather_evac(k):
                act.wait_ge(S["gath_done"], k)
                for b in range(2):
                    ins = A(he_hi[:, 4 * b:4 * b + 4, :], B[5 + b][:, :].rearrange("p (k s) -> p k s", k=4), ACT.Copy)
                ins.then_inc(S["geh"], 1)

            def silu(u, turns):
                used(act, u + 1, turns)
                A(es[:, :], B[0][:, :], ACT.Silu).then_inc(S["esilu"], 1)

            def turned_hi(u):
                act.wait_ge(S["eturned"], u)
                A(eT_hi[:, :, :], B[4][:, :].rearrange("p (k s) -> p k s", k=4), ACT.Copy).then_inc(S["ehi"], 1)

            def y_high(i):
                used(act, U_MOE - 1, i * FE_STEPS)
                act.wait_ge(S["comb_done"], i + 1)
                act.wait_ge(S["selT_copied"], i + 1)
                for hf in range(2):
                    ins = A(y_hi[:, hf * H:(hf + 1) * H], B[2 + hf][:, :], ACT.Copy, scale=gslot[:, 0:1])
                ins.then_inc(S["yhi"], 1)

            gather_evac(1)
            act.wait_ge(S["items_ready"], 1)
            n_items = act.value_load(items[0:1, 12:13], min_val=N_EXPERTS, max_val=MAX_ITEMS)
            act.wait_ge(S["moe_init"], 3)
            with act.Fori(0, n_items) as i:
                turns = i * FE_STEPS
                round_hi(U_MOE + 1, turns)
                round_hi(U_MOE + 2, turns)
                y_high(i)
                round_hi(U_MOE + 3, turns)
                round_hi(U_MOE + 4, turns)
                silu(U_MOE, turns)
                with act.Fori(1, FE_STEPS) as f:
                    done = turns + f
                    round_hi(U_STEP + 1, done)
                    round_hi(U_STEP + 2, done)
                    turned_hi(done)
                    for k in range(3, 7):
                        round_hi(U_STEP + k, done)
                    silu(U_STEP, done)
                round_hi(U_TAIL + 1, turns + (FE_STEPS - 1))
                turned_hi(turns + FE_STEPS)
                gather_evac(i + 2)
                round_hi(U_TAIL + 2, turns + (FE_STEPS - 1))
            y_high(n_items + 0)
            all_turns = n_items * FE_STEPS
            p_turned_hi(1)
            nxt[0] = U_MOE + 1
            ahead(U_MOE + SPLIT, all_turns)
            post(4, lambda t, hf: acc[:, t, hf * H:(hf + 1) * H], lambda k: act.wait_ge(S["moe_acc"], k + 1))
            norm(5)
            turned(6, V_GAIN["ple1"])
            ple(1, U_MOE, all_turns)

        @block.vector
        def _(dve):
            steps = [0]
            TT, TS, STT = dve.tensor_tensor, dve.tensor_scalar, dve.scalar_tensor_tensor

            def mark(ins):
                steps[0] += 1
                ins.then_inc(S["dve_step"], 1)
                return steps[0]

            def link(ins):
                dve.wait_ge(S["dve_step"], mark(ins))

            def take_lo(u, turns=None):
                dve.wait_ge(S["hi_ready"], unit_count(u + 1, turns))
                TT(lo[u % SPLIT][:, :], raw[u % RAW][:, :], hi[u % SPLIT][:, :].bitcast(F32),
                   ALU.subtract).then_inc(S["lo_ready"], 1)

            nxt = [0]

            def ahead(end, turns=None):
                while nxt[0] < end:
                    take_lo(nxt[0], turns)
                    nxt[0] += 1

            def inverse_roots(r):
                dve.wait_ge(S["root_done"], r + 1)
                link(dve.reciprocal(rstd[:, :], root[:, 0:NT]))

            def add_eps(r):
                dve.wait_ge(S["sq_done"], 4 * r + 2)
                TS(sums_e[:, :], sums[:, 0:2], EPS, None, ALU.add).then_inc(S["eps_added"], 1)

            def norm(n):
                add_eps(2 * n)
                inverse_roots(2 * n)
                for t in range(NT):
                    ins = TS(diags[n][:, t, :], ident[:, :], rstd[:, t:t + 1], None, ALU.mult)
                ins.then_inc(S["diag_ready"], 1)

            def turned(m, gain=None, js=range(4)):
                for j in js:
                    dve.wait_ge(S["hT_hi_done"], 4 * m + j + 1)
                    for b in range(2):
                        kt = 2 * j + b
                        src, top = turn_bank(m, j)[:, b * SEQ:(b + 1) * SEQ], hT_hi[:, kt, :].bitcast(F32)
                        if gain is None:
                            ins = TT(hT_lo[:, kt, :], src, top, ALU.subtract)
                        else:
                            ins = STT(hT_lo[:, kt, :], src, vcol[:, gain + kt:gain + kt + 1], top, ALU.mult, ALU.subtract)
                    ins.then_inc(S["hT_lo_done"], 1)

            def post(n, src):
                g, r = n if n < 4 else n + 1, 2 * n + 1
                dve.wait_ge(gb_in[g % 2], 16 * (g // 2 + 1))
                for k, (t, hf) in enumerate(QUARTERS):
                    cols = slice(hf * H, (hf + 1) * H)
                    dve.wait_ge(S["sq_done"], 4 * r + k + 1)
                    TT(xn[:, t, cols], src(t, hf), gb[g % 2][:, cols], ALU.mult)
                    if k == 1:
                        add_eps(r)
                inverse_roots(r)
                for t, hf in QUARTERS:
                    cols = slice(hf * H, (hf + 1) * H)
                    STT(x[:, t, cols], xn[:, t, cols], rstd[:, t:t + 1], x[:, t, cols],
                        ALU.mult, ALU.add).then_inc(S["x_ready"], 1)

            dve.wait_ge(S["vcol_t"], 1)
            dve.tensor_copy(vcol[:, :], B[7][:, 0:V_N]).then_inc(S["vcol_ready"], 1)
            dve.wait_ge(S["vcol_ready"], 1)
            raw3 = vcol[:, V_LB:V_LB + 12].rearrange("p (l h) -> p l h", l=3)
            link(TT(lbt[:, 6, :], raw3[:, 0, :], raw3[:, 1, :], ALU.max))
            link(TT(lbt[:, 7, :], lbt[:, 6, :], raw3[:, 2, :], ALU.max))
            for l in range(3):
                ins = TT(lbt[:, l, :], raw3[:, l, :], lbt[:, 7, :], ALU.subtract)
            ins.then_inc(S["gates_done"], 1)
            norm(0)
            ahead(1)
            turned(0, V_GAIN["mix0"])
            dve.wait_ge(S["wdt_hi_done"], 1)
            TT(wdt_lo[:, :, :], wdt[:, :, :], wdt_hi[:, :, :].bitcast(F32), ALU.subtract).then_inc(S["wdt_lo_done"], 1)

            def lower_bounds():
                dve.wait_ge(S["logs_done"], 1)
                link(TT(lbt[:, 6, :], lbt[:, 3, :], lbt[:, 4, :], ALU.add))
                link(TT(lbt[:, 6, :], lbt[:, 6, :], lbt[:, 5, :], ALU.add))
                link(dve.reciprocal(lbt[:, 7, :], lbt[:, 6, :]))
                link(TT(lbt[:, 8, :], lbt[:, 3, :], lbt[:, 7, :], ALU.mult))
                link(TS(lbt[:, 9, :], lbt[:, 8, :], -1.0, 1.0, ALU.mult, ALU.add))

            def gates(d):
                dve.wait_ge(S["win_evac"], d + 1)
                for h in range(A_HEADS):
                    ins = TS(G[d][:, h, :], G[d][:, h, :], lbt[:, 9, h:h + 1], lbt[:, 8, h:h + 1], ALU.mult, ALU.add)
                    n = mark(ins)
                dve.wait_ge(S["dve_step"], n)
                TS(kT[d][:, :, :], G[d][:, :, :], -1.0, 1.0, ALU.mult, ALU.add).then_inc(S["gates_done"], 1)

            def scans(d):
                dve.wait_ge(S["logs_done"], 2 + d)
                dve.wait_ge(S["consts"], 1)
                if d:
                    v = PS[1][:, :, :].rearrange("p h (t c) -> p (h t) c", c=P)
                    dve.memset(v[:, :, 0:1], 0.0)
                for h in range(A_HEADS):
                    for t in range(NT):
                        if d == 0:
                            o, i_ = PS[0][:, h, t * P:(t + 1) * P], G[0][:, h, t * P:(t + 1) * P]
                        else:
                            o, i_ = PS[1][:, h, t * P + 1:(t + 1) * P], G[1][:, h, t * P:(t + 1) * P - 1]
                        n = mark(dve.tensor_tensor_scan(o, ones[:, 0:P - d], i_, 0.0, ALU.mult, ALU.add))
                dve.wait_ge(S["dve_step"], n)
                if d:
                    link(TT(btot[:, :, :], PS[1][:, :, P - 1:P], G[1][:, :, P - 1:P], ALU.add))
                dve.sem_inc(S["scans_done"], 1)

            def job_mul(j):
                d, lv = JOBS[j]
                dve.wait_ge(S["job_exp"], j + 1)
                E = EB[JBUF[j][0] % 4]
                if lv == 0:
                    E2_ = EB[JBUF[j][1] % 4]
                    eq, ek = (E, E2_) if d == 0 else (E2_, E)
                    TT(eq, eq, qT[:, :, :], ALU.mult)
                    TT(ek, ek, kT[d][:, :, :], ALU.mult).then_inc(S["job_mul"], 1)
                    return
                w = 2 * lv
                e, q_, k_ = (v.rearrange("p h (b x) -> p (h b) x", x=w) for v in (E, qT[:, :, :], kT[d][:, :, :]))
                left, right = (k_, q_) if d == 0 else (q_, k_)
                TT(e[:, :, :lv], e[:, :, :lv], left[:, :, :lv], ALU.mult)
                TT(e[:, :, lv:], e[:, :, lv:], right[:, :, lv:], ALU.mult).then_inc(S["job_mul"], 1)

            def job_evac(j):
                d, lv = JOBS[j]
                dve.wait_ge(S["job_pe"], j + 1)
                if j == 0:
                    dve.wait_ge(S["consts"], 3)
                for n, w in enumerate(JBANK[j]):
                    bank = B[4 + w % 4][:, :].rearrange("p (h t) -> p h t", h=A_HEADS)
                    if w >= 2:
                        dve.wait_ge(S["job_evac"], w - 1)
                    if lv == 128:
                        s_, t0 = (0, P) if d == 0 else (1, 0)
                        dve.tensor_copy(AT[:, :, s_, t0:t0 + P], bank).then_inc(S["job_evac"], 1)
                        continue
                    if lv == 64:
                        ks, qs = (0, 64) if d == 0 else (64, 0)
                        dve.tensor_copy(AT[ks:ks + 64, :, n, n * P + qs:n * P + qs + 64],
                                        bank[ks:ks + 64, :, qs:qs + 64]).then_inc(S["job_evac"], 1)
                        continue
                    m = hmask[(d, lv)][:, :].bitcast(I32).rearrange("p (o t) -> p o t", o=1).to_broadcast([P, A_HEADS, P])
                    own = AT[:, :, n, n * P:(n + 1) * P]
                    if (d, lv) == (1, 0):
                        link(dve.copy_predicated(AT2[:, :, :], m, bank))
                        link(TT(own, own, AT2[:, :, :], ALU.add))
                        dve.sem_inc(S["job_evac"], 1)
                    else:
                        dve.copy_predicated(own, m, bank).then_inc(S["job_evac"], 1)

            def softplus():
                dve.wait_ge(S["dt_mm"], 1)
                dve.wait_ge(S["small_in"], 16 * 4)
                b16 = dtbb.rearrange("p (o c) -> p o c", o=1).to_broadcast([P, NT, 16])
                link(TT(dts[:, 0, :, :], B[5][:, 0:2 * 16].rearrange("p (t c) -> p t c", t=NT), b16, ALU.add))
                STT(dts[:, 1, :, :], dts[:, 0, :, :], -1.0, dts[:, 0, :, :], ALU.mult, ALU.max).then_inc(S["dt_ready"], 1)

            def softplus2():
                dve.wait_ge(S["dt_done"], 1)
                TS(dts[:, 3, :, :], dts[:, 2, :, :], 1.0, None, ALU.add).then_inc(S["dt_ready"], 1)

            def softplus3():
                e = dts[:, 2, :, :]
                dve.wait_ge(S["dt_ready"], 2)
                link(TS(dts[:, 5, :, :], dts[:, 3, :, :], -1.0, 1e-30, ALU.add, ALU.max))
                link(dve.reciprocal(dts[:, 6, :, :], dts[:, 5, :, :]))
                link(TT(dts[:, 6, :, :], dts[:, 6, :, :], e, ALU.mult))
                link(TS(dts[:, 5, :, :], e, -0.5, 1.0, ALU.mult, ALU.add))
                link(TT(dts[:, 5, :, :], dts[:, 5, :, :], e, ALU.mult))
                dve.wait_ge(S["dt_done"], 3)
                link(TT(dts[:, 6, :, :], dts[:, 6, :, :], dts[:, 4, :, :], ALU.mult))
                link(TT(dts[:, 6, :, :], dts[:, 6, :, :], dts[:, 5, :, :], ALU.max))
                link(TS(dts[:, 7, :, :], dts[:, 0, :, :], 0.0, None, ALU.max))
                link(TT(dta[:, :, :], dts[:, 7, :, :], dts[:, 6, :, :], ALU.add))
                link(TS(nexpa[:, :], nexpa[:, :], -1.0, None, ALU.mult))
                n16 = nexpa[:, :].rearrange("p (o c) -> p o c", o=1).to_broadcast([P, NT, 16])
                TT(acs[:, :, :], dta[:, :, :], n16, ALU.mult).then_inc(S["dt_ready"], 1)

            def conv(b):
                dve.wait_ge(S["win_evac"], 4 + 2 * b)
                made = [0] * 4
                for j in range(B_CONV):
                    for i in range(4):
                        ct = 4 * b + i
                        src, dst = cin[:, i, j:j + SEQ], cout[:, ct, :]
                        w = vcol[:, V_CW + 8 * j + ct:V_CW + 8 * j + ct + 1]
                        if j == 0:
                            ins = TS(dst, src, w, vcol[:, V_CB + ct:V_CB + ct + 1], ALU.mult, ALU.add)
                        else:
                            dve.wait_ge(S["dve_step"], made[i])
                            ins = STT(dst, src, w, dst, ALU.mult, ALU.add)
                        if j == B_CONV - 1:
                            ins.then_inc(S["conv_done"], 1)
                        else:
                            made[i] = mark(ins)

            for c in range(9):
                ahead(min(U_WIN + 2 * c + SPLIT, U_WOUT0))
                if c == 1:
                    lower_bounds()
                if c == 2:
                    gates(0)
                if c == 3:
                    gates(1)
                    scans(0)
                    dve.wait_ge(S["win_evac"], 3)
                    softplus()
                if c == 4:
                    scans(1)
                if c > JOB_ROUND0:
                    for j in (2 * (c - 1 - JOB_ROUND0), 2 * (c - 1 - JOB_ROUND0) + 1):
                        job_evac(j)
                if JOB_ROUND0 <= c < 8:
                    for j in (2 * (c - JOB_ROUND0), 2 * (c - JOB_ROUND0) + 1):
                        job_mul(j)
                if c == 5:
                    softplus2()
                    conv(0)
                if c == 7:
                    softplus3()
                    conv(1)

            dve.wait_ge(S["cols_done"], 1)
            cb = B[0][:, 0:48]
            for t in range(NT):
                TS(Ccol[:, t, 0:8], cb[:, 16 * t:16 * t + 8], 1.0, None, ALU.mult)
                ins = TS(Ccol[:, t, 8:16], cb[:, 16 * t + 8:16 * t + 16], -1.0, None, ALU.mult)
            n = mark(ins)
            dve.wait_ge(S["dve_step"], n)
            TT(Cx[:, 0:8], Ccol[:, 0, 0:8], cb[:, 32:40], ALU.subtract)
            TT(Cx[:, 8:16], Ccol[:, 1, 8:16], cb[:, 40:48], ALU.subtract).then_inc(S["cols_copied"], 1)
            dve.wait_ge(S["rows_turned"], 1)
            dve.wait_ge(S["cs_hi_done"], 1)
            TT(cs_lo, B[1][0:16, 0:SEQ], cs_hi.bitcast(F32), ALU.subtract).then_inc(S["rows_copied"], 1)

            def exponents(h):
                dve.wait_ge(S["rbc_done"], h + 1)
                if h >= 2:
                    dve.wait_ge(S["w_done"], h - 1)
                bank, L = B[2 + h % 2], Lb[h % 2]
                f, b = slice(h, h + 1), slice(8 + h, 9 + h)
                for o, c0, col in ((0, 0, Ccol[:, 0, f]), (1, P, Cx[:, f]), (2, P, Ccol[:, 1, f]),
                                   (3, 2 * P, Ccol[:, 0, b]), (4, 2 * P, Cx[:, b]), (5, 3 * P, Ccol[:, 1, b])):
                    ins = TS(L[:, o * P:(o + 1) * P], bank[:, c0:c0 + P], col, 0.0, ALU.subtract, ALU.min)
                ins.then_inc(S["rbc_used"], 1)

            dve.wait_ge(S["g_done"], 1)
            for g in range(B_GROUPS):
                bank = B[4 + g]
                TT(Gm[g][:, 0:P], bank[:, 0:P], le[:, :], ALU.mult)
                dve.tensor_copy(Gm[g][:, P:2 * P], bank[:, P:2 * P])
                TT(Gm[g][:, 2 * P:3 * P], bank[:, 3 * P:4 * P], le[:, :], ALU.mult)
                TT(Gm[g][:, 3 * P:4 * P], bank[:, 0:P], ge[:, :], ALU.mult)
                dve.tensor_copy(Gm[g][:, 4 * P:5 * P], bank[:, 2 * P:3 * P])
                TT(Gm[g][:, 5 * P:6 * P], bank[:, 3 * P:4 * P], ge[:, :], ALU.mult).then_inc(S["gm_done"], 1)
            dve.wait_ge(S["root_a"], 1)
            dve.reciprocal(nrm[:, 0:8], nrm[:, 0:8]).then_inc(S["inverse_a"], 1)
            dve.wait_ge(S["xs_turned"], 1)
            for t in range(NT):
                ins = dve.tensor_copy(xsn[:, t, :], B[6 + t][:, :])
            ins.then_inc(S["xs_copied"], 1)
            def scores(h):
                dve.wait_ge(S["l_exp"], h + 1)
                if h >= 2:
                    dve.wait_ge(S["y_pe"], h - 1)
                L, W, g = Lb[h % 2], Wb[h % 2], Gm[h // (B_HEADS // B_GROUPS)]
                for c0, c1, t, k in ((0, 256, 0, h), (256, 384, 1, h), (384, 512, 0, 8 + h), (512, 768, 1, 8 + h)):
                    ins = STT(W[:, c0:c1], L[:, c0:c1], dta[:, t, k:k + 1], g[:, c0:c1], ALU.mult, ALU.mult)
                ins.then_inc(S["w_done"], 1)

            dve.wait_ge(S["gm_done"], 2)
            for h in range(B_HEADS + 1):
                if h < B_HEADS:
                    exponents(h)
                if h:
                    scores(h - 1)
                if 2 <= h <= 4:
                    ahead(U_WOUT0 + h - 1)
                if h == 5:
                    turned(1, None, (0, 1))
            dve.wait_ge(S["y_pe"], B_HEADS)
            dve.wait_ge(S["dxs_done"], 2)
            ob = [xn[:, t, H + 256:D] for t in range(NT)]
            for t in range(NT):
                n = mark(TT(ob[t], Y_BANKS[1][t][:, 0:256], tmpn[:, t, 256:], ALU.add))
            dve.wait_ge(S["dve_step"], n)
            for t in range(NT):
                TT(ob[t], ob[t], vgz[:, 2, t, 256:], ALU.mult).then_inc(S["second_gated"], 1)
            dve.wait_ge(S["root_b"], 1)
            dve.wait_ge(S["bnb_in"], 16)
            link(dve.reciprocal(nrm[:, 8:12], nrm[:, 8:12]))
            for g in range(B_GROUPS):
                for t in range(NT):
                    c = slice(g * 256, (g + 1) * 256)
                    k = 8 + 2 * t + g
                    v = xn[:, t, H + g * 256:H + (g + 1) * 256]
                    ins = STT(v, v, nrm[:, k:k + 1], bnb[:, c], ALU.mult, ALU.mult)
                ins.then_inc(S["mix_b"], 1)
            ahead(U_WOUT0 + 4)
            turned(1, None, (2, 3))
            ahead(U_FFN + SPLIT)

            def bank_src(t, hf):
                return B[2 * hf + t][:, :]
            post(0, bank_src)
            norm(1)
            turned(2, V_GAIN["ffn0"])

            def ff_evac(c, b, loop=None):
                k = lambda v: v if loop is None else loop * 2 + v
                dve.wait_ge(S["ff_silu"], k(c + 1))
                for j in range(2):
                    ins = TT(ffs[:, j, :], ffs[:, j, :], B[2 * b + j][:, SEQ:], ALU.mult)
                ins.then_inc(S["ff_mul"], 1)
                dve.wait_ge(S["ff_hi"], k(c + 1))
                TT(ffl[b][:, :, :], ffs[:, :, :], ffh[b][:, :, :].bitcast(F32), ALU.subtract).then_inc(S["ff_lo"], 1)

            ff_evac(0, 0)
            with dve.Fori(0, (FF_STEPS - 1) // 2) as it:
                for b in range(2):
                    for m in range(3):
                        take_lo(U_FFN + 3 + 3 * b + m, it)
                    ff_evac(1 + b, (1 + b) % 2, it)

            def p_turned_lo(n):
                dve.wait_ge(S["pT_hi_done"], n + 1)
                TT(pT_lo[n][:, :, :], P_BANK[n][:, :].rearrange("p (k t) -> p k t", k=2), pT_hi[n][:, :, :].bitcast(F32),
                   ALU.subtract).then_inc(S["pT_lo_done"], 1)

            nxt[0] = U_PLE0
            p_turned_lo(0)
            ahead(U_PLE0 + SPLIT)

            def bank_y(t, hf):
                return B[4 + 2 * t + hf][:, :]
            post(1, bank_y)
            norm(2)
            turned(3, V_GAIN["ple0"])

            def ple(n, u0, turns=None):
                ahead(u0 + 5, turns)
                for k, (t, hf) in enumerate(QUARTERS):
                    dve.wait_ge(S["sig_done"], 4 * n + k + 1)
                    v = gate[n][:, t, hf * H:(hf + 1) * H]
                    TT(v, v, PROJ_BANKS[n][k][:, :], ALU.mult).then_inc(S["ply_done"], 1)
                    if k == 1 and n == 0:
                        ahead(U_QKV + 1)
                post(2 if n == 0 else 5, lambda t, hf: gate[n][:, t, hf * H:(hf + 1) * H])

            ple(0, U_PLE0)
            norm(3)
            ahead(U_QKV + SPLIT)
            turned(4, V_GAIN["mix1"])

            for c in range(6):
                ahead(U_QKV + 2 * c + 2 + SPLIT)
            for h in range(C_HEADS):
                dve.wait_ge(S["s_done"], h + 1)
                if h >= 2:
                    dve.wait_ge(S["e_done"], 2 * (h - 1))
                link(STT(sc[h % 2][:, :, :].rearrange("p t s -> p (t s)"), B[h % 2][:, :], C_HD ** -0.5,
                         bias[:, h, :, :].rearrange("p t s -> p (t s)"), ALU.mult, ALU.add))
                dve.tensor_reduce(nmax[:, h, :], sc[h % 2][:, :, :], AX.X, ALU.max, negate=True).then_inc(S["nm_done"], 1)
            dve.wait_ge(S["e_done"], 2 * C_HEADS)
            link(dve.reciprocal(rden[:, :, :], den[:, :, :]))
            for half in range(2):
                dve.wait_ge(S["oc_done"], 8 * half + 8)
                for t in range(NT):
                    r_ = rden[:, t, 8 * half:8 * half + 8].rearrange("p (h o) -> p h o", o=1).to_broadcast([P, 8, C_HD])
                    TT(xn[:, t, half * H:(half + 1) * H].rearrange("p (h c) -> p h c", c=C_HD),
                       B[4 + 2 * half + t][:, :].rearrange("p (h c) -> p h c", c=C_HD), r_, ALU.mult).then_inc(S["oc_norm"], 1)
            turned(5)
            ahead(U_MOE + 1)
            post(3, bank_src)
            add_eps(2 * 4)
            inverse_roots(2 * 4)
            dve.wait_ge(gb_in[0], 16 * 3)
            for t, hf in QUARTERS:
                cols = slice(hf * H, (hf + 1) * H)
                STT(xn[:, t, cols], x[:, t, cols], rstd[:, t:t + 1], gb[0][:, cols], ALU.mult, ALU.mult) \
                    .then_inc(S["xg_ready"], 1)
            dve.wait_ge(S["lg_done"], 1)
            link(dve.tensor_copy(lg[:, :, :], B[5][:, 0:16].rearrange("p (t e) -> p t e", t=NT)))
            for t in range(NT):
                n = mark(dve.max(mx8[:, t, :], lg[:, t, :]))
            dve.wait_ge(S["dve_step"], n)
            TT(r1[:, 0, :, 0:1], mx8[:, :, 1:2], mx8[:, :, 0:1], ALU.subtract).then_inc(S["top_done"], 1)
            for t in range(NT):
                n = mark(dve.max_index(ix8[:, t, :], mx8[:, t, :], lg[:, t, :]))
            dve.wait_ge(S["dve_step"], n)
            link(dve.tensor_copy(ixf[:, :, :], ix8[:, :, :]))
            dve.wait_ge(S["moe_consts"], 3)
            iota8 = iota_f[:, 0:8].rearrange("p (a b e) -> p a b e", a=1, b=1)
            link(TT(oh[:, :, :, :], iota8.to_broadcast([P, NT, 2, 8]),
                    ixf[:, :, 0:2].rearrange("p t (c o) -> p t c o", o=1).to_broadcast([P, NT, 2, 8]), ALU.is_equal))
            TT(msk[:, :, :], oh[:, :, 0, :], oh[:, :, 1, :], ALU.add).then_inc(S["mask_done"], 1)
            dve.wait_ge(S["top_exp"], 1)
            link(TS(r1[:, 2, :, 0:1], r1[:, 1, :, 0:1], 1.0, None, ALU.add))
            link(dve.reciprocal(r1[:, 3, :, 0:1], r1[:, 2, :, 0:1]))
            link(TT(r1[:, 4, :, 0:1], r1[:, 3, :, 0:1], r1[:, 1, :, 0:1], ALU.mult))
            over8 = lambda v: v.to_broadcast([P, NT, 8])
            TT(r1[:, 5, :, :], oh[:, :, 1, :], over8(r1[:, 4, :, 0:1]), ALU.mult)
            link(TT(r1[:, 7, :, :], oh[:, :, 0, :], over8(r1[:, 3, :, 0:1]), ALU.mult))
            link(TT(gat[:, :, 0:8], r1[:, 5, :, :], r1[:, 7, :, :], ALU.add))
            dve.wait_ge(S["pos_done"], 1)
            pos = B[4][:, 0:16].rearrange("p (t e) -> p t e", t=NT)
            link(STT(r1[:, 6, :, :], pos, 1.0, msk[:, :, :], ALU.add, ALU.mult))
            link(TS(posx[:, :, 0:8], r1[:, 6, :, :], -1.0, None, ALU.add))

            def build_sel(i):
                for t in range(NT):
                    TS(sel[:, t, :], iota_f[:, :], posx[:, t, bass.ds(i, 1)], None, ALU.is_equal)
                dve.tensor_copy(gcol[:, :, :], gat[:, :, bass.ds(i, 1)]).then_inc(S["sel_built"], 1)

            build_sel(0)
            TS(flag[:, :], B[4][:, 16:24], float(P), None, ALU.is_gt)
            link(dve.memset(fpos[:, 0:1], 0.0))
            dve.tensor_tensor_scan(fpos[:, 1:9], ones[:, 0:8], flag[:, :], 0.0, ALU.mult, ALU.add)
            link(STT(r1[:, 7, :, :], msk[:, :, :], -float(P), r1[:, 6, :, :], ALU.mult, ALU.add))
            iota3 = iota_f[:, 0:3].rearrange("p (k o) -> p k o", o=1).to_broadcast([P, 3, 8])
            by3 = lambda v: v.rearrange("p (o e) -> p o e", o=1).to_broadcast([P, 3, 8])
            link(TT(ohx[:, :, :], by3(fpos[:, 0:8]), iota3, ALU.is_equal))
            link(TT(ohx[:, :, :], ohx[:, :, :], by3(flag[:, :]), ALU.mult))
            TT(r3[:, 0, 0, :, :], ohx[:, :, :], by3(iota_f[:, 0:8]), ALU.mult)
            link(TS(itf[:, 12:13], fpos[:, 8:9], float(N_EXPERTS), None, ALU.add))
            link(dve.tensor_reduce(itf[:, 8:11], r3[:, 0, 0, :, :], AX.X, ALU.add))
            dve.tensor_copy(items[0:1, :], itf[0:1, :]).then_inc(S["items_ready"], 1)
            each = ohx[:, :, :].rearrange("p (o k) e -> p o k e", o=1).to_broadcast([P, NT, 3, 8])
            for n, v in enumerate((r1[:, 7, :, :], gat[:, :, 0:8])):
                n_done = mark(TT(r3[:, n, :, :, :], each, v.rearrange("p t (o e) -> p t o e", o=1).to_broadcast([P, NT, 3, 8]),
                                 ALU.mult))
            dve.wait_ge(S["dve_step"], n_done)
            for n, v in enumerate((posx, gat)):
                ins = dve.tensor_reduce(v[:, :, 8:11], r3[:, n, :, :, :], AX.X, ALU.add)
            link(ins)
            TS(posx[:, :, 8:11], posx[:, :, 8:11], -1.0, None, ALU.add)
            dve.memset(posx[:, :, 11:12], -1.0)
            link(dve.memset(gat[:, :, 11:12], 0.0))
            dve.wait_ge(S["items_ready"], 1)
            n_items = dve.value_load(items[0:1, 12:13], min_val=N_EXPERTS, max_val=MAX_ITEMS)

            def gather_evac(k):
                dve.wait_ge(S["geh"], k)
                for b in range(2):
                    ins = TT(he_lo[:, 4 * b:4 * b + 4, :], B[5 + b][:, :].rearrange("p (k s) -> p k s", k=4),
                             he_hi[:, 4 * b:4 * b + 4, :].bitcast(F32), ALU.subtract)
                ins.then_inc(S["gel"], 1)

            def product(k, u, turns):
                dve.wait_ge(S["esilu"], k)
                used(dve, u + 3, turns)
                TT(ea[:, :], es[:, :], B[1][:, :], ALU.mult).then_inc(S["emul"], 1)

            def turned_lo(u):
                dve.wait_ge(S["ehi"], u)
                TT(eT_lo[:, :, :], B[4][:, :].rearrange("p (k s) -> p k s", k=4), eT_hi[:, :, :].bitcast(F32),
                   ALU.subtract).then_inc(S["elo"], 1)

            def y_low(i):
                dve.wait_ge(S["yhi"], i + 1)
                for hf in range(2):
                    c = slice(hf * H, (hf + 1) * H)
                    ins = STT(y_lo[:, c], B[2 + hf][:, :], gslot[:, 0:1], y_hi[:, c].bitcast(F32), ALU.mult, ALU.subtract)
                ins.then_inc(S["ylo"], 1)

            COMB = [B[5], B[6], B[7], B[3]]

            def add_item(i, s=None):
                dve.wait_ge(S["comb_done"], i + 2)
                for k, (t, hf) in enumerate(QUARTERS):
                    v = acc[:, t, hf * H:(hf + 1) * H]
                    ins = TT(v, v, COMB[k][:, :], ALU.add)
                    if s:
                        ins.then_inc(s, 1)
                return ins

            dve.memset(B[2][:, :], 0.0)
            dve.memset(B[3][:, :], 0.0)
            dve.memset(gslot[:, :], 0.0).then_inc(S["selT_copied"], 1)
            gather_evac(1)
            dve.wait_ge(S["moe_init"], 3)
            with dve.Fori(0, n_items) as i:
                turns = i * FE_STEPS
                take_lo(U_MOE + 1, turns)
                take_lo(U_MOE + 2, turns)
                y_low(i)
                take_lo(U_MOE + 3, turns)
                take_lo(U_MOE + 4, turns)
                product(turns + 1, U_MOE, turns)
                add_item(i).then_inc(S["comb_added"], 1)
                dve.wait_ge(S["selT_done"], i + 1)
                dve.tensor_copy(selT[:, :], B[2][:, 0:SEQ])
                dve.tensor_copy(gslot[:, :], B[2][:, SEQ:SEQ + 1]).then_inc(S["selT_copied"], 1)
                build_sel(i + 1)
                with dve.Fori(1, FE_STEPS) as f:
                    done = turns + f
                    take_lo(U_STEP + 1, done)
                    take_lo(U_STEP + 2, done)
                    turned_lo(done)
                    for k in range(3, 7):
                        take_lo(U_STEP + k, done)
                    product(done + 1, U_STEP, done)
                take_lo(U_TAIL + 1, turns + (FE_STEPS - 1))
                turned_lo(turns + FE_STEPS)
                gather_evac(i + 2)
                take_lo(U_TAIL + 2, turns + (FE_STEPS - 1))
            y_low(n_items + 0)
            all_turns = n_items * FE_STEPS
            p_turned_lo(1)
            nxt[0] = U_MOE + 1
            ahead(U_MOE + SPLIT, all_turns)
            add_item(n_items + 0, S["moe_acc"])
            post(4, lambda t, hf: acc[:, t, hf * H:(hf + 1) * H])
            norm(5)
            turned(6, V_GAIN["ple1"])
            ple(1, U_MOE, all_turns)

        @block.tensor
        def _(pe):
            def mm(o, l, r, first, last=False):
                return pe.matmul(o, l, r, start=first, stop=last, skip_group_check=True)

            def mm3(o, l, r, first, last=False):
                mm(o, l[0], r[0], first)
                mm(o, l[0], r[1], False)
                return mm(o, l[1], r[0], False, last)

            def unit_ready(u, turns=None):
                pe.wait_ge(S["lo_ready"], unit_count(u + 1, turns))

            def parts(u, k):
                return views(hi[u % SPLIT], k), views(lo[u % SPLIT], k)

            def turn(m, src_ready, n=None, js=range(4)):
                src_ready()
                for j in js:
                    if j >= 2 and m != 1:
                        pe.wait_ge(S["hT_lo_done"], 4 * m + j - 1)
                    for b in range(2):
                        for t in range(NT):
                            kt = 2 * j + b
                            o = turn_bank(m, j)[:, b * SEQ + t * P:b * SEQ + (t + 1) * P]
                            cols = slice(kt * P, (kt + 1) * P)
                            if n is None:
                                ins = pe.transpose(o, xn[:, t, cols], ident[:, :])
                            else:
                                ins = mm(o, x[:, t, cols], diags[n][:, t, :], b == 0 and t == 0, True)
                    ins.then_inc(S["turned"], 1)

            def turn_norm(m, n):
                turn(m, lambda: pe.wait_ge(S["diag_ready"], n + 1 if n < 4 else n), n)

            def weights_still(u, hf, banks):
                w = parts(u, 4)
                for ct in range(4):
                    for kk in range(4):
                        o = banks[ct // 2][:, (ct % 2) * SEQ:(ct % 2 + 1) * SEQ]
                        l = [v[:, kk, ct * P:(ct + 1) * P] for v in w]
                        r = [hT_hi[:, 4 * hf + kk, :], hT_lo[:, 4 * hf + kk, :]]
                        ins = mm3(o, l, r, hf == 0 and kk == 0 and ct % 2 == 0, hf == 1 and kk == 3)
                return ins

            def tokens_still(u, k, kt0, outs, src, first, last, n_cols=H):
                w = parts(u, k)
                for bank, t, c0 in outs:
                    for kk in range(k):
                        l = [v[:, kt0 + kk, t * P:(t + 1) * P] for v in src]
                        r = [v[:, kk, c0:c0 + n_cols] for v in w]
                        ins = mm3(bank[:, 0:n_cols], l, r, first and kk == 0, last and kk == k - 1)
                return ins

            hT = (hT_hi[:, :, :], hT_lo[:, :, :])

            pe.wait_ge(S["ident_ready"], 1)
            pe.wait_ge(S["vrow_in"], 16 * 8)
            pe.transpose(B[7][:, 0:V_N], vrow, ident[0:V_N, 0:V_N]).then_inc(S["vcol_t"], 1)
            pe.wait_ge(S["vcol_ready"], 1)
            turn_norm(0, 0)

            def job(j):
                d, lv = JOBS[j]
                pe.wait_ge(S["job_mul"], j + 1)
                E = EB[JBUF[j][0] % 4]
                for n, w in enumerate(JBANK[j]):
                    if w >= 4:
                        pe.wait_ge(S["job_evac"], w - 3)
                    bank = B[4 + w % 4]
                    own = slice(n * P, (n + 1) * P)
                    for h in range(A_HEADS):
                        if lv == 0:
                            eq, ek = (E, EB[JBUF[j][1] % 4]) if d == 0 else (EB[JBUF[j][1] % 4], E)
                            l, r = ek[:, h, own], eq[:, h, own]
                        elif lv < 128:
                            l = r = E[:, h, own]
                        else:
                            l, r = (E[:, h, 0:P], E[:, h, P:]) if d == 0 else (E[:, h, P:], E[:, h, 0:P])
                        ins = mm(bank[:, h * P:(h + 1) * P], l, r, h == 0, True)
                ins.then_inc(S["job_pe"], 1)

            pe.wait_ge(S["hT_lo_done"], 4)
            for c, (name, _) in enumerate(WIN_GROUPS):
                still = name not in ("v", "g", "z")
                banks = [B[2 * (c % 2)], B[2 * (c % 2) + 1]]
                if c >= 2:
                    pe.wait_ge(S["win_evac"], c - 1)
                for hf in range(2):
                    u = U_WIN + 2 * c + hf
                    unit_ready(u)
                    if still:
                        ins = weights_still(u, hf, banks)
                    else:
                        ins = tokens_still(u, 4, 4 * hf, [(banks[t], t, 0) for t in range(NT)], hT, hf == 0, hf == 1)
                    ins.then_inc(S["unit_used"], 1)
                if c == 2:
                    pe.wait_ge(S["wdt_lo_done"], 1)
                    for t in range(NT):
                        for kt in range(KT):
                            l = [v[:, kt, t * P:(t + 1) * P] for v in hT]
                            ins = mm3(B[5][:, t * 16:(t + 1) * 16], l, [wdt_hi[:, kt, :], wdt_lo[:, kt, :]],
                                      t == 0 and kt == 0, kt == KT - 1)
                    ins.then_inc(S["dt_mm"], 1)
                if c >= JOB_ROUND0:
                    if c == JOB_ROUND0:
                        pe.wait_ge(S["dt_ready"], 1)
                    for j in (2 * (c - JOB_ROUND0), 2 * (c - JOB_ROUND0) + 1):
                        job(j)

            pe.wait_ge(S["dt_ready"], 3)
            pe.wait_ge(S["win_evac"], 7)
            for t in range(NT):
                mm(B[0][:, 16 * t:16 * t + 8], le, acs[:, t, 0:8], t == 0, True)
                mm(B[0][:, 16 * t + 8:16 * t + 16], lt[:, :], acs[:, t, 8:16], False, True)
            mm(B[0][:, 32:48], ones[:, :], acs[:, 0, :], False, True).then_inc(S["cols_done"], 1)
            pe.wait_ge(S["cols_copied"], 1)
            for t in range(NT):
                ins = pe.transpose(B[1][0:16, t * P:(t + 1) * P], Ccol[:, t, :], ident[:, :])
            ins.then_inc(S["rows_turned"], 1)

            pe.wait_ge(S["job_evac"], JBANK[-1][-1] + 1)
            pe.wait_ge(S["rows_copied"], 1)
            for t in range(NT):
                for h in range(A_HEADS):
                    for s_ in range(NT):
                        ins = mm(B[t][:, h * P:(h + 1) * P], AT[:, h, s_, t * P:(t + 1) * P],
                                 vgz[:, 0, s_, h * P:(h + 1) * P], h == 0 and s_ == 0, s_ == NT - 1)
            ins.then_inc(S["o_done"], 1)

            def rbc(h):
                if h >= 2:
                    pe.wait_ge(S["rbc_used"], h - 1)
                for d in range(2):
                    k = 8 * d + h
                    pick = ident_r[0:16, k:k + 1].to_broadcast([16, P])
                    for n, v in enumerate((cs_hi, cs_lo)):
                        ins = mm(B[2 + h % 2][:, d * SEQ:(d + 1) * SEQ], pick, v, d == 0 and n == 0, n == 1)
                ins.then_inc(S["rbc_done"], 1)

            pe.wait_ge(S["conv_silu"], 2)
            for g in range(B_GROUPS):
                for s_ in range(NT):
                    ins = mm(B[4 + g][:, s_ * SEQ:(s_ + 1) * SEQ], cout[:, 4 + g, s_ * P:(s_ + 1) * P], cout[:, 6 + g, :],
                             s_ == 0, True)
            ins.then_inc(S["g_done"], 1)
            for t in range(NT):
                for ct in range(4):
                    ins = pe.transpose(B[6 + t][:, ct * P:(ct + 1) * P], cout[:, ct, t * P:(t + 1) * P], ident[:, :])
            ins.then_inc(S["xs_turned"], 1)
            pe.wait_ge(S["win_evac"], 8)
            rbc(0)
            rbc(1)
            pe.wait_ge(S["xs_copied"], 1)
            for h in range(B_HEADS):
                if h + 2 < B_HEADS:
                    rbc(h + 2)
                if h == 3:
                    turn(1, lambda: pe.wait_ge(S["mix_a"], 2), None, (0, 1))
                pe.wait_ge(S["w_done"], h + 1)
                W, g = Wb[h % 2], h // 4
                c = slice((h % 4) * B_HD, (h % 4 + 1) * B_HD)
                for t, blocks in ((0, ((0, 0), (3, 0), (4, 1))), (1, ((1, 0), (2, 1), (5, 1)))):
                    for n, (blk, s_) in enumerate(blocks):
                        ins = mm(Y_BANKS[g][t][:, c], W[:, blk * P:(blk + 1) * P],
                                 xsn[:, s_, h * B_HD:(h + 1) * B_HD], h % 4 == 0 and n == 0, n == 2)
                ins.then_inc(S["y_pe"], 1)
            for hf in range(2):
                pe.wait_ge(S["hT_lo_done"], 4 + 2 * hf + 2)
                for c in range(2):
                    unit_ready(U_WOUT0 + 2 * hf + c)
                    tokens_still(U_WOUT0 + 2 * hf + c, 4, 4 * hf, [(B[2 * c + t], t, 0) for t in range(NT)], hT,
                                 hf == 0, hf == 1).then_inc(S["unit_used"], 1)
                if hf == 0:
                    for g in range(B_GROUPS):
                        turn(1, lambda: pe.wait_ge(S["mix_b"], g + 1), None, (2 + g,))

            def square(u0, m):
                pe.wait_ge(S["hT_lo_done"], 4 * m + 4)
                for c in range(2):
                    for hf in range(2):
                        u = u0 + 2 * c + hf
                        unit_ready(u)
                        tokens_still(u, 4, 4 * hf, [(B[2 * c + t], t, 0) for t in range(NT)], hT,
                                     hf == 0, hf == 1).then_inc(S["unit_used"], 1)

            turn_norm(2, 1)

            pe.wait_ge(S["hT_lo_done"], 12)
            def ff_up(u, m, b, turns):
                unit_ready(u, turns)
                w = parts(u, KT)
                for j in range(2):
                    for kt in range(KT):
                        l = [v[:, kt, j * P:(j + 1) * P] for v in w]
                        ins = mm3(B[2 * b + j][:, m * SEQ:(m + 1) * SEQ], l, [hT_hi[:, kt, :], hT_lo[:, kt, :]],
                                  m == 0 and kt == 0, kt == KT - 1)
                ins.then_inc(S["unit_used"], 1)

            def ff_down(u, b, turns, first, last=False):
                unit_ready(u, turns)
                w = parts(u, 2)
                for k, (t, hf) in enumerate(QUARTERS):
                    for j in range(2):
                        l = [ffh[b][:, j, t * P:(t + 1) * P], ffl[b][:, j, t * P:(t + 1) * P]]
                        ins = mm3(B[4 + 2 * t + hf][:, :], l, [v[:, j, hf * H:(hf + 1) * H] for v in w],
                                  first and j == 0)
                    if last and k < 3:
                        ins.then_inc(S["ff_quarter"], 1)
                return ins.then_inc(S["unit_used"], 1)

            def ff_step(c, b, loop=None, first=False):
                k = lambda v: v if loop is None else loop * 2 + v
                base = U_FFN + 2 + 3 * (c - 1)
                for m in range(2):
                    ff_up(base + m, m, b, loop)
                pe.wait_ge(S["ff_lo"], k(c))
                ff_down(base + 2, 1 - b, loop, first)

            for m in range(2):
                ff_up(U_FFN + m, m, 0, None)
            ff_step(1, 1, None, True)
            ff_step(2, 0)
            with pe.Fori(1, (FF_STEPS - 1) // 2) as it:
                ff_step(1, 1, it)
                ff_step(2, 0, it)

            def turn_p(n):
                pe.wait_ge(S["p_in"], 16 * (n + 1))
                for k in range(2):
                    for t in range(NT):
                        ins = pe.transpose(P_BANK[n][:, k * SEQ + t * P:k * SEQ + (t + 1) * P],
                                           pin[n][:, t, k * P:(k + 1) * P], ident[:, :])
                ins.then_inc(S["p_turned"], 1)

            def ple_proj(n, u, turns=None):
                unit_ready(u, turns)
                pe.wait_ge(S["pT_lo_done"], n + 1)
                outs = [(PROJ_BANKS[n][k], t, hf * H) for k, (t, hf) in enumerate(QUARTERS)]
                tokens_still(u, 2, 0, outs, (pT_hi[n][:, :, :], pT_lo[n][:, :, :]), True, True).then_inc(S["unit_used"], 1)

            def ple_gate(n, u0, m, turns=None):
                pe.wait_ge(S["hT_lo_done"], 4 * m + 4)
                for c in range(2):
                    for hf in range(2):
                        u = u0 + 2 * c + hf
                        unit_ready(u, turns)
                        tokens_still(u, 4, 4 * hf, [(GATE_BANKS[n][2 * c + t], t, 0) for t in range(NT)], hT,
                                     hf == 0, hf == 1).then_inc(S["unit_used"], 1)

            turn_p(0)
            pe.wait_ge(S["ff_lo"], FF_STEPS)
            ff_down(U_PLE0 - 1, 0, None, False, True)
            ple_proj(0, U_PLE0)
            turn_norm(3, 2)
            ple_gate(0, U_PLE0 + 1, 3)
            turn_norm(4, 3)

            pe.wait_ge(S["hT_lo_done"], 20)
            for c in range(6):
                banks = [B[2 * (c % 2)], B[2 * (c % 2) + 1]]
                if c >= 2:
                    pe.wait_ge(S["qkv_evac"], c - 1)
                for hf in range(2):
                    u = U_QKV + 2 * c + hf
                    unit_ready(u)
                    if c < 4:
                        ins = weights_still(u, hf, banks)
                    else:
                        ins = tokens_still(u, 4, 4 * hf, [(banks[t], t, 0) for t in range(NT)], hT, hf == 0, hf == 1)
                    ins.then_inc(S["unit_used"], 1)
            pe.wait_ge(S["qkv_evac"], 6)

            def attn_scores(h):
                if h >= 2:
                    pe.wait_ge(S["nm_done"], h - 1)
                p0, kt = C_HD * (h % 2), h // 2
                for t in range(NT):
                    ins = mm(B[h % 2][:, t * SEQ:(t + 1) * SEQ], qcT[p0:p0 + C_HD, kt, t * P:(t + 1) * P],
                             kcT[p0:p0 + C_HD, kt, :], t == 0, True)
                ins.then_inc(S["s_done"], 1)

            def attn_turn(h):
                pe.wait_ge(S["e_done"], 2 * h + 2)
                if h >= 2:
                    pe.wait_ge(S["pt_copied"], h - 1)
                for s_ in range(NT):
                    for t in range(NT):
                        ins = pe.transpose(B[2 + h % 2][:, s_ * SEQ + t * P:s_ * SEQ + (t + 1) * P],
                                           pr[h % 2][:, t, s_ * P:(s_ + 1) * P], ident[:, :])
                ins.then_inc(S["pt_done"], 1)

            def attn_out(h):
                pe.wait_ge(S["pt_copied"], h + 1)
                for t in range(NT):
                    for s_ in range(NT):
                        ins = mm(B[4 + 2 * (h // 8) + t][:, (h % 8) * C_HD:(h % 8 + 1) * C_HD],
                                 prT[h % 2][:, s_, t * P:(t + 1) * P], vc[:, s_, h * C_HD:(h + 1) * C_HD],
                                 h % 8 == 0 and s_ == 0, s_ == NT - 1)
                ins.then_inc(S["oc_done"], 1)

            for i in range(C_HEADS + 3):
                if i < C_HEADS:
                    attn_scores(i)
                if 2 <= i < C_HEADS + 2:
                    attn_turn(i - 2)
                if i >= 3:
                    attn_out(i - 3)
            turn(5, lambda: pe.wait_ge(S["oc_norm"], 4))
            square(U_WOUT1, 5)

            for j in range(4):
                pe.wait_ge(S["xg_ready"], 2 if j < 2 else 4)
                if j >= 2:
                    pe.wait_ge(S["hF_copied"], j - 1)
                for b in range(2):
                    for t in range(NT):
                        kt = 2 * j + b
                        ins = pe.transpose(B[6 + j % 2][:, b * SEQ + t * P:b * SEQ + (t + 1) * P],
                                           xn[:, t, kt * P:(kt + 1) * P], ident[:, :])
                ins.then_inc(S["hF_turned"], 1)
            pe.wait_ge(S["hF_copied"], 4)
            pe.wait_ge(S["wr_in"], 16)
            for t in range(NT):
                for kt in range(KT):
                    ins = mm(B[5][:, t * 8:t * 8 + 8], hF[:, kt, t * P:(t + 1) * P], wr[:, kt, :],
                             t == 0 and kt == 0, kt == KT - 1)
            ins.then_inc(S["lg_done"], 1)
            pe.wait_ge(S["mask_done"], 1)
            mm(B[4][:, 0:8], lt[:, :], msk[:, 0, :], True, True)
            mm(B[4][:, 8:16], lt[:, :], msk[:, 1, :], False)
            mm(B[4][:, 8:16], ones[:, :], msk[:, 0, :], False, True)
            mm(B[4][:, 16:24], ones[:, :], msk[:, 0, :], False)
            mm(B[4][:, 16:24], ones[:, :], msk[:, 1, :], False, True).then_inc(S["pos_done"], 1)

            def gather(k):
                pe.wait_ge(S["sel_built"], k)
                if isinstance(k, int):
                    pe.wait_ge(S["xgl_done"], 1)
                for kt in range(KT):
                    for t in range(NT):
                        for n, v in enumerate((xg_hi, xg_lo)):
                            ins = mm(B[5 + kt // 4][:, (kt % 4) * P:(kt % 4 + 1) * P], v[:, t, kt * P:(kt + 1) * P],
                                     sel[:, t, :], kt % 4 == 0 and t == 0 and n == 0, t == NT - 1 and n == 1)
                ins.then_inc(S["gath_done"], 1)

            he = (he_hi[:, :, :], he_lo[:, :, :])

            def gate_up(u, turns):
                for m in range(2):
                    for hf in range(2):
                        unit_ready(u + 2 * m + hf, turns)
                        w = parts(u + 2 * m + hf, 4)
                        for kk in range(4):
                            ins = mm3(B[m][:, :], [v[:, 4 * hf + kk, :] for v in he], [v[:, kk, :] for v in w],
                                      hf == 0 and kk == 0, hf == 1 and kk == 3)
                        ins.then_inc(S["unit_used"], 1)

            def turn_product(k):
                pe.wait_ge(S["emul"], k)
                for j in range(4):
                    ins = pe.transpose(B[4][:, j * P:(j + 1) * P], ea[:, j * P:(j + 1) * P], ident[:, :])
                ins.then_inc(S["eturned"], 1)

            def down(u, turns, k, first=False):
                pe.wait_ge(S["elo"], k)
                for n in range(2):
                    unit_ready(u + n, turns)
                    w = parts(u + n, 2)
                    for hf in range(2):
                        for kk in range(2):
                            l = [v[:, 2 * n + kk, :] for v in (eT_hi, eT_lo)]
                            ins = mm3(B[2 + hf][:, :], l, [v[:, kk, hf * H:(hf + 1) * H] for v in w], first and n == 0 and kk == 0)
                    ins.then_inc(S["unit_used"], 1)

            COMB = [B[5], B[6], B[7], B[3]]

            def combine(i):
                pe.wait_ge(S["ylo"], i + 1)
                for k, (t, hf) in enumerate(QUARTERS):
                    for n, v in enumerate((y_hi, y_lo)):
                        ins = mm(COMB[k][:, :], selT[:, t * P:(t + 1) * P], v[:, hf * H:(hf + 1) * H], n == 0, n == 1)
                ins.then_inc(S["comb_done"], 1)

            gather(1)
            pe.wait_ge(S["items_ready"], 1)
            n_items = pe.value_load(items[0:1, 12:13], min_val=N_EXPERTS, max_val=MAX_ITEMS)
            pe.sem_inc(S["comb_done"], 1)
            pe.wait_ge(S["moe_init"], 3)
            with pe.Fori(0, n_items) as i:
                turns = i * FE_STEPS
                pe.wait_ge(S["gel"], i + 1)
                gate_up(U_MOE, turns)
                combine(i)
                for t in range(NT):
                    pe.transpose(B[2][:, t * P:(t + 1) * P], sel[:, t, :].bitcast(F32), ident[:, :])
                for t in range(NT):
                    ins = mm(B[2][:, SEQ:SEQ + 1], sel[:, t, :].bitcast(F32), gcol[:, t, :], False if t else True, t == 1)
                ins.then_inc(S["selT_done"], 1)
                turn_product(turns + 1)
                gate_up(U_MOE + 4, turns)
                pe.wait_ge(S["selT_copied"], i + 2)
                down(U_MOE + 8, turns, turns + 1, True)
                with pe.Fori(2, FE_STEPS) as f:
                    done = turns + f
                    turn_product(done)
                    gate_up(U_STEP, done)
                    down(U_STEP + 4, done, done)
                turn_product(turns + FE_STEPS)
                gather(i + 2)
                down(U_TAIL, turns + (FE_STEPS - 1), turns + FE_STEPS)
            turn_p(1)
            combine(n_items + 0)
            all_turns = n_items * FE_STEPS
            ple_proj(1, U_MOE, all_turns)
            turn_norm(6, 5)
            ple_gate(1, U_MOE + 1, 6, all_turns)


_INS = ["x", "p", "hgrn_lb_raw", "e_norm_mix_pre", "e_w_in", "e_conv_w", "e_conv_b", "e_A_log", "e_dt_bias", "e_D",
        "e_a_norm", "e_b_norm", "e_w_out", "e_norm_mix_post", "e_norm_ffn_pre", "e_w_ffn_gate", "e_w_ffn_up",
        "e_w_ffn_down", "e_norm_ffn_post", "o_norm_mix_pre", "o_w_qkv", "o_rpb", "o_w_out", "o_norm_mix_post",
        "o_norm_ffn_pre", "o_w_router", "o_w_exp_gate", "o_w_exp_up", "o_w_exp_down", "o_norm_ffn_post",
        "ple_norm_in", "ple_w_gate", "ple_w_proj", "ple_norm_post"]


def kernel(**inputs):
    import concourse.bacc as bacc
    from concourse.bass_utils import run_bass_kernel_spmd

    nc = bacc.Bacc("TRN2", target_bir_lowering=False, num_devices=1)
    arrays, args = {}, {}
    for name in _INS:
        v = np.ascontiguousarray(inputs[name])
        arrays[f"in_{name}"] = v
        args[name] = nc.dram_tensor(f"in_{name}", v.shape, mybir.dt.from_np(v.dtype), kind="ExternalInput").ap()
    out = nc.dram_tensor("out", (1, SEQ, D), F32, kind="ExternalOutput").ap()
    trunk(nc, args, out)
    r = run_bass_kernel_spmd(nc, [arrays], core_ids=[0])
    return r.results[0]["out"]
```
